# Optimizing a Trainium2 kernel written in Bass

```python
import jax, jax.numpy as jnp
from jax import lax
import numpy as np

D_MODEL = 1024
BATCH = 1
SEQ = 256
DEPTH = 2

N_MIXERS = 2
N_RGLRU_LAYERS = (DEPTH + 1) // 2
N_DSA_LAYERS = DEPTH // 2
RMS_EPS = 1e-6
ROPE_THETA = 500000.0

LRU_W = D_MODEL
LRU_BLOCKS = 16
LRU_BW = LRU_W // LRU_BLOCKS
LRU_CONV = 4
LRU_C = 8.0

ATT_HEADS = 8
ATT_HD = 128
ATT_W = ATT_HEADS * ATT_HD
ATT_ROT = ATT_HD // 4
IDX_HEADS = 8
IDX_HD = 64
IDX_ROT = IDX_HD // 4
TOPK_MAX = 256
DSA_Q_BLOCK = 32

MEM_TOKENS = 256
MEM_HEADS = 4
MEM_HD = 128
MEM_W = MEM_HEADS * MEM_HD

D_FF = 2816
FFN_CONV = 3

LRU_IN_SIZES = (LRU_W, LRU_W, MEM_W)
DSA_IN_SIZES = (ATT_W, ATT_W, ATT_W, IDX_HEADS * IDX_HD, IDX_HD, IDX_HEADS, MEM_W)
LRU_IN = sum(LRU_IN_SIZES)
DSA_IN = sum(DSA_IN_SIZES)

kernel_name = "hybrid_rglru_dsa_memxattn_convffn"

def split_cols(z, sizes):
    return jnp.split(z, [int(c) for c in np.cumsum(sizes)[:-1]], axis=-1)

def rms_norm(x, g):
    xf = x.astype(jnp.float32)
    y = xf * lax.rsqrt(jnp.mean(xf * xf, axis=-1, keepdims=True) + RMS_EPS)
    return (y * g.astype(jnp.float32)).astype(x.dtype)

def causal_dwconv(x, w, b):
    k_w = w.shape[0]
    s = x.shape[1]
    xp = jnp.pad(x, ((0, 0), (k_w - 1, 0), (0, 0)))
    y = b + xp[:, 0:s] * w[0]
    for k in range(1, k_w):
        y = y + xp[:, k:k + s] * w[k]
    return y

def rope_tables(positions, rot_dim):
    inv = ROPE_THETA ** (-jnp.arange(0, rot_dim, 2, dtype=jnp.float32) / rot_dim)
    ang = positions.astype(jnp.float32)[..., None] * inv
    return jnp.cos(ang), jnp.sin(ang)

def apply_partial_rope(x, cos, sin):
    half = cos.shape[-1]
    c = cos[:, :, None, :].astype(x.dtype)
    s = sin[:, :, None, :].astype(x.dtype)
    x1 = x[..., :half]
    x2 = x[..., half:2 * half]
    return jnp.concatenate([x1 * c - x2 * s, x2 * c + x1 * s, x[..., 2 * half:]], axis=-1)

def memory_attention(q, mem_k, mem_v):
    b, s = q.shape[0], q.shape[1]
    sc = jnp.einsum('bshd,bmhd->bhsm', q, mem_k).astype(jnp.float32) * (MEM_HD ** -0.5)
    p = jax.nn.softmax(sc, axis=-1).astype(mem_v.dtype)
    return jnp.einsum('bhsm,bmhd->bshd', p, mem_v).reshape(b, s, MEM_W)

def rglru_mixer(h, mem_k, mem_v, w_in, conv_w, conv_b, w_a, b_a, w_x, b_x, lam, w_out):
    b, s, _ = h.shape
    xb, gb, mq = split_cols(h @ w_in, LRU_IN_SIZES)
    xc = causal_dwconv(xb, conv_w, conv_b)
    xblk = xc.reshape(b, s, LRU_BLOCKS, LRU_BW)
    r = jax.nn.sigmoid(jnp.einsum('bsnc,ncd->bsnd', xblk, w_a).reshape(b, s, LRU_W) + b_a)
    i = jax.nn.sigmoid(jnp.einsum('bsnc,ncd->bsnd', xblk, w_x).reshape(b, s, LRU_W) + b_x)
    log_a = -LRU_C * r.astype(jnp.float32) * jax.nn.softplus(-lam.astype(jnp.float32))
    a = jnp.exp(log_a)
    gain = jnp.sqrt(-jnp.expm1(2.0 * log_a))
    bt = gain * (i * xc).astype(jnp.float32)

    def combine(left, right):
        a1, b1 = left
        a2, b2 = right
        return a1 * a2, a2 * b1 + b2

    _, hs = lax.associative_scan(combine, (a, bt), axis=1)
    y = hs.astype(h.dtype) * jax.nn.gelu(gb)
    m = memory_attention(mq.reshape(b, s, MEM_HEADS, MEM_HD), mem_k, mem_v)
    return jnp.concatenate([y, m], axis=-1) @ w_out

def dsa_mixer(h, cos_a, sin_a, cos_i, sin_i, mem_k, mem_v, w_in, w_out):
    b, s, _ = h.shape
    q, k, v, iq, ik, iw, mq = split_cols(h @ w_in, DSA_IN_SIZES)
    q = apply_partial_rope(q.reshape(b, s, ATT_HEADS, ATT_HD), cos_a, sin_a)
    k = apply_partial_rope(k.reshape(b, s, ATT_HEADS, ATT_HD), cos_a, sin_a)
    iq = apply_partial_rope(iq.reshape(b, s, IDX_HEADS, IDX_HD), cos_i, sin_i)
    ik = apply_partial_rope(ik[:, :, None, :], cos_i, sin_i)[:, :, 0].astype(jnp.float32)
    iw = iw * (IDX_HEADS ** -0.5)
    topk = min(TOPK_MAX, s // 4)
    n_blk = s // DSA_Q_BLOCK
    k_flat = k.reshape(b, s, ATT_W)
    v_flat = v.reshape(b, s, ATT_W)
    key_pos = jnp.arange(s)
    gather = jax.vmap(lambda arr, ix: arr[ix])

    def to_blocks(t):
        return jnp.moveaxis(t.reshape(b, n_blk, DSA_Q_BLOCK, *t.shape[2:]), 1, 0)

    def attend_block(args):
        qb, iqb, iwb, t0 = args
        qpos = t0 + jnp.arange(DSA_Q_BLOCK)
        rel = jax.nn.relu(jnp.einsum('bqhd,bsd->bqhs', iqb.astype(jnp.float32), ik) * (IDX_HD ** -0.5))
        score = jnp.einsum('bqh,bqhs->bqs', iwb.astype(jnp.float32), rel)
        causal = key_pos[None, :] <= qpos[:, None]
        score = jnp.where(causal[None], score, -jnp.inf)
        _, idx = lax.top_k(score, topk)
        valid = idx <= qpos[None, :, None]
        flat_idx = idx.reshape(b, DSA_Q_BLOCK * topk)
        ks = gather(k_flat, flat_idx).reshape(b, DSA_Q_BLOCK, topk, ATT_HEADS, ATT_HD)
        vs = gather(v_flat, flat_idx).reshape(b, DSA_Q_BLOCK, topk, ATT_HEADS, ATT_HD)
        sc = jnp.einsum('bqhd,bqkhd->bhqk', qb, ks).astype(jnp.float32) * (ATT_HD ** -0.5)
        sc = jnp.where(valid[:, None], sc, -jnp.inf)
        p = jax.nn.softmax(sc, axis=-1).astype(vs.dtype)
        return jnp.einsum('bhqk,bqkhd->bqhd', p, vs)

    out = lax.map(attend_block, (to_blocks(q), to_blocks(iq), to_blocks(iw),
                                 jnp.arange(n_blk) * DSA_Q_BLOCK))
    out = jnp.moveaxis(out, 0, 1).reshape(b, s, ATT_W)
    m = memory_attention(mq.reshape(b, s, MEM_HEADS, MEM_HD), mem_k, mem_v)
    return jnp.concatenate([out, m], axis=-1) @ w_out

def conv_ffn(h, w_up, conv_w, conv_b, w_down):
    u = causal_dwconv(h @ w_up, conv_w, conv_b)
    g, val = jnp.split(u, 2, axis=-1)
    return (jax.nn.silu(g) * val) @ w_down

def setup_inputs(seed: int = 0) -> dict:
    key = jax.random.key(seed)
    ks = jax.random.split(key, 24)
    f32 = jnp.float32

    def nrm(k, shape, fan_in):
        return jax.random.normal(k, shape, f32) * (fan_in ** -0.5)

    def gain(k, shape):
        return 1.0 + 0.01 * jax.random.normal(k, shape, f32)

    def small(k, shape):
        return 0.01 * jax.random.normal(k, shape, f32)

    x = jax.random.normal(ks[0], (BATCH, SEQ, D_MODEL), f32)
    mem = jax.random.normal(ks[1], (BATCH, MEM_TOKENS, D_MODEL), f32)
    offs = jax.random.randint(ks[2], (BATCH, 1), 0, 1024, dtype=jnp.int32)
    positions = offs + jnp.arange(SEQ, dtype=jnp.int32)[None, :]
    a_init = jax.random.uniform(ks[3], (N_RGLRU_LAYERS, LRU_W), f32, 0.9, 0.999)
    s_init = a_init ** (1.0 / LRU_C)
    lru_lambda = jnp.log(s_init) - jnp.log1p(-s_init)
    return {
        "x": x,
        "mem": mem,
        "positions": positions,
        "norm_mix": gain(ks[4], (DEPTH, D_MODEL)),
        "norm_ffn": gain(ks[5], (DEPTH, D_MODEL)),
        "mem_norm": gain(ks[6], (D_MODEL,)),
        "final_norm": gain(ks[7], (D_MODEL,)),
        "w_mem_kv": nrm(ks[8], (DEPTH, D_MODEL, 2 * MEM_W), D_MODEL),
        "w_ffn_up": nrm(ks[9], (DEPTH, D_MODEL, 2 * D_FF), D_MODEL),
        "ffn_conv_w": nrm(ks[10], (DEPTH, FFN_CONV, 2 * D_FF), FFN_CONV),
        "ffn_conv_b": small(ks[11], (DEPTH, 2 * D_FF)),
        "w_ffn_down": nrm(ks[12], (DEPTH, D_FF, D_MODEL), D_FF),
        "lru_w_in": nrm(ks[13], (N_RGLRU_LAYERS, D_MODEL, LRU_IN), D_MODEL),
        "lru_conv_w": nrm(ks[14], (N_RGLRU_LAYERS, LRU_CONV, LRU_W), LRU_CONV),
        "lru_conv_b": small(ks[15], (N_RGLRU_LAYERS, LRU_W)),
        "lru_w_a": nrm(ks[16], (N_RGLRU_LAYERS, LRU_BLOCKS, LRU_BW, LRU_BW), LRU_BW),
        "lru_b_a": small(ks[17], (N_RGLRU_LAYERS, LRU_W)),
        "lru_w_x": nrm(ks[18], (N_RGLRU_LAYERS, LRU_BLOCKS, LRU_BW, LRU_BW), LRU_BW),
        "lru_b_x": small(ks[19], (N_RGLRU_LAYERS, LRU_W)),
        "lru_lambda": lru_lambda,
        "lru_w_out": nrm(ks[20], (N_RGLRU_LAYERS, LRU_W + MEM_W, D_MODEL), LRU_W + MEM_W),
        "dsa_w_in": nrm(ks[21], (N_DSA_LAYERS, D_MODEL, DSA_IN), D_MODEL),
        "dsa_w_out": nrm(ks[22], (N_DSA_LAYERS, ATT_W + MEM_W, D_MODEL), ATT_W + MEM_W),
    }

def reference(x, mem, positions, norm_mix, norm_ffn, mem_norm, final_norm, w_mem_kv,
              w_ffn_up, ffn_conv_w, ffn_conv_b, w_ffn_down,
              lru_w_in, lru_conv_w, lru_conv_b, lru_w_a, lru_b_a, lru_w_x, lru_b_x,
              lru_lambda, lru_w_out, dsa_w_in, dsa_w_out):
    b = x.shape[0]
    cos_a, sin_a = rope_tables(positions, ATT_ROT)
    cos_i, sin_i = rope_tables(positions, IDX_ROT)
    memn = rms_norm(mem, mem_norm)
    for i in range(DEPTH):
        mk, mv = jnp.split(memn @ w_mem_kv[i], 2, axis=-1)
        mk = mk.reshape(b, MEM_TOKENS, MEM_HEADS, MEM_HD)
        mv = mv.reshape(b, MEM_TOKENS, MEM_HEADS, MEM_HD)
        hn = rms_norm(x, norm_mix[i])
        j = i // N_MIXERS
        if i % N_MIXERS == 0:
            x = x + rglru_mixer(hn, mk, mv, lru_w_in[j], lru_conv_w[j], lru_conv_b[j],
                                lru_w_a[j], lru_b_a[j], lru_w_x[j], lru_b_x[j],
                                lru_lambda[j], lru_w_out[j])
        else:
            x = x + dsa_mixer(hn, cos_a, sin_a, cos_i, sin_i, mk, mv, dsa_w_in[j], dsa_w_out[j])
        x = x + conv_ffn(rms_norm(x, norm_ffn[i]), w_ffn_up[i], ffn_conv_w[i], ffn_conv_b[i],
                         w_ffn_down[i])
    return rms_norm(x, final_norm)


_drawn_inputs = setup_inputs


def setup_inputs(seed=0):
    import zlib

    import numpy as np

    out = dict(_drawn_inputs(seed))
    spreads = {}
    factors = {'norm_mix': 3.59,
     'norm_ffn': 3.66,
     'mem_norm': 8.0,
     'final_norm': 5.741,
     'ffn_conv_b': 3.775,
     'lru_b_a': 8.0,
     'lru_b_x': 8.0}
    for name, (base, spread) in spreads.items():
        noise = np.random.default_rng([zlib.crc32(name.encode()), seed]).standard_normal(out[name].shape)
        drawn = base * np.exp(spread * noise) if base else spread * noise
        out[name] = __import__('jax').numpy.asarray(drawn.astype(out[name].dtype))
    for name, factor in factors.items():
        out[name] = (out[name] * factor).astype(out[name].dtype)
    return out
```

```python
import math
from contextlib import ExitStack

import numpy as np
import concourse.bass as bass
from concourse import mybir


P = 128
S = 256
D = 1024
NT = S // P
KD = D // P
MEM_H, MEM_HD = 4, 128
MEM_W = MEM_H * MEM_HD
LRU_TAPS = 4
FF = 2816
FFN_TAPS = 3
AH, AD = 8, 128
AROT = AD // 4
IH, ID = 8, 64
IROT = ID // 4
TOPK = min(256, S // 4)
NPAIR = FF // (2 * P)
FC = 2 * FF // P
CAT = (D + MEM_W) // P
EPS = 1e-6
THETA = 500000.0
FILL = -3.0e38
PICKED = -3.4e38

U_MEM = 0
U_LRU_IN = 8
U_LRU_OUT = 18
U_FFN0 = 24
U_IDX = U_FFN0 + 3 * NPAIR
U_QKV = U_IDX + 4
U_DMQ = U_QKV + 12
U_DSA_OUT = U_DMQ + 2
U_FFN1 = U_DSA_OUT + 6
U_END = U_FFN1 + 3 * NPAIR
RING = 3

C_MIX, C_FFN, C_MEM, C_LCW, C_LCB, C_BA, C_BX, C_LAM = 0, 16, 32, 40, 72, 80, 88, 96
C_MISC = 104
C_F = (C_FFN_W0, C_FFN_W1) = (C_MISC, C_MISC + (FFN_TAPS + 1) * FC)
NPRM = C_MISC + 2 * (FFN_TAPS + 1) * FC


def trunk(nc, x_in, mem_in, pos_in, norm_mix, norm_ffn, mem_norm, final_norm, w_mem_kv, w_ffn_up, ffn_conv_w,
          ffn_conv_b, w_ffn_down, lru_w_in, lru_conv_w, lru_conv_b, lru_w_a, lru_b_a, lru_w_x, lru_b_x,
          lru_lambda, lru_w_out, dsa_w_in, dsa_w_out, out):
    fp32, f32r, i32 = mybir.dt.float32, mybir.dt.float32r, mybir.dt.int32
    ALU, ACT, AX = mybir.AluOpType, mybir.ActivationFunctionType, mybir.AxisListType
    ds = bass.ds

    with ExitStack() as ctx:
        def sb(name, shape, dt=fp32):
            return ctx.enter_context(nc.sbuf_tensor(name, shape, dt))

        def sem(name):
            return ctx.enter_context(nc.semaphore(name))

        w_raw = sb("w_raw", [P, RING, 2048])
        w_hi = sb("w_hi", [P, RING, 2048], f32r)
        w_lo = sb("w_lo", [P, RING, 2048], f32r)
        x = sb("x_res", [P, NT, D])
        hT = sb("hT", [P, KD, 2, S], f32r)
        cat = sb("cat", [P, CAT, 2, S], f32r)
        memT = cat[:, 0:KD]
        mkT = sb("mkT", [P, 2, MEM_H, S])
        mv = sb("mv", [P, 2, NT, MEM_W])
        mqT = sb("mqT", [P, MEM_H, S])
        ident = sb("ident", [P, P])
        prm = sb("prm", [P, NPRM])
        trig = sb("trig", [P, 2, NT, 24])
        eps_t = sb("eps_t", [P, 1])
        ssq = sb("ssq", [P, NT])
        std = sb("std", [P, NT])
        rstd = sb("rstd", [P, NT])
        sp8 = sb("sp8", [P, 2, KD])
        smax = sb("smax", [P, 2, NT])
        nmax = sb("nmax", [P, 2, NT])
        ssum = sb("ssum", [P, 2, NT])
        rsum = sb("rsum", [P, 2, NT])
        scratch = sb("scratch", [P, 2048])
        arena = sb("arena", [P, 14 * 1024])

        xn = scratch[:, :].rearrange("p (t d) -> p t d", t=NT)
        prob = scratch[:, 0:1024].rearrange("p (b n) -> p b n", b=2)
        probT = scratch[:, 1024:2048].rearrange("p (b n) -> p b n", b=2)

        t1_low = scratch[:, 1024:1536].rearrange("p (e s) -> p e s", e=2)

        def part(kib, n, pattern=None, **dims):
            v = arena[:, kib * 256:kib * 256 + n]
            return v.rearrange(pattern, **dims) if pattern else v

        rows = part(16, 640, "p (r c) -> p r c", r=5)
        mem_tok = part(8, 2048, "p (t d) -> p t d", t=NT)
        inv_t = part(24, NT * 24, "p (t f) -> p t f", t=NT)
        ang = part(25, NT * 24, "p (t f) -> p t f", t=NT)
        turns = part(26, NT * 24, "p (t f) -> p t f", t=NT)
        wrap = part(27, NT * 24, "p (t f) -> p t f", t=NT)
        pos_i = part(28, NT).bitcast(i32)
        pos_f = part(29, NT)
        lam_t = part(30, 10 * KD, "p (r c) -> p r c", r=10)
        B = [part(8 * n, 2048, "p (c s) -> p c s", c=KD) for n in range(6)]
        xbT, xcT, rT, iT, gbT, tT = B
        w_bd = part(48, 2048, "p (w c n) -> p w c n", w=2, c=KD)
        ffn_low = part(0, 1024, "p (c s) -> p c s", c=4)
        ffn_u = part(4, 1024, "p (c s) -> p c s", c=4)
        ffn_y = part(8, 1024, "p (c s) -> p c s", c=4)
        ffn_g = part(12, 512, "p (c s) -> p c s", c=2)
        ffn_p = part(14, 512, "p (c s) -> p c s", c=2)
        qk_tok = part(0, 4096, "p (t h d) -> p t h d", t=NT, h=2 * AH)
        v_tok = part(16, 2048, "p (t d) -> p t d", t=NT)
        qkT = part(24, 4096, "p (h s) -> p h s", h=2 * AH)
        iqT = part(40, 1024, "p (c s) -> p c s", c=4)
        iq_tok = part(44, 1024, "p (t h d) -> p t h d", t=NT, h=IH)
        ikT = part(48, 512, "p (e s) -> p e s", e=2)
        ikpad = part(50, 512, "p (t e d) -> p t e d", t=NT, e=2)
        score = part(52, 384)
        kbias = arena[:, 52 * 256 + 384:52 * 256 + 768]
        ikw_tok = part(55, 144, "p (t d) -> p t d", t=NT)
        top8 = arena[:, 55 * 256 + 144:55 * 256 + 160].rearrange("p (t d) -> p t d", t=NT)
        rope_t = part(24, 4 * 512, "p (r n) -> p r n", r=4)
        fin_g = part(48, D)

        U = [ctx.enter_context(nc.psum_tensor(f"ps_up{n}", [P, 512], fp32)) for n in range(4)]
        A = [ctx.enter_context(nc.psum_tensor(f"ps_acc{n}", [P, 512], fp32)) for n in range(4)]

        x_in_s, mem_in_s, rows_in_s, pos_in_s, bd_in_s, fg_in_s = (
            sem(n) for n in ("x_loaded", "mem_loaded", "rows_loaded", "pos_loaded", "bd_loaded", "fg_loaded"))
        raw_in = [sem(f"raw_loaded{n}") for n in range(RING)]
        out_s = sem("out_stored")
        hi_ready, lo_ready, unit_done = sem("hi_ready"), sem("lo_ready"), sem("unit_done")
        zeroed, consts = sem("zeroed"), sem("consts")
        bd_zero = sem("bd_zero")
        prm_t, prm_ready = sem("prm_transposed"), sem("prm_ready")
        chain = sem("dve_chain")
        lam_exp, lam_ready = sem("lam_exp"), sem("lam_ready")
        trig_args, trig_ready = sem("trig_args"), sem("trig_ready")
        sq_act, sq_dve, std_s, rstd_s, xn_ready = (sem(n) for n in ("sq_act", "sq_dve", "std", "rstd", "xn_ready"))
        n_tr, n_hi, n_lo = sem("norm_transposed"), sem("norm_hi"), sem("norm_lo")
        tile_done, res_done = sem("tile_done"), sem("res_done")
        t1_lowed, t1_sum = sem("t1_lowed"), sem("t1_sum")
        t2_done = sem("t2_copied")
        cv_tap, cv_acc, xc_ready = sem("conv_tap"), sem("conv_acc"), sem("xc_ready")
        gate_mm, gate_sig = sem("gate_mm"), sem("gate_sig")
        l_exp, l_tanh, l_gain2, l_sqrt, l_bt, l_h, l_gelu, l_y, l_yhi, l_ylo = (
            sem("lru_" + n) for n in ("exp", "tanh", "gain2", "sqrt", "bt", "h", "gelu", "y", "yhi", "ylo"))
        l_ix, l_a2 = sem("lru_ix"), sem("lru_a2")
        at_s, at_max, at_nmax, at_exp, at_rs, at_p, at_t, at_pt, at_o, at_hi, at_lo, at_sc = (
            sem("att_" + n) for n in ("s", "max", "nmax", "exp", "rsum", "p", "t", "pt", "o", "hi", "lo", "sc"))
        ik_zero, rope_i, ik_copied = sem("ik_zero"), sem("rope_i"), sem("ik_copied")
        ix_tr, ix_trc, ix_mm, ix_relu, ix_acc = (sem("idx_" + n) for n in ("tr", "trc", "mm", "relu", "acc"))
        causal_s, top_s, bias_s, bias_ready = sem("causal"), sem("top"), sem("bias"), sem("bias_ready")
        rope_q, q_tr, q_trc = sem("rope_q"), sem("q_tr"), sem("q_trc")
        f_low, f_sum, f_tap, f_acc, f_conv, f_silu, f_prod, f_hi, f_lo = (
            [sem(f"ffn{l}_{n}") for l in range(2)]
            for n in ("lowed", "summed", "tap", "acc", "conv", "silu", "prod", "hi", "lo"))

        out_ready, xn_free = sem("out_ready"), sem("xn_free")

        block = ctx.enter_context(nc.Block())

        def raw3(slot, k, c):
            return w_raw[:, slot, 0:k * c].rearrange("p (k c) -> p k c", k=k)

        def kxc(w, k0, k, c0, c):
            return w[k0 * P:(k0 + k) * P, c0:c0 + c].rearrange("(k p) c -> p k c", p=P)

        mem_w = [w_mem_kv[l] for l in range(2)]
        lru_in, dsa_in = lru_w_in[0], dsa_w_in[0]
        c_iq, c_mq = 3 * D, 3 * D + IH * ID + ID + IH
        units = []
        for l in range(2):
            units += [(8, 256, kxc(mem_w[l], 0, 8, 256 * j, 256)) for j in range(2)]
            units += [(4, 512, kxc(mem_w[l], 4 * j, 4, MEM_W, MEM_W)) for j in range(2)]
        units += [(8, 256, kxc(lru_in, 0, 8, 256 * j, 256)) for j in range(10)]
        out_order = (8, 10, 0, 2, 4, 6)
        units += [(2, 1024, kxc(lru_w_out[0], k, 2, 0, D)) for k in out_order]
        units_dsa = [(4, 512, kxc(dsa_in, 4 * j, 4, c_iq, IH * ID)) for j in range(2)]
        units_dsa += [(4, ID + IH, kxc(dsa_in, 4 * j, 4, c_iq + IH * ID, ID + IH)) for j in range(2)]
        units_dsa += [(4, 512, kxc(dsa_in, 4 * j, 4, 512 * c, 512)) for c in range(6) for j in range(2)]
        units_dsa += [(8, 256, kxc(dsa_in, 0, 8, c_mq + 256 * j, 256)) for j in range(2)]
        units_dsa += [(2, 1024, kxc(dsa_w_out[0], k, 2, 0, D)) for k in out_order]

        def unit_size(n):
            if U_IDX + 2 <= n < U_IDX + 4:
                return 4 * (ID + IH)
            return 2048

        @block.sync
        def _(sp):
            def load(n, slot, k, c, src):
                if not isinstance(n, int) or n >= RING:
                    sp.wait_ge(lo_ready, n - (RING - 1))
                sp.dma_start(raw3(slot, k, c), src).then_inc(raw_in[slot], 16)

            mem_v = mem_in[0].rearrange("(t p) d -> p t d", p=P)
            sp.dma_start(mem_tok[:, :, :], mem_v).then_inc(mem_in_s, 16)
            vecs = [(norm_mix, 0, 16), (norm_ffn, 16, 16), (mem_norm, 32, 8), (lru_conv_w, 40, 32), (lru_conv_b, 72, 8),
                    (lru_b_a, 80, 8), (lru_b_x, 88, 8), (lru_lambda, 96, 8)]
            for v, at, n in vecs:
                flat = {1: "(r c) -> r c", 2: "a (r c) -> (a r) c", 3: "a b (r c) -> (a b r) c"}[len(v.shape)]
                sp.dma_start(rows[at:at + n, 0, :], v.rearrange(flat, c=P)).then_inc(rows_in_s, 16)
            for l in range(2):
                taps = ffn_conv_w[l].rearrange("k (r c) -> (k r) c", c=P)
                nw = FFN_TAPS * FC
                sp.dma_start(rows[:, 1 + 2 * l, :], taps[0:P]).then_inc(rows_in_s, 16)
                sp.dma_start(rows[0:nw - P, 2 + 2 * l, :], taps[P:nw]).then_inc(rows_in_s, 16)
                sp.dma_start(rows[nw - P:nw - P + FC, 2 + 2 * l, :],
                             ffn_conv_b[l].rearrange("(r c) -> r c", c=P)).then_inc(rows_in_s, 16)
            for n in range(2):
                load(n, n % RING, *units[n])
            sp.dma_start(x[:, :, :], x_in[0].rearrange("(t p) d -> p t d", p=P)).then_inc(x_in_s, 16)
            load(2, 2, *units[2])
            for t in range(NT):
                sp.dma_start(pos_i[:, t:t + 1], pos_in[0, t * P:(t + 1) * P].rearrange("(p o) -> p o", o=1)).then_inc(pos_in_s, 16)
            sp.wait_ge(bd_zero, 1)
            for w, src in enumerate((lru_w_a, lru_w_x)):
                two = src[0].rearrange("(c e) i d -> e i c d", e=2)
                for e in range(2):
                    sp.dma_start(w_bd[64 * e:64 * e + 64, w, :, 64 * e:64 * e + 64], two[e]).then_inc(bd_in_s, 16)
            for n in range(3, U_FFN0):
                load(n, n % RING, *units[n])

            def ffn_loads(l, first):
                def up(n, slot, i, half):
                    load(n, slot, 8, 256, w_ffn_up[l][:, ds(half * FF + i * 256, 256)].rearrange("(k p) c -> p k c", p=P))

                def down(n, slot, i):
                    load(n, slot, 2, 1024, w_ffn_down[l][ds(i * 256, 256), :].rearrange("(k p) c -> p k c", p=P))

                up(first, 0, 0, 0)
                up(first + 1, 1, 0, 1)
                with sp.Fori(1, NPAIR) as i:
                    up(first - 1 + i * 3, 2, i, 0)
                    up(first + i * 3, 0, i, 1)
                    down(first + 1 + i * 3, 1, i - 1)
                down(first + 3 * NPAIR - 1, 2, NPAIR - 1)

            ffn_loads(0, U_FFN0)
            for n in range(U_IDX, U_FFN1):
                load(n, n % RING, *units_dsa[n - U_IDX])
            ffn_loads(1, U_FFN1)
            sp.dma_start(fin_g, final_norm.rearrange("(o d) -> o d", o=1).broadcast_to((P, D))).then_inc(fg_in_s, 16)
            out_v = out[0].rearrange("(t p) d -> p t d", p=P)
            for t in range(NT):
                sp.wait_ge(out_ready, t + 1)
                sp.dma_start(out_v[:, t, :], xn[:, t, :]).then_inc(out_s, 16)
            sp.wait_ge(out_s, 16 * NT)

        @block.gpsimd
        def _(pool):
            nc.gpsimd.memset(ident[:, :], 0.0).then_inc(zeroed, 1)
            nc.gpsimd.memset(w_bd[:, :, :, :], 0.0).then_inc(bd_zero, 1)
            nc.gpsimd.memset(eps_t[:, :], EPS)
            pool.wait_ge(zeroed, 1)
            nc.gpsimd.affine_select(out=ident[:, :], in_=ident[:, :], compare_op=ALU.not_equal, fill=1.0, base=0,
                                    pattern=[[-1, P]], channel_multiplier=1).then_inc(consts, 1)
            freqs = [THETA ** (-f / AROT) for f in range(0, AROT, 2)] + [THETA ** (-f / IROT) for f in range(0, IROT, 2)]
            for f, v in enumerate(freqs):
                ins = nc.gpsimd.memset(inv_t[:, :, f:f + 1], float(np.float32(v)))
            ins.then_inc(consts, 1)
            pool.wait_ge(unit_done, U_IDX)
            nc.gpsimd.memset(ikpad[:, :, :, :], 0.0).then_inc(ik_zero, 1)

            def causal(src, n):
                nc.gpsimd.affine_select(out=src[:, 0:P], in_=src[:, 0:P], compare_op=ALU.is_ge, fill=FILL, base=0,
                                        pattern=[[-1, P]], channel_multiplier=1)
                nc.gpsimd.affine_select(out=src[:, P:3 * P], in_=src[:, P:3 * P], compare_op=ALU.is_ge, fill=FILL,
                                        base=P, pattern=[[-1, S]], channel_multiplier=1).then_inc(n, 1)

            pool.wait_ge(ix_acc, IH * NT)
            causal(score, causal_s)
            pool.wait_ge(bias_s, 1)
            causal(kbias, bias_ready)

        @block.scalar
        def _(act):
            def copy(dst, src):
                return nc.scalar.activation(dst, src, ACT.Copy)

            def split_hi(n, slot):
                if isinstance(n, int):
                    if n >= U_END:
                        return
                    act.wait_ge(raw_in[slot], 16 * (n // RING + 1))
                    size = unit_size(n)
                    if n >= RING:
                        act.wait_ge(unit_done, n - (RING - 1))
                else:
                    size = 2048
                    act.wait_ge(unit_done, n - (RING - 1))
                copy(w_hi[:, slot, 0:size], w_raw[:, slot, 0:size]).then_inc(hi_ready, 1)

            def norm_stats(k, src, loaded, n):
                act.wait_ge(loaded, n)
                nc.scalar.activation(xn[:, 0, :], src[:, 0, :], ACT.Square, accum_out=ssq[:, 0:1]).then_inc(sq_act, 1)
                act.wait_ge(sq_act, k + 1)
                act.wait_ge(sq_dve, k + 1)
                nc.scalar.activation(std[:, :], ssq[:, :], ACT.Sqrt, scale=1.0 / D, bias=eps_t[:, 0:1]).then_inc(std_s, 1)

            def norm_hi(k, dst, gain):
                for b in range(4):
                    act.wait_ge(n_tr, 4 * k + b + 1)
                    for e in range(2):
                        c = 2 * b + e
                        ins = nc.scalar.activation(dst[:, c, 0, :], U[b][:, e * S:(e + 1) * S], ACT.Copy,
                                                   scale=prm[:, gain + c:gain + c + 1])
                    ins.then_inc(n_hi, 1)

            def t1_lows(n, t1):
                act.wait_ge(unit_done, n + 1)
                for e in range(2):
                    if t1:
                        act.wait_ge(t1_sum, t1 + e - 1)
                    copy(t1_low[:, e, :], U[(t1 + e) % 4][:, S:2 * S]).then_inc(t1_lowed, 1)

            def attention_head(m, softmax, evac_pt):
                b = m % 2
                act.wait_ge(at_nmax, m + 1)
                for t, (lo, hi_) in enumerate(softmax):
                    src = A[b][:, lo:hi_] if evac_pt is mem_pt else prob[:, b, lo:hi_]
                    ins = nc.scalar.activation(prob[:, b, lo:hi_], src, ACT.Exp, bias=nmax[:, b, t:t + 1],
                                               scale=evac_pt[1], accum_out=ssum[:, b, t:t + 1])
                ins.then_inc(at_exp, 1)

            mem_pt = (2 * S, MEM_HD ** -0.5)
            dsa_pt = (3 * P, 1.0)

            def attention_out(m, kind, cat_at):
                b = m % 2
                act.wait_ge(at_t, m + 1)
                copy(probT[:, b, 0:kind[0]], A[2 + b][:, 0:kind[0]]).then_inc(at_pt, 1)
                act.wait_ge(at_o, m + 1)
                copy(cat[:, cat_at, 0, :], U[b][:, 0:S]).then_inc(at_hi, 1)

            act.wait_ge(consts, 2)
            norm_stats(0, mem_tok, mem_in_s, 16)
            act.wait_ge(prm_t, 1)
            copy(prm[:, :], U[0][:, 0:NPRM]).then_inc(prm_ready, 1)
            for n in range(RING):
                split_hi(n, n)
            act.wait_ge(prm_ready, 1)
            norm_hi(0, memT, C_MEM)
            act.wait_ge(xn_free, 1)
            norm_stats(1, x, x_in_s, 16)
            norm_hi(1, hT, C_MIX)
            act.wait_ge(lam_exp, 1)
            nc.scalar.activation(lam_t[:, 1, :], lam_t[:, 0, :], ACT.Exp, scale=-1.0).then_inc(lam_exp, 1)
            act.wait_ge(trig_args, 1)
            nc.scalar.activation(trig[:, 0], ang[:, :, :], ACT.Sin)
            nc.scalar.activation(trig[:, 1], wrap[:, :, :], ACT.Sin).then_inc(trig_ready, 1)
            for l in range(2):
                for j in range(2):
                    n = U_MEM + 4 * l + j
                    t1_lows(n, 4 * l + 2 * j)
                    split_hi(n + 3, n % RING)
                split_hi(U_MEM + 4 * l + 5, (U_MEM + 4 * l + 2) % RING)
                act.wait_ge(unit_done, U_MEM + 4 * l + 4)
                for t in range(NT):
                    copy(mv[:, l, t, :], A[2 * l + t][:, :]).then_inc(t2_done, 1)
                split_hi(U_MEM + 4 * l + 6, (U_MEM + 4 * l + 3) % RING)

            def conv_taps(j):
                for c in (2 * j, 2 * j + 1):
                    act.wait_ge(t1_sum, 8 + c + 1)
                    nc.scalar.activation(xcT[:, c, :], xbT[:, c, :], ACT.Identity, bias=prm[:, C_LCB + c:C_LCB + c + 1],
                                         scale=prm[:, C_LCW + 24 + c:C_LCW + 25 + c]).then_inc(cv_tap, 1)

            for j in range(10):
                n = U_LRU_IN + j
                t1_lows(n, 8 + 2 * j)
                split_hi(n + 3, n % RING)
                if j < 4:
                    conv_taps(j)
                if j == 5:
                    for c in range(KD):
                        act.wait_ge(gate_mm, c + 1)
                        nc.scalar.activation(rT[:, c, :], A[c % 4][:, 0:S], ACT.Sigmoid, bias=prm[:, C_BA + c:C_BA + c + 1])
                        nc.scalar.activation(iT[:, c, :], A[c % 4][:, S:2 * S], ACT.Sigmoid,
                                             bias=prm[:, C_BX + c:C_BX + c + 1]).then_inc(gate_sig, 1)
                if j == 6:
                    act.wait_ge(gate_sig, KD)
                    act.wait_ge(lam_ready, 1)
                    for c in range(KD):
                        nc.scalar.activation(xbT[:, c, :], rT[:, c, :], ACT.Exp, scale=sp8[:, 1, c:c + 1]).then_inc(l_exp, 1)
                        nc.scalar.activation(tT[:, c, :], rT[:, c, :], ACT.Tanh, scale=sp8[:, 0, c:c + 1]).then_inc(l_tanh, 1)
                if j == 8:
                    for h in range(2):
                        cs = slice(4 * h, 4 * h + 4)
                        act.wait_ge(l_gain2, h + 1)
                        nc.scalar.activation(rT[:, cs, :], tT[:, cs, :], ACT.Sqrt).then_inc(l_sqrt, 1)
            act.wait_ge(t1_sum, 8 + 16)
            for h in range(2):
                cs = slice(4 * h, 4 * h + 4)
                nc.scalar.activation(gbT[:, cs, :], gbT[:, cs, :], ACT.Gelu_apprx_tanh).then_inc(l_gelu, 1)
            for h in range(MEM_H):
                attention_head(h, ((0, S), (S, 2 * S)), mem_pt)
                attention_out(h, mem_pt, KD + h)
            for h in range(2):
                cs = slice(4 * h, 4 * h + 4)
                act.wait_ge(l_y, h + 1)
                nc.scalar.activation(cat[:, cs, 0, :], xbT[:, cs, :], ACT.Copy).then_inc(l_yhi, 1)
            for n in range(U_LRU_OUT, U_FFN0):
                split_hi(n + 3, n % RING)
            norm_stats(2, x, res_done, 4)
            norm_hi(2, hT, C_FFN)

            def ffn(l, first):
                cw, cb = C_F[l], C_F[l] + FFN_TAPS * FC

                def half(i, h, unit, nxt, slot):
                    act.wait_ge(unit_done, unit + 1)
                    for c in range(2):
                        copy(ffn_low[:, 2 * h + c, :], U[2 * h + c][:, S:2 * S]).then_inc(f_low[l], 1)
                    if nxt is not None:
                        split(nxt, slot)
                    for c in range(2):
                        ch = i * 2 + (h * (FC // 2) + c)
                        act.wait_ge(f_sum[l], i * 4 + (2 * h + c + 1))
                        nc.scalar.activation(ffn_y[:, 2 * h + c, :], ffn_u[:, 2 * h + c, :], ACT.Identity,
                                             bias=prm[:, ds(cb + ch, 1)], scale=prm[:, ds(cw + 2 * FC + ch, 1)]).then_inc(f_tap[l], 1)

                def split(nxt, slot):
                    n, turn = nxt
                    if isinstance(n, int):
                        split_hi(n, slot)
                    else:
                        act.wait_ge(raw_in[slot], turn)
                        split_hi(n, slot)

                def tail(i, nxt, slot):
                    act.wait_ge(f_conv[l], i * 4 + 2)
                    nc.scalar.activation(ffn_g[:, :, :], ffn_y[:, 0:2, :], ACT.Silu).then_inc(f_silu[l], 1)
                    split(nxt, slot)
                    act.wait_ge(f_prod[l], i + 1)
                    act.wait_ge(unit_done, first + 2 + i * 3)
                    nc.scalar.activation(cat[:, 0:2, 0, :], ffn_p[:, :, :], ACT.Copy).then_inc(f_hi[l], 1)

                r0 = first // RING * 16
                half(0, 0, first, (first + 3, 0), 0)
                half(0, 1, first + 1, (first + 4, 0), 1)
                act.wait_ge(f_conv[l], 2)
                nc.scalar.activation(ffn_g[:, :, :], ffn_y[:, 0:2, :], ACT.Silu).then_inc(f_silu[l], 1)
                act.wait_ge(f_prod[l], 1)
                nc.scalar.activation(cat[:, 0:2, 0, :], ffn_p[:, :, :], ACT.Copy).then_inc(f_hi[l], 1)
                with act.Fori(1, NPAIR - 1) as i:
                    half(i, 0, first - 1 + i * 3, (first + 2 + i * 3, r0 + 16 + i * 16), 2)
                    half(i, 1, first + i * 3, (first + 3 + i * 3, r0 + 32 + i * 16), 0)
                    tail(i, (first + 4 + i * 3, r0 + 32 + i * 16), 1)
                i = NPAIR - 1
                half(i, 0, first - 1 + 3 * i, (first + 2 + 3 * i, 0), 2)
                half(i, 1, first + 3 * i, (first + 3 + 3 * i, 0), 0)
                tail(i, (first + 4 + 3 * i, 0), 1)
                split_hi(first + 5 + 3 * i, 2)

            ffn(0, U_FFN0)
            norm_stats(3, x, res_done, 8)
            norm_hi(3, hT, C_MIX + KD)

            def t2_copies(n, s, dsts):
                act.wait_ge(unit_done, n + 1)
                for t in range(NT):
                    copy(dsts[t], A[2 * (s % 2) + t][:, 0:dsts[t].free_size()]).then_inc(t2_done, 1)

            iq_f = iq_tok[:, :, :, :].rearrange("p t h d -> p t (h d)")
            qk_f = qk_tok[:, :, :, :].rearrange("p t h d -> p t (h d)")
            chunks = [[iq_f[:, t, :] for t in range(NT)], [ikw_tok[:, t, :] for t in range(NT)]]
            chunks += [[qk_f[:, t, 512 * c:512 * c + 512] for t in range(NT)] for c in range(4)]
            chunks += [[v_tok[:, t, 512 * c:512 * c + 512] for t in range(NT)] for c in range(2)]
            for s, dsts in enumerate(chunks):
                n = U_IDX + 2 * s
                split_hi(n + 3, n % RING)
                t2_copies(n + 1, s, dsts)
                split_hi(n + 4, (n + 1) % RING)
                if s == 3:
                    for b in range(3):
                        act.wait_ge(ix_tr, b + 1)
                        dst = ikT[:, :, :] if b == 2 else iqT[:, 2 * b:2 * b + 2, :]
                        copy(dst.rearrange("p c s -> p (c s)"), U[b][:, :]).then_inc(ix_trc, 1)
                if s == 4:
                    for hp in range(IH // 2):
                        for t in range(NT):
                            step = NT * hp + t
                            width = (t + 1) * P
                            act.wait_ge(ix_mm, step + 1)
                            if step >= 2:
                                act.wait_ge(ix_acc, 2 * (step - 1))
                            nc.scalar.activation(prob[:, step % 2, 0:2 * width], U[step % 4][:, 0:2 * width], ACT.Relu,
                                                 scale=ID ** -0.5).then_inc(ix_relu, 1)
            for j in range(2):
                n = U_DMQ + j
                t1_lows(n, 28 + 2 * j)
                split_hi(n + 3, n % RING)
            for b in range(8):
                act.wait_ge(q_tr, b + 1)
                copy(qkT[:, 2 * b:2 * b + 2, :].rearrange("p h s -> p (h s)"), U[b % 4][:, :]).then_inc(q_trc, 1)
            for h in range(MEM_H):
                attention_head(4 + h, ((0, S), (S, 2 * S)), mem_pt)
                attention_out(4 + h, mem_pt, KD + h)
            for h in range(AH):
                attention_head(8 + h, ((0, P), (P, 3 * P)), dsa_pt)
                attention_out(8 + h, dsa_pt, h)
            for n in range(U_DSA_OUT, U_FFN1):
                split_hi(n + 3, n % RING)
            norm_stats(4, x, res_done, 12)
            norm_hi(4, hT, C_FFN + KD)
            ffn(1, U_FFN1)
            norm_stats(5, x, res_done, 16)

        @block.vector
        def _(dve):
            TT, TS, STT = nc.vector.tensor_tensor, nc.vector.tensor_scalar, nc.vector.scalar_tensor_tensor
            links = [0]

            def link(ins):
                links[0] += 1
                ins.then_inc(chain, 1)
                dve.wait_ge(chain, links[0])

            def split_lo(n, slot):
                if isinstance(n, int) and n >= U_END:
                    return
                size = unit_size(n) if isinstance(n, int) else 2048
                dve.wait_ge(hi_ready, n + 1)
                TT(w_lo[:, slot, 0:size], w_raw[:, slot, 0:size], w_hi[:, slot, 0:size].bitcast(fp32),
                   ALU.subtract).then_inc(lo_ready, 1)

            def norm_stats(k, src, loaded, n):
                dve.wait_ge(loaded, n)
                STT(xn[:, 1, :], src[:, 1, :], 1.0, src[:, 1, :], ALU.mult, ALU.mult,
                    accum_out=ssq[:, 1:2]).then_inc(sq_dve, 1)
                dve.wait_ge(std_s, k + 1)
                nc.vector.reciprocal(rstd[:, :], std[:, :]).then_inc(rstd_s, 1)
                dve.wait_ge(rstd_s, k + 1)
                if k < 5:
                    for t in range(NT):
                        TS(xn[:, t, :], src[:, t, :], rstd[:, t:t + 1], None, ALU.mult).then_inc(xn_ready, 1)

            def norm_lo(k, dst, gain):
                for b in range(4):
                    dve.wait_ge(n_hi, 4 * k + b + 1)
                    for e in range(2):
                        c = 2 * b + e
                        ins = STT(dst[:, c, 1, :], U[b][:, e * S:(e + 1) * S], prm[:, gain + c:gain + c + 1],
                                  dst[:, c, 0, :].bitcast(fp32), ALU.mult, ALU.subtract)
                    ins.then_inc(n_lo, 1)

            def t1_sums(t1, dsts):
                for e in range(2):
                    dve.wait_ge(t1_lowed, t1 + e + 1)
                    TT(dsts[e], U[(t1 + e) % 4][:, 0:S], t1_low[:, e, :], ALU.add).then_inc(t1_sum, 1)

            def softmax_max(m, spans, src, scale):
                b = m % 2
                if isinstance(src, bass.AP) is False:
                    src = src[b]
                for t, (lo, hi_) in enumerate(spans):
                    ins = nc.vector.reduce_max(smax[:, b, t:t + 1], src[:, lo:hi_], AX.X)
                ins.then_inc(at_max, 1)
                dve.wait_ge(at_max, m + 1)
                TS(nmax[:, b, :], smax[:, b, :], -scale, None, ALU.mult).then_inc(at_nmax, 1)

            def softmax_scale(m, spans):
                b = m % 2
                dve.wait_ge(at_exp, m + 1)
                nc.vector.reciprocal(rsum[:, b, :], ssum[:, b, :]).then_inc(at_rs, 1)
                dve.wait_ge(at_rs, m + 1)
                for t, (lo, hi_) in enumerate(spans):
                    ins = TS(prob[:, b, lo:hi_], prob[:, b, lo:hi_], rsum[:, b, t:t + 1], None, ALU.mult)
                ins.then_inc(at_p, 1)

            def attention_lo(m, cat_at):
                dve.wait_ge(at_hi, m + 1)
                TT(cat[:, cat_at, 1, :], U[m % 2][:, 0:S], cat[:, cat_at, 0, :].bitcast(fp32),
                   ALU.subtract).then_inc(at_lo, 1)

            def residual(k, last_unit):
                for t in range(NT):
                    if t == 0:
                        dve.wait_ge(tile_done, k + 1)
                    else:
                        dve.wait_ge(unit_done, last_unit + 1)
                    for n in range(2):
                        xs = x[:, t, 512 * n:512 * n + 512]
                        TT(xs, xs, A[2 * t + n][:, :], ALU.add).then_inc(res_done, 1)

            norm_stats(0, mem_tok, mem_in_s, 16)
            for n in range(RING):
                split_lo(n, n)
            dve.wait_ge(prm_ready, 1)
            norm_lo(0, memT, C_MEM)
            norm_stats_wait = n_tr
            dve.wait_ge(norm_stats_wait, 4)
            nc.vector.memset(ssq[:, :], 0.0).then_inc(xn_free, 1)
            dve.wait_ge(xn_free, 1)
            norm_stats(1, x, x_in_s, 16)
            norm_lo(1, hT, C_MIX)

            lam = prm[:, C_LAM:C_LAM + KD]
            absl, u, den, s1, s2, q = (lam_t[:, r, :] for r in range(6))
            STT(absl, lam, -1.0, lam, ALU.mult, ALU.max).then_inc(lam_exp, 1)
            dve.wait_ge(lam_exp, 2)
            link(TS(den, u, 2.0, None, ALU.add))
            link(nc.vector.reciprocal(den, den))
            link(TT(s1, u, den, ALU.mult))
            link(TT(s2, s1, s1, ALU.mult))
            link(TS(q, s2, 1.0 / 17, None, ALU.mult))
            for odd in range(15, 1, -2):
                link(STT(q, q, 1.0 / odd, s2, ALU.add, ALU.mult))
            link(STT(q, q, 1.0, s1, ALU.add, ALU.mult))
            link(TS(den, lam, -1.0, 0.0, ALU.mult, ALU.max))
            link(STT(q, q, 2.0, den, ALU.mult, ALU.add))
            TS(sp8[:, 0, :], q, 8.0, None, ALU.mult)
            TS(sp8[:, 1, :], q, -8.0, None, ALU.mult).then_inc(lam_ready, 1)

            dve.wait_ge(pos_in_s, 16 * NT)
            dve.wait_ge(consts, 2)
            link(nc.vector.tensor_copy(pos_f, pos_i))
            for t in range(NT):
                link(TS(ang[:, t, :], inv_t[:, t, :], pos_f[:, t:t + 1], None, ALU.mult))
            magic = 1.5 * 2.0 ** 23
            link(TS(turns, ang, 1.0 / (2 * math.pi), magic, ALU.mult, ALU.add))
            link(TS(turns, turns, -magic, None, ALU.add))
            c1 = 6.28125
            c2 = round((2 * math.pi - c1) * 2 ** 18) / 2 ** 18
            c3 = 2 * math.pi - c1 - c2
            for c in (c1, c2, c3):
                link(STT(ang, turns, -c, ang, ALU.mult, ALU.add))
            top = float(np.nextafter(np.float32(math.pi), np.float32(0)))
            link(TS(wrap, ang, math.pi / 2, None, ALU.add))
            link(TS(turns, wrap, math.pi, -2 * math.pi, ALU.is_gt, ALU.mult))
            link(TT(wrap, wrap, turns, ALU.add))
            link(TS(wrap, wrap, top, -top, ALU.min, ALU.max))
            TS(ang, ang, top, -top, ALU.min, ALU.max).then_inc(trig_args, 1)

            for l in range(2):
                for j in range(2):
                    n = U_MEM + 4 * l + j
                    t1_sums(4 * l + 2 * j, [mkT[:, l, 2 * j + e, :] for e in range(2)])
                    split_lo(n + 3, n % RING)
                for j in range(2, 4):
                    n = U_MEM + 4 * l + j
                    split_lo(n + 3, n % RING)

            for j in range(10):
                n = U_LRU_IN + j
                dst = xbT if j < 4 else gbT
                if j == 4:
                    dve.wait_ge(cv_tap, KD)
                if j < 8:
                    dsts = [dst[:, (2 * j + e) % KD, :] for e in range(2)]
                else:
                    dsts = [mqT[:, 2 * (j - 8) + e, :] for e in range(2)]
                t1_sums(8 + 2 * j, dsts)
                split_lo(n + 3, n % RING)
                if j < 4:
                    for tap in range(1, LRU_TAPS):
                        for c in (2 * j, 2 * j + 1):
                            w = C_LCW + 8 * (LRU_TAPS - 1 - tap) + c
                            if tap == 1:
                                dve.wait_ge(cv_tap, c + 1)
                            else:
                                dve.wait_ge(cv_acc, 4 * j + 2 * (tap - 2) + c % 2 + 1)
                            STT(xcT[:, c, tap:], xbT[:, c, 0:S - tap], prm[:, w:w + 1], xcT[:, c, tap:], ALU.mult,
                                ALU.add).then_inc(xc_ready if tap == LRU_TAPS - 1 else cv_acc, 1)
                if j == 6:
                    dve.wait_ge(gate_sig, KD)
                    for h in range(2):
                        cs = slice(4 * h, 4 * h + 4)
                        TT(iT[:, cs, :], iT[:, cs, :], xcT[:, cs, :], ALU.mult).then_inc(l_ix, 1)
                if j == 7:
                    for h in range(2):
                        cs = slice(4 * h, 4 * h + 4)
                        dve.wait_ge(l_exp, 4 * h + 4)
                        dve.wait_ge(l_ix, h + 1)
                        TT(xcT[:, cs, :], xbT[:, cs, :], xbT[:, cs, :], ALU.mult).then_inc(l_a2, 1)
                    for h in range(2):
                        cs = slice(4 * h, 4 * h + 4)
                        dve.wait_ge(l_tanh, 4 * h + 4)
                        dve.wait_ge(l_a2, h + 1)
                        STT(tT[:, cs, :], xcT[:, cs, :], 1.0, tT[:, cs, :], ALU.add, ALU.mult).then_inc(l_gain2, 1)

            def recurrence(h):
                cs = slice(4 * h, 4 * h + 4)
                dve.wait_ge(l_sqrt, h + 1)
                TT(iT[:, cs, :], iT[:, cs, :], rT[:, cs, :], ALU.mult).then_inc(l_bt, 1)
                dve.wait_ge(l_bt, h + 1)
                for c in range(4 * h, 4 * h + 4):
                    nc.vector.tensor_tensor_scan(tT[:, c, :], xbT[:, c, :], iT[:, c, :], 0.0, ALU.mult,
                                                 ALU.add).then_inc(l_h, 1)
                dve.wait_ge(l_gelu, h + 1)
                dve.wait_ge(l_h, 4 * h + 4)
                TT(xbT[:, cs, :], tT[:, cs, :], gbT[:, cs, :], ALU.mult).then_inc(l_y, 1)

            mem_spans = ((0, S), (S, 2 * S))

            def mem_heads(base):
                for h in range(MEM_H):
                    m = base + h
                    dve.wait_ge(at_s, m + 1)
                    softmax_max(m, mem_spans, A[m % 2][:, :], MEM_HD ** -0.5)
                    softmax_scale(m, mem_spans)
                    attention_lo(m, KD + h)

            recurrence(0)
            recurrence(1)
            mem_heads(0)
            for h in range(2):
                cs = slice(4 * h, 4 * h + 4)
                dve.wait_ge(l_yhi, h + 1)
                TT(cat[:, cs, 1, :], xbT[:, cs, :], cat[:, cs, 0, :].bitcast(fp32), ALU.subtract).then_inc(l_ylo, 1)
            for n in range(U_LRU_OUT, U_FFN0):
                split_lo(n + 3, n % RING)
            residual(0, U_FFN0 - 1)
            norm_stats(2, x, res_done, 4)
            norm_lo(2, hT, C_FFN)

            def ffn(l, first):
                cw = C_F[l]

                def half(i, h, nxt, slot):
                    for c in range(2):
                        dve.wait_ge(f_low[l], i * 4 + (2 * h + c + 1))
                        TT(ffn_u[:, 2 * h + c, :], U[2 * h + c][:, 0:S], ffn_low[:, 2 * h + c, :],
                           ALU.add).then_inc(f_sum[l], 1)
                    split_lo(nxt, slot)
                    for c in range(2):
                        ch = i * 2 + (h * (FC // 2) + c)
                        k = 2 * h + c
                        dve.wait_ge(f_tap[l], i * 4 + (k + 1))
                        STT(ffn_y[:, k, 1:], ffn_u[:, k, 0:S - 1], prm[:, ds(cw + FC + ch, 1)], ffn_y[:, k, 1:], ALU.mult,
                            ALU.add).then_inc(f_acc[l], 1)
                    for c in range(2):
                        ch = i * 2 + (h * (FC // 2) + c)
                        k = 2 * h + c
                        dve.wait_ge(f_acc[l], i * 4 + (k + 1))
                        STT(ffn_y[:, k, 2:], ffn_u[:, k, 0:S - 2], prm[:, ds(cw + ch, 1)], ffn_y[:, k, 2:], ALU.mult,
                            ALU.add).then_inc(f_conv[l], 1)

                def tail(i, nxt, slot):
                    dve.wait_ge(f_silu[l], i + 1)
                    dve.wait_ge(f_conv[l], i * 4 + 4)
                    TT(ffn_p[:, :, :], ffn_g[:, :, :], ffn_y[:, 2:4, :], ALU.mult).then_inc(f_prod[l], 1)
                    if nxt is not None:
                        split_lo(nxt, slot)
                    dve.wait_ge(f_hi[l], i + 1)
                    TT(cat[:, 0:2, 1, :], ffn_p[:, :, :], cat[:, 0:2, 0, :].bitcast(fp32), ALU.subtract).then_inc(f_lo[l], 1)

                half(0, 0, first + 3, 0)
                half(0, 1, first + 4, 1)
                tail(0, None, 0)
                with dve.Fori(1, NPAIR - 1) as i:
                    half(i, 0, first + 2 + i * 3, 2)
                    half(i, 1, first + 3 + i * 3, 0)
                    tail(i, first + 4 + i * 3, 1)
                i = NPAIR - 1
                half(i, 0, first + 2 + 3 * i, 2)
                half(i, 1, first + 3 + 3 * i, 0)
                tail(i, first + 4 + 3 * i, 1)
                split_lo(first + 5 + 3 * i, 2)

            ffn(0, U_FFN0)
            residual(1, U_IDX - 1)
            norm_stats(3, x, res_done, 8)
            norm_lo(3, hT, C_MIX + KD)

            def rope(v, half, f0, done, count):
                heads = v.shape[2]
                a, b = v[:, :, :, 0:half], v[:, :, :, half:2 * half]
                sin, cos = (trig[:, r, :, f0:f0 + half].unsqueeze(2).broadcast_to((P, NT, heads, half)) for r in range(2))
                n = NT * heads * half
                t0, t1, t2, t3 = (rope_t[:, r, 0:n].rearrange("p (t h d) -> p t h d", t=NT, h=heads) for r in range(4))
                TT(t0, a, cos, ALU.mult)
                TT(t1, b, sin, ALU.mult)
                TT(t2, b, cos, ALU.mult)
                link(TT(t3, a, sin, ALU.mult))
                TT(a, t0, t1, ALU.subtract)
                TT(b, t2, t3, ALU.add).then_inc(done, 1)
                dve.wait_ge(done, count)

            def dsa_splits(n):
                split_lo(n + 3, n % RING)
                split_lo(n + 4, (n + 1) % RING)

            dve.wait_ge(trig_ready, 1)
            dsa_splits(U_IDX)
            dsa_splits(U_IDX + 2)
            dve.wait_ge(t2_done, 4 + 4)
            rope(iq_tok[:, :, :, :], IROT // 2, AROT // 2, rope_i, 1)
            rope(ikw_tok[:, :, 0:ID].unsqueeze(2), IROT // 2, AROT // 2, rope_i, 2)
            dve.wait_ge(ik_zero, 1)
            for e in range(2):
                nc.vector.tensor_copy(ikpad[:, :, e, ID * e:ID * e + ID], ikw_tok[:, :, 0:ID])
            TS(ikw_tok[:, :, ID:], ikw_tok[:, :, ID:], IH ** -0.5, None, ALU.mult).then_inc(ik_copied, 1)
            dsa_splits(U_QKV)
            dsa_splits(U_QKV + 2)
            dsa_splits(U_QKV + 4)
            dve.wait_ge(ik_copied, 1)
            for hp in range(IH // 2):
                for t in range(NT):
                    step = NT * hp + t
                    width = (t + 1) * P
                    dst = score[:, 0:P] if t == 0 else score[:, P:3 * P]
                    dve.wait_ge(ix_relu, step + 1)
                    for e in range(2):
                        h = 2 * hp + e
                        src = prob[:, step % 2, e * width:(e + 1) * width]
                        w = ikw_tok[:, t, ID + h:ID + h + 1]
                        if h == 0:
                            TS(dst, src, w, None, ALU.mult).then_inc(ix_acc, 1)
                        else:
                            dve.wait_ge(ix_acc, 2 * step + e if e else 2 * step - 2)
                            STT(dst, src, w, dst, ALU.mult, ALU.add).then_inc(ix_acc, 1)
            dve.wait_ge(causal_s, 1)
            spans = ((0, P), (P, 3 * P))

            def top_round(r):
                for t, (lo, hi_) in enumerate(spans):
                    if r:
                        dve.wait_ge(top_s, 4 * r - 1 + t)
                    nc.vector.max(top8[:, t, :], score[:, lo:hi_]).then_inc(top_s, 1)
                for t, (lo, hi_) in enumerate(spans):
                    dve.wait_ge(top_s, 4 * r + 1 + t)
                    nc.vector.match_replace(score[:, lo:hi_], top8[:, t, :], score[:, lo:hi_], PICKED).then_inc(top_s, 1)

            for r in range(TOPK // 8):
                top_round(r)
                if r == 2:
                    dsa_splits(U_QKV + 6)
                if r == 5:
                    dsa_splits(U_QKV + 8)
            dve.wait_ge(top_s, 4 * (TOPK // 8))
            TS(kbias, score, PICKED, FILL, ALU.not_equal, ALU.mult).then_inc(bias_s, 1)
            dve.wait_ge(t2_done, 4 + 12)
            for half in range(2):
                rope(qk_tok[:, :, AH * half:AH * half + AH, :], AROT // 2, 0, rope_q, half + 1)
            dsa_splits(U_QKV + 10)
            for j in range(2):
                n = U_DMQ + j
                t1_sums(28 + 2 * j, [mqT[:, 2 * j + e, :] for e in range(2)])
                split_lo(n + 3, n % RING)
            mem_heads(4)
            dve.wait_ge(bias_ready, 1)
            for h in range(AH):
                m = 8 + h
                b = m % 2
                dve.wait_ge(at_s, m + 1)
                STT(prob[:, b, 0:3 * P], A[b][:, 0:3 * P], AD ** -0.5, kbias, ALU.mult, ALU.add).then_inc(at_sc, 1)
                dve.wait_ge(at_sc, h + 1)
                softmax_max(m, spans, prob[:, b, :], 1.0)
                softmax_scale(m, spans)
                attention_lo(m, h)
            for n in range(U_DSA_OUT, U_FFN1):
                split_lo(n + 3, n % RING)
            residual(2, U_FFN1 - 1)
            norm_stats(4, x, res_done, 12)
            norm_lo(4, hT, C_FFN + KD)
            ffn(1, U_FFN1)
            residual(3, U_END - 1)
            norm_stats(5, x, res_done, 16)
            dve.wait_ge(fg_in_s, 16)
            for t in range(NT):
                STT(xn[:, t, :], x[:, t, :], rstd[:, t:t + 1], fin_g, ALU.mult, ALU.mult).then_inc(out_ready, 1)

        @block.tensor
        def _(pe):
            mm = nc.tensor.matmul

            def transpose(dst, src):
                return nc.tensor.transpose(dst, src, ident[0:src.shape[0], 0:src.shape[0]])

            def weights(n):
                pe.wait_ge(lo_ready, n + 1)

            def norm_transpose(k, src):
                for t in range(NT):
                    pe.wait_ge(xn_ready, 2 * k + t + 1)
                for b in range(4):
                    for e in range(2):
                        c = 2 * b + e
                        for t in range(NT):
                            ins = transpose(U[b][:, e * S + t * P:e * S + (t + 1) * P], src[:, t, c * P:(c + 1) * P])
                    ins.then_inc(n_tr, 1)

            def chan_major(slot, e, rhs, bank):
                for k in range(8):
                    at = k * 256 + e * P
                    hi_args = (bank[:, :], w_hi[:, slot, at:at + P], rhs[:, k, :, :].rearrange("p a s -> p (a s)"))
                    lo_args = (bank[:, 0:S], w_lo[:, slot, at:at + P], rhs[:, k, 0, :])
                    if k < 7:
                        mm(*hi_args, start=(k == 0), stop=False)
                        mm(*lo_args, start=False, stop=False)
                    else:
                        mm(*lo_args, start=False, stop=False)
                        last = mm(*hi_args, start=False, stop=True)
                return last

            def tok_major(slot, width, ktiles, lhs, k0, first, last, bank_of, done=None):
                nn = (width + 511) // 512
                for t in range(NT):
                    for k in range(ktiles):
                        hi_l = lhs[:, k0 + k, 0, t * P:(t + 1) * P]
                        lo_l = lhs[:, k0 + k, 1, t * P:(t + 1) * P]
                        w = [(n, n * 512, min(width, n * 512 + 512)) for n in range(nn)]
                        for part_no, (l_, src) in enumerate(((hi_l, w_hi), (hi_l, w_lo), (lo_l, w_hi))):
                            for n, a, b in w:
                                ins = mm(bank_of(t, n)[:, 0:b - a], l_, src[:, slot, k * width + a:k * width + b],
                                         start=(first and k == 0 and part_no == 0),
                                         stop=(last and k == ktiles - 1 and part_no == 2))
                    if done is not None and t == 0:
                        ins.then_inc(done, 1)
                return ins

            def t1_unit(n, t1, rhs):
                weights(n)
                for e in range(2):
                    if t1 + e >= 4:
                        pe.wait_ge(t1_sum, t1 + e - 3)
                    ins = chan_major(n % RING, e, rhs, U[(t1 + e) % 4])
                ins.then_inc(unit_done, 1)

            def out_units(first, lhs):
                for j, k0 in enumerate(out_order):
                    n = first + j
                    if k0 == 0 and first == U_LRU_OUT:
                        pe.wait_ge(l_ylo, 2)
                    weights(n)
                    last = j == 5
                    tok_major(n % RING, D, 2, lhs, k0, j == 0, last, lambda t, h: A[2 * t + h],
                              tile_done if last else None).then_inc(unit_done, 1)

            pe.wait_ge(consts, 1)
            pe.wait_ge(rows_in_s, 16 * 14)
            nw2 = (FFN_TAPS + 1) * FC - P
            transpose(U[0][:, 0:C_MISC], rows[0:C_MISC, 0, :])
            for l in range(2):
                transpose(U[0][:, C_F[l]:C_F[l] + P], rows[:, 1 + 2 * l, :])
                last = transpose(U[0][:, C_F[l] + P:C_F[l] + P + nw2], rows[0:nw2, 2 + 2 * l, :])
            last.then_inc(prm_t, 1)
            pe.wait_ge(prm_ready, 1)
            norm_transpose(0, xn)
            pe.wait_ge(n_lo, 4)
            norm_transpose(1, xn)
            for l in range(2):
                for j in range(2):
                    n = U_MEM + 4 * l + j
                    if n == 0:
                        pe.wait_ge(n_lo, 8)
                    t1_unit(n, 4 * l + 2 * j, memT)
                for j in range(2):
                    n = U_MEM + 4 * l + 2 + j
                    weights(n)
                    tok_major(n % RING, 512, 4, memT, 4 * j, j == 0, j == 1,
                              lambda t, h: A[2 * l + t]).then_inc(unit_done, 1)
            for j in range(10):
                t1_unit(U_LRU_IN + j, 8 + 2 * j, hT)
                if j == 5:
                    pe.wait_ge(bd_in_s, 64)
                    pe.wait_ge(t2_done, 4)
                    for c in range(KD):
                        pe.wait_ge(xc_ready, c + 1)
                        if c >= 4:
                            pe.wait_ge(gate_sig, c - 3)
                        mm(A[c % 4][:, 0:S], w_bd[:, 0, c, :], xcT[:, c, :], start=True, stop=True)
                        mm(A[c % 4][:, S:2 * S], w_bd[:, 1, c, :], xcT[:, c, :], start=True, stop=True).then_inc(gate_mm, 1)

            def att_scores(m, h, l):
                b = m % 2
                if m >= 2:
                    pe.wait_ge(at_exp, m - 1)
                if l is not None:
                    for t in range(NT):
                        ins = mm(A[b][:, t * S:(t + 1) * S], mqT[:, h, t * P:(t + 1) * P], mkT[:, l, h, :],
                                 start=True, stop=True)
                else:
                    mm(A[b][:, 0:P], qkT[:, h, 0:P], qkT[:, AH + h, 0:P], start=True, stop=True)
                    ins = mm(A[b][:, P:3 * P], qkT[:, h, P:2 * P], qkT[:, AH + h, :], start=True, stop=True)
                ins.then_inc(at_s, 1)

            def att_values(m, h, l):
                b = m % 2
                pe.wait_ge(at_p, m + 1)
                if m >= 2:
                    pe.wait_ge(at_pt, m - 1)
                if l is not None:
                    for k in range(NT):
                        for t in range(NT):
                            ins = transpose(A[2 + b][:, k * S + t * P:k * S + (t + 1) * P],
                                            prob[:, b, t * S + k * P:t * S + (k + 1) * P])
                else:
                    transpose(A[2 + b][:, 0:P], prob[:, b, 0:P])
                    transpose(A[2 + b][:, P:2 * P], prob[:, b, P:2 * P])
                    ins = transpose(A[2 + b][:, 2 * P:3 * P], prob[:, b, 2 * P:3 * P])
                ins.then_inc(at_t, 1)
                pe.wait_ge(at_pt, m + 1)
                if m >= 2:
                    pe.wait_ge(at_lo, m - 1)
                if l is not None:
                    for k in range(NT):
                        ins = mm(U[b][:, 0:S], mv[:, l, k, h * P:(h + 1) * P], probT[:, b, k * S:(k + 1) * S],
                                 start=(k == 0), stop=(k == 1))
                else:
                    mm(U[b][:, 0:S], v_tok[:, 0, h * P:(h + 1) * P], probT[:, b, 0:S], start=True, stop=False)
                    ins = mm(U[b][:, P:S], v_tok[:, 1, h * P:(h + 1) * P], probT[:, b, S:S + P], start=False, stop=True)
                ins.then_inc(at_o, 1)

            def heads(base, n, l):
                att_scores(base, 0, l)
                for h in range(n):
                    if h + 1 < n:
                        att_scores(base + h + 1, h + 1, l)
                    att_values(base + h, h, l)

            pe.wait_ge(gate_sig, KD)
            pe.wait_ge(t1_sum, 28)
            heads(0, MEM_H, 0)
            pe.wait_ge(at_lo, MEM_H)
            out_units(U_LRU_OUT, cat)
            norm_transpose(2, xn)

            def ffn(l, first, k):
                def up(i, h, n, slot):
                    weights(n)
                    if not (isinstance(i, int) and i == 0):
                        pe.wait_ge(f_sum[l], i * 4 - 4 + (2 * h + 2))
                    for c in range(2):
                        ins = chan_major(slot, c, hT, U[2 * h + c])
                    ins.then_inc(unit_done, 1)

                def down(i, n, slot, first_, last_):
                    weights(n)
                    pe.wait_ge(f_lo[l], i + 1)
                    tok_major(slot, D, 2, cat, 0, first_, last_, lambda t, h: A[2 * t + h],
                              tile_done if last_ else None).then_inc(unit_done, 1)

                pe.wait_ge(n_lo, 4 * k + 4)
                up(0, 0, first, 0)
                up(0, 1, first + 1, 1)
                up(1, 0, first + 2, 2)
                up(1, 1, first + 3, 0)
                down(0, first + 4, 1, True, False)
                with pe.Fori(2, NPAIR) as i:
                    up(i, 0, first - 1 + i * 3, 2)
                    up(i, 1, first + i * 3, 0)
                    down(i - 1, first + 1 + i * 3, 1, False, False)
                down(NPAIR - 1, first + 3 * NPAIR - 1, 2, False, True)

            ffn(0, U_FFN0, 2)
            norm_transpose(3, xn)
            pe.wait_ge(n_lo, 16)

            def chunk(s):
                if s >= 2:
                    pe.wait_ge(t2_done, 4 + 2 * (s - 1))
                width = ID + IH if s == 1 else 512
                for j in range(2):
                    n = U_IDX + 2 * s + j
                    weights(n)
                    tok_major(n % RING, width, 4, hT, 4 * j, j == 0, j == 1,
                              lambda t, h: A[2 * (s % 2) + t]).then_inc(unit_done, 1)

            for s in range(4):
                chunk(s)
            pe.wait_ge(rope_i, 2)
            pe.wait_ge(ik_copied, 1)
            iq_f = iq_tok[:, :, :, :].rearrange("p t h d -> p t (h d)")
            for b in range(3):
                for e in range(2):
                    for t in range(NT):
                        src = ikpad[:, t, e, :] if b == 2 else iq_f[:, t, (2 * b + e) * P:(2 * b + e + 1) * P]
                        ins = transpose(U[b][:, e * S + t * P:e * S + (t + 1) * P], src)
                ins.then_inc(ix_tr, 1)
            chunk(4)
            pe.wait_ge(ix_trc, 3)
            for hp in range(IH // 2):
                for t in range(NT):
                    step = NT * hp + t
                    width = (t + 1) * P
                    if step >= 4:
                        pe.wait_ge(ix_relu, step - 3)
                    for e in range(2):
                        ins = mm(U[step % 4][:, e * width:(e + 1) * width], iqT[:, hp, t * P:(t + 1) * P],
                                 ikT[:, e, 0:width], start=True, stop=True)
                    ins.then_inc(ix_mm, 1)
            for s in range(5, 8):
                chunk(s)
            pe.wait_ge(ix_relu, 8)
            for j in range(2):
                t1_unit(U_DMQ + j, 28 + 2 * j, hT)
            pe.wait_ge(t1_sum, 32)
            pe.wait_ge(rope_q, 2)
            qk_f = qk_tok[:, :, :, :].rearrange("p t h d -> p t (h d)")
            for b in range(8):
                if b >= 4:
                    pe.wait_ge(q_trc, b - 3)
                for e in range(2):
                    for t in range(NT):
                        ins = transpose(U[b % 4][:, e * S + t * P:e * S + (t + 1) * P],
                                        qk_f[:, t, (2 * b + e) * P:(2 * b + e + 1) * P])
                ins.then_inc(q_tr, 1)
            pe.wait_ge(q_trc, 8)
            pe.wait_ge(t2_done, 4 + 16)
            heads(4, MEM_H, 1)
            heads(8, AH, None)
            pe.wait_ge(at_lo, 16)
            out_units(U_DSA_OUT, cat)
            norm_transpose(4, xn)
            ffn(1, U_FFN1, 4)


_INS = ["x", "mem", "positions", "norm_mix", "norm_ffn", "mem_norm", "final_norm", "w_mem_kv", "w_ffn_up", "ffn_conv_w",
        "ffn_conv_b", "w_ffn_down", "lru_w_in", "lru_conv_w", "lru_conv_b", "lru_w_a", "lru_b_a", "lru_w_x", "lru_b_x",
        "lru_lambda", "lru_w_out", "dsa_w_in", "dsa_w_out"]


def kernel(**inputs):
    import numpy as _np
    import concourse.bacc as _bacc
    from concourse import mybir as _mybir
    from concourse.bass_utils import run_bass_kernel_spmd as _run

    nc = _bacc.Bacc("TRN2", target_bir_lowering=False, num_devices=1)
    arrays, args = {}, []
    for name in _INS:
        a = _np.ascontiguousarray(inputs[name])
        arrays[f"in_{name}_dram"] = a
        args.append(nc.dram_tensor(f"in_{name}_dram", a.shape, _mybir.dt.from_np(a.dtype), kind="ExternalInput").ap())
    args.append(nc.dram_tensor("out_0_dram", (1, S, D), _mybir.dt.from_np(_np.dtype("float32")), kind="ExternalOutput").ap())
    trunk(nc, *args)
    r = _run(nc, [arrays], core_ids=[0])
    return r.results[0]["out_0_dram"]
```

```python
import math
from contextlib import ExitStack

import numpy as np
import concourse.bass as bass
from concourse import mybir


P = 128
S = 256
D = 1024
NT = S // P
KD = D // P
MEM_H, MEM_HD = 4, 128
MEM_W = MEM_H * MEM_HD
LRU_TAPS = 4
FF = 2816
FFN_TAPS = 3
AH, AD = 8, 128
AROT = AD // 4
IH, ID = 8, 64
IROT = ID // 4
TOPK = min(256, S // 4)
NPAIR = FF // (2 * P)
FC = 2 * FF // P
CAT = (D + MEM_W) // P
EPS = 1e-6
THETA = 500000.0
FILL = -3.0e38
PICKED = -3.4e38

L0_GROUPS = [("chan", "x0"), ("chan", "x1"), ("chan", "x2"), ("chan", "x3"), ("chan", "mq0"), ("chan", "mq1"),
             ("chan", "mk0"), ("chan", "mk1"), ("tok", "mv"),
             ("chan", "gate0"), ("chan", "gate1"), ("chan", "gate2"), ("chan", "gate3")]
FILL1_GROUPS = [("chan", "mk0"), ("chan", "mk1")]
FILL2_GROUPS = [("tok", "mv")]
L1_GROUPS = [("tok", "iq"), ("tok", "ikw"), ("chan", "mq0"), ("chan", "mq1"),
             ("tok", "v0"), ("tok", "q0"), ("tok", "k0"), ("tok", "q1"), ("tok", "k1"), ("tok", "v1")]


class Group:

    def __init__(self, kind, name, layer, unit, turn, chans, toks):
        self.kind, self.name, self.layer, self.unit, self.pair = kind, name, layer, unit, turn % 2
        self.units = 1 if kind == "chan" else 2
        self.before = chans if kind == "chan" else toks
        self.after = self.before + 2


def place_groups():
    unit, chans, toks, placed, starts = 0, 0, 0, {}, {}
    for key, layer, groups in (("l0", 0, L0_GROUPS), ("out0", 0, 6), ("fill1", 1, FILL1_GROUPS), ("ffn0", 0, 3 * NPAIR),
                               ("fill2", 1, FILL2_GROUPS), ("l1", 1, L1_GROUPS), ("out1", 1, 6), ("ffn1", 1, 3 * NPAIR)):
        starts[key] = unit
        if isinstance(groups, int):
            unit += groups
            continue
        placed[key] = []
        for turn, (kind, name) in enumerate(groups):
            g = Group(kind, name, layer, unit, turn, chans, toks)
            placed[key].append(g)
            unit += g.units
            if kind == "chan":
                chans += 2
            else:
                toks += 2
    return placed, starts, unit


GROUPS, START, U_END = place_groups()
U_OUT = (START["out0"], START["out1"])
U_FFN = (START["ffn0"], START["ffn1"])
RING = 3

C_MIX, C_FFN, C_MEM, C_LCW, C_LCB, C_BA, C_BX, C_LAM = 0, 16, 32, 40, 72, 80, 88, 96
C_MISC = 104
C_F = (C_FFN_W0, C_FFN_W1) = (C_MISC, C_MISC + (FFN_TAPS + 1) * FC)
NPRM = C_MISC + 2 * (FFN_TAPS + 1) * FC


def trunk(nc, x_in, mem_in, pos_in, norm_mix, norm_ffn, mem_norm, final_norm, w_mem_kv, w_ffn_up, ffn_conv_w,
          ffn_conv_b, w_ffn_down, lru_w_in, lru_conv_w, lru_conv_b, lru_w_a, lru_b_a, lru_w_x, lru_b_x,
          lru_lambda, lru_w_out, dsa_w_in, dsa_w_out, out):
    fp32, f32r, i32 = mybir.dt.float32, mybir.dt.float32r, mybir.dt.int32
    ALU, ACT, AX = mybir.AluOpType, mybir.ActivationFunctionType, mybir.AxisListType
    ds = bass.ds

    with ExitStack() as ctx:
        def sb(name, shape, dt=fp32):
            return ctx.enter_context(nc.sbuf_tensor(name, shape, dt))

        def sem(name):
            return ctx.enter_context(nc.semaphore(name))

        w_raw = sb("w_raw", [P, RING, 2048])
        w_hi = sb("w_hi", [P, RING, 2048], f32r)
        w_lo = sb("w_lo", [P, RING, 2048], f32r)
        x = sb("x_res", [P, NT, D])
        hT = sb("hT", [P, KD, 2, S], f32r)
        memT = sb("memT", [P, KD, 2, S], f32r)
        cat = sb("cat", [P, CAT, 2, S], f32r)
        mkT = sb("mkT", [P, MEM_H, S])
        mv = sb("mv", [P, NT, MEM_W])
        mqT = sb("mqT", [P, MEM_H, S])
        ident = sb("ident", [P, P])
        prm = sb("prm", [P, NPRM])
        trig = sb("trig", [P, 2, NT, 24])
        eps_t = sb("eps_t", [P, 1])
        warm = sb("warm", [P, 1])
        ssq = sb("ssq", [P, NT])
        std = sb("std", [P, NT])
        rstd = sb("rstd", [P, NT])
        sp8 = sb("sp8", [P, 2, KD])
        smax = sb("smax", [P, 2, NT])
        nmax = sb("nmax", [P, 2, NT])
        ssum = sb("ssum", [P, 2, NT])
        rsum = sb("rsum", [P, 2, NT])
        scratch = sb("scratch", [P, 2048])
        arena = sb("arena", [P, 12 * 1024])

        xn = scratch[:, :].rearrange("p (t d) -> p t d", t=NT)
        prob = scratch[:, 0:1024].rearrange("p (b n) -> p b n", b=2)
        probT = scratch[:, 1024:1536]
        chan_low = scratch[:, 1536:2048].rearrange("p (e s) -> p e s", e=2)

        def part(kib, n, pattern=None, **dims):
            v = arena[:, kib * 256:kib * 256 + n]
            return v.rearrange(pattern, **dims) if pattern else v

        B = [part(8 * n, 2048, "p (c s) -> p c s", c=KD) for n in range(6)]
        xbT, xcT, rT, iT, gbT, tT = B
        w_bd = part(40, 2048, "p (w c n) -> p w c n", w=2, c=KD)
        rows = part(16, 640, "p (r c) -> p r c", r=5)
        junk = part(20, 1024)
        mem_tok = part(32, 2048, "p (t d) -> p t d", t=NT)
        inv_t = part(24, NT * 24, "p (t f) -> p t f", t=NT)
        ang = part(25, NT * 24, "p (t f) -> p t f", t=NT)
        turns = part(26, NT * 24, "p (t f) -> p t f", t=NT)
        wrap = part(27, NT * 24, "p (t f) -> p t f", t=NT)
        pos_i = part(28, NT).bitcast(i32)
        pos_f = part(29, NT)
        lam_t = part(30, 6 * KD, "p (r c) -> p r c", r=6)
        ffn_low = part(0, 1024, "p (c s) -> p c s", c=4)
        ffn_u = part(4, 1024, "p (c s) -> p c s", c=4)
        ffn_y = part(8, 1024, "p (c s) -> p c s", c=4)
        ffn_g = part(12, 512, "p (c s) -> p c s", c=2)
        ffn_p = part(14, 512, "p (c s) -> p c s", c=2)
        fill_low = part(20, 512, "p (e s) -> p e s", e=2)
        qk_tok = part(0, 4096, "p (t h d) -> p t h d", t=NT, h=2 * AH)
        v_tok = part(16, 2048, "p (t d) -> p t d", t=NT)
        qkT = part(24, 4096, "p (h s) -> p h s", h=2 * AH)
        ikT = part(28, 512, "p (e s) -> p e s", e=2)
        ikpad = part(30, 512, "p (t e d) -> p t e d", t=NT, e=2)
        iqT = part(32, 1024, "p (c s) -> p c s", c=4)
        iq_tok = part(36, 1024, "p (t h d) -> p t h d", t=NT, h=IH)
        score = part(40, 384)
        kbias = arena[:, 40 * 256 + 384:40 * 256 + 768]
        ikw_tok = part(43, 144, "p (t d) -> p t d", t=NT)
        top8 = arena[:, 43 * 256 + 144:43 * 256 + 160].rearrange("p (t d) -> p t d", t=NT)
        rope_t = part(44, 4 * 128 * NT // 2 * 2, "p (r n) -> p r n", r=4)
        fin_g = part(20, D)

        U = [ctx.enter_context(nc.psum_tensor(f"ps_u{n}", [P, 512], fp32)) for n in range(4)]
        A = [ctx.enter_context(nc.psum_tensor(f"ps_a{n}", [P, 512], fp32)) for n in range(4)]
        SCORES, TURNED, VALUES = U[0:2], U[2], U[3]

        x_in_s = [sem(f"x_loaded{t}") for t in range(NT)]
        mem_in_s, gain_in_s, rows_in_s, taps_in_s, pos_in_s, bd_in_s, fg_in_s = (
            sem(n) for n in ("mem_loaded", "gain_loaded", "rows_loaded", "taps_loaded", "pos_loaded", "bd_loaded", "fg_loaded"))
        raw_in = [sem(f"raw_loaded{n}") for n in range(RING)]
        out_ready, out_s = sem("out_ready"), sem("out_stored")
        hi_ready, lo_ready, unit_done = sem("hi_ready"), sem("lo_ready"), sem("unit_done")
        eps_ready, zeroed, consts, inv_ready, bd_zero = sem("eps_ready"), sem("zeroed"), sem("consts"), sem("inv_ready"), sem("bd_zero")
        prm_t, prm_ready = sem("prm_transposed"), sem("prm_ready")
        chain = sem("dve_chain")
        lam_exp, lam_ready = sem("lam_exp"), sem("lam_ready")
        trig_args, trig_ready = sem("trig_args"), sem("trig_ready")
        sq_s, std_s, rstd_s, xn_ready = (sem(n) for n in ("squares", "std", "rstd", "xn_ready"))
        n_tr, n_hi, n_lo = sem("norm_transposed"), sem("norm_hi"), sem("norm_lo")
        tile_done, res_done = sem("tile_done"), sem("res_done")
        lowed, summed, copied = sem("chan_lowed"), sem("chan_summed"), sem("tok_copied")
        cv_tap, cv_acc, xc_ready = sem("conv_tap"), sem("conv_acc"), sem("xc_ready")
        gate_mm, gate_sig = sem("gate_mm"), sem("gate_sig")
        l_exp, l_tanh, l_ix, l_a2, l_gain2, l_sqrt, l_bt, l_h, l_gelu, l_y, l_yhi, l_ylo = (
            sem("lru_" + n) for n in ("exp", "tanh", "ix", "a2", "gain2", "sqrt", "bt", "h", "gelu", "y", "yhi", "ylo"))
        at_s, at_sc, at_max, at_nmax, at_exp, at_rs, at_p, at_t, at_pt, at_o, at_hi, at_lo = (
            sem("att_" + n) for n in ("s", "sc", "max", "nmax", "exp", "rsum", "p", "t", "pt", "o", "hi", "lo"))
        ik_zero, rope_i, ik_copied = sem("ik_zero"), sem("rope_i"), sem("ik_copied")
        ix_tr, ix_trc, ix_mm, ix_relu, ix_acc = (sem("idx_" + n) for n in ("tr", "trc", "mm", "relu", "acc"))
        causal_s, top_s, bias_s, bias_ready = sem("causal"), sem("top"), sem("bias"), sem("bias_ready")
        rope_q, q_tr, q_trc = sem("rope_q"), sem("q_tr"), sem("q_trc")
        f_low, f_sum, f_tap, f_acc, f_conv, f_silu, f_prod, f_hi, f_lo = (
            [sem(f"ffn{l}_{n}") for l in range(2)]
            for n in ("lowed", "summed", "tap", "acc", "conv", "silu", "prod", "hi", "lo"))

        block = ctx.enter_context(nc.Block())

        def kxc(w, k0, k, c0, c):
            return k, c, w[k0 * P:(k0 + k) * P, c0:c0 + c].rearrange("(k p) c -> p k c", p=P)

        kv, lru_in, dsa_in = w_mem_kv, lru_w_in[0], dsa_w_in[0]
        c_idx = 3 * D
        c_ik = c_idx + IH * ID
        sources = {}
        for j in range(4):
            sources[0, f"x{j}"] = (lru_in, 256 * j, 256)
            sources[0, f"gate{j}"] = (lru_in, D + 256 * j, 256)
        for j in range(2):
            sources[0, f"mq{j}"] = (lru_in, 2 * D + 256 * j, 256)
            sources[1, f"mq{j}"] = (dsa_in, c_ik + ID + IH + 256 * j, 256)
            for l in range(2):
                sources[l, f"mk{j}"] = (kv[l], 256 * j, 256)
            for c, name in enumerate("qkv"):
                sources[1, f"{name}{j}"] = (dsa_in, D * c + 512 * j, 512)
        for l in range(2):
            sources[l, "mv"] = (kv[l], MEM_W, MEM_W)
        sources[1, "iq"] = (dsa_in, c_idx, IH * ID)
        sources[1, "ikw"] = (dsa_in, c_ik, ID + IH)
        out_order = (8, 10, 0, 2, 4, 6)

        units = {}
        for key, groups in GROUPS.items():
            for g in groups:
                w, c0, c = sources[g.layer, g.name]
                k = KD // g.units
                for j in range(g.units):
                    units[g.unit + j] = kxc(w, k * j, k, c0, c)
        for l, w in enumerate((lru_w_out[0], dsa_w_out[0])):
            for j, k in enumerate(out_order):
                units[U_OUT[l] + j] = kxc(w, k, 2, 0, D)

        def unit_size(n):
            k, c, _ = units.get(n, (2, 1024, None)) if isinstance(n, int) else (2, 1024, None)
            return k * c

        def group(key, name):
            return next(g for g in GROUPS[key] if g.name == name)

        @block.sync
        def _(sp):
            def load(n, slot, k, c, src):
                if not isinstance(n, int) or n >= RING:
                    sp.wait_ge(lo_ready, n - (RING - 1))
                sp.dma_start(w_raw[:, slot, 0:k * c].rearrange("p (k c) -> p k c", k=k), src).then_inc(raw_in[slot], 16)

            x_v = x_in[0].rearrange("(t p) d -> p t d", p=P)
            for t in range(NT):
                sp.dma_start(x[:, t, :], x_v[:, t, :]).then_inc(x_in_s[t], 16)
            for n in range(2):
                load(n, n, *units[n])
            sp.dma_start(mem_tok[:, :, :], mem_in[0].rearrange("(t p) d -> p t d", p=P)).then_inc(mem_in_s, 16)
            load(2, 2, *units[2])
            for l in range(2):
                taps = ffn_conv_w[l].rearrange("k (r c) -> (k r) c", c=P)
                nw = FFN_TAPS * FC
                sp.dma_start(rows[:, 1 + 2 * l, :], taps[0:P]).then_inc(taps_in_s, 16)
                sp.dma_start(rows[0:nw - P, 2 + 2 * l, :], taps[P:nw]).then_inc(taps_in_s, 16)
                sp.dma_start(rows[nw - P:nw - P + FC, 2 + 2 * l, :],
                             ffn_conv_b[l].rearrange("(r c) -> r c", c=P)).then_inc(taps_in_s, 16)
            for t in range(NT):
                sp.dma_start(pos_i[:, t:t + 1], pos_in[0, t * P:(t + 1) * P].rearrange("(p o) -> p o", o=1)).then_inc(pos_in_s, 16)
            sp.wait_ge(bd_zero, 1)
            for w, src in enumerate((lru_w_a, lru_w_x)):
                two = src[0].rearrange("(c e) i d -> e i c d", e=2)
                for e in range(2):
                    sp.dma_start(w_bd[64 * e:64 * e + 64, w, :, 64 * e:64 * e + 64], two[e]).then_inc(bd_in_s, 16)

            def ffn_loads(l):
                first = U_FFN[l]

                def up(n, i, half, slot):
                    load(n, slot, 8, 256, w_ffn_up[l][:, ds(half * FF + i * 256, 256)].rearrange("(k p) c -> p k c", p=P))

                def down(n, i, slot):
                    load(n, slot, 2, 1024, w_ffn_down[l][ds(i * 256, 256), :].rearrange("(k p) c -> p k c", p=P))

                up(first, 0, 0, first % RING)
                up(first + 1, 0, 1, (first + 1) % RING)
                with sp.Fori(1, NPAIR) as i:
                    up(first - 1 + i * 3, i, 0, (first - 1) % RING)
                    up(first + i * 3, i, 1, first % RING)
                    down(first + 1 + i * 3, i - 1, (first + 1) % RING)
                down(first + 3 * NPAIR - 1, NPAIR - 1, (first + 3 * NPAIR - 1) % RING)

            for n in range(3, U_FFN[0]):
                load(n, n % RING, *units[n])
            ffn_loads(0)
            for n in range(START["fill2"], U_FFN[1]):
                load(n, n % RING, *units[n])
            ffn_loads(1)
            sp.dma_start(fin_g, final_norm.rearrange("(o d) -> o d", o=1).broadcast_to((P, D))).then_inc(fg_in_s, 16)
            out_v = out[0].rearrange("(t p) d -> p t d", p=P)
            for t in range(NT):
                sp.wait_ge(out_ready, t + 1)
                sp.dma_start(out_v[:, t, :], xn[:, t, :]).then_inc(out_s, 16)
            sp.wait_ge(out_s, 16 * NT)

        @block.gpsimd
        def _(pool):
            nc.gpsimd.memset(eps_t[:, :], EPS).then_inc(eps_ready, 1)
            nc.gpsimd.memset(ident[:, :], 0.0).then_inc(zeroed, 1)
            pool.wait_ge(zeroed, 1)
            nc.gpsimd.affine_select(out=ident[:, :], in_=ident[:, :], compare_op=ALU.not_equal, fill=1.0, base=0,
                                    pattern=[[-1, P]], channel_multiplier=1).then_inc(consts, 1)
            for v, at, n in ((norm_ffn, 16, 16), (mem_norm, 32, 8), (lru_conv_w, 40, 32), (lru_conv_b, 72, 8),
                             (lru_b_a, 80, 8), (lru_b_x, 88, 8), (lru_lambda, 96, 8)):
                flat = {1: "(r c) -> r c", 2: "a (r c) -> (a r) c", 3: "a b (r c) -> (a b r) c"}[len(v.shape)]
                pool.dma_start(rows[at:at + n, 0, :], v.rearrange(flat, c=P)).then_inc(rows_in_s, 16)
            nc.gpsimd.memset(w_bd[:, :, :, :], 0.0).then_inc(bd_zero, 1)
            freqs = [THETA ** (-f / AROT) for f in range(0, AROT, 2)] + [THETA ** (-f / IROT) for f in range(0, IROT, 2)]
            for f, v in enumerate(freqs):
                ins = nc.gpsimd.memset(inv_t[:, :, f:f + 1], float(np.float32(v)))
            ins.then_inc(inv_ready, 1)
            for h in range(2):
                cs = slice(4 * h, 4 * h + 4)
                pool.wait_ge(gate_sig, 4 * h + 4)
                nc.gpsimd.tensor_tensor(iT[:, cs, :], iT[:, cs, :], xcT[:, cs, :], ALU.mult).then_inc(l_ix, 1)
            pool.wait_ge(unit_done, START["fill2"])
            nc.gpsimd.memset(ikpad[:, :, :, :], 0.0).then_inc(ik_zero, 1)

            def causal(src, n):
                nc.gpsimd.affine_select(out=src[:, 0:P], in_=src[:, 0:P], compare_op=ALU.is_ge, fill=FILL, base=0,
                                        pattern=[[-1, P]], channel_multiplier=1)
                nc.gpsimd.affine_select(out=src[:, P:3 * P], in_=src[:, P:3 * P], compare_op=ALU.is_ge, fill=FILL,
                                        base=P, pattern=[[-1, S]], channel_multiplier=1).then_inc(n, 1)

            pool.wait_ge(ix_acc, IH * NT)
            causal(score, causal_s)
            pool.wait_ge(bias_s, 1)
            causal(kbias, bias_ready)

        MEM_SPANS, DSA_SPANS = ((0, S), (S, 2 * S)), ((0, P), (P, 3 * P))

        def is_mem(m):
            return m < 2 * MEM_H

        def cat_tile(m):
            return KD + m % MEM_H if is_mem(m) else m - 2 * MEM_H

        @block.scalar
        def _(act):
            def copy(dst, src):
                return nc.scalar.activation(dst, src, ACT.Copy)

            def split_hi(n, slot=None, turn=None):
                if isinstance(n, int):
                    if n >= U_END:
                        return
                    slot, turn = n % RING, 16 * (n // RING + 1)
                act.wait_ge(raw_in[slot], turn)
                if not isinstance(n, int) or n >= RING:
                    act.wait_ge(unit_done, n - (RING - 1))
                size = unit_size(n)
                copy(w_hi[:, slot, 0:size], w_raw[:, slot, 0:size]).then_inc(hi_ready, 1)

            def load_table(func):
                nc.scalar.activation(warm[:, :], eps_t[:, :], func)

            def norm_stats(k, src, scrap):
                for t in range(NT):
                    if k == 0:
                        act.wait_ge(x_in_s[t], 16)
                    elif k == 1:
                        act.wait_ge(mem_in_s, 16)
                    else:
                        act.wait_ge(res_done, 4 * (k - 2) + 2 * t + 2)
                    nc.scalar.activation(scrap[t], src[:, t, :], ACT.Square, accum_out=ssq[:, t:t + 1]).then_inc(sq_s, 1)
                    act.wait_ge(sq_s, 2 * k + t + 1)
                    nc.scalar.activation(std[:, t:t + 1], ssq[:, t:t + 1], ACT.Sqrt, scale=1.0 / D,
                                         bias=eps_t[:, 0:1]).then_inc(std_s, 1)

            def norm_hi(k, dst, gain, banks):
                for b in range(4):
                    act.wait_ge(n_tr, 4 * k + b + 1)
                    for e in range(2):
                        c = 2 * b + e
                        ins = nc.scalar.activation(dst[:, c, 0, :], banks[b][:, e * S:(e + 1) * S], ACT.Copy,
                                                   scale=prm[:, gain + c:gain + c + 1])
                    ins.then_inc(n_hi, 1)

            def chan_lows(g, banks=None, buf=chan_low):
                act.wait_ge(unit_done, g.unit + 1)
                for e in range(2):
                    if g.before:
                        act.wait_ge(summed, g.before + e - 1)
                    src = (banks or A[2 * g.pair:2 * g.pair + 2])[e]
                    copy(buf[:, e, :], src[:, S:2 * S]).then_inc(lowed, 1)

            def tok_copies(g, dsts, banks=None):
                act.wait_ge(unit_done, g.unit + 2)
                for t in range(NT):
                    src = (banks or A[2 * g.pair:2 * g.pair + 2])[t]
                    copy(dsts[t], src[:, 0:dsts[t].free_size()]).then_inc(copied, 1)

            def exp_of(m):
                b = m % 2
                act.wait_ge(at_nmax, m + 1)
                if is_mem(m) and m >= 2:
                    act.wait_ge(at_t, m - 1)
                for t, (lo, hi_) in enumerate(MEM_SPANS if is_mem(m) else DSA_SPANS):
                    src = SCORES[b][:, lo:hi_] if is_mem(m) else prob[:, b, lo:hi_]
                    ins = nc.scalar.activation(prob[:, b, lo:hi_], src, ACT.Exp, bias=nmax[:, b, t:t + 1],
                                               scale=MEM_HD ** -0.5 if is_mem(m) else 1.0, accum_out=ssum[:, b, t:t + 1])
                ins.then_inc(at_exp, 1)

            def turned_of(m):
                act.wait_ge(at_t, m + 1)
                if m:
                    act.wait_ge(at_o, m)
                width = 2 * S if is_mem(m) else 3 * P
                copy(probT[:, 0:width], TURNED[:, 0:width]).then_inc(at_pt, 1)

            def values_hi(m):
                act.wait_ge(at_o, m + 1)
                copy(cat[:, cat_tile(m), 0, :], VALUES[:, 0:S]).then_inc(at_hi, 1)

            def heads(step, lo, hi_):
                if lo <= step - 2 < hi_:
                    values_hi(step - 2)
                if lo <= step - 1 < hi_:
                    turned_of(step - 1)
                if lo <= step < hi_:
                    exp_of(step)

            act.dma_start(rows[0:16, 0, :], norm_mix.rearrange("a (r c) -> (a r) c", c=P)).then_inc(gain_in_s, 16)
            act.wait_ge(eps_ready, 1)
            load_table(ACT.Sqrt)
            norm_stats(0, x, [xn[:, 0, :], xn[:, 1, :]])
            split_hi(0)
            act.wait_ge(prm_t, 1)
            copy(prm[:, 0:16], U[0][:, 0:16]).then_inc(prm_ready, 1)
            act.wait_ge(prm_ready, 1)
            norm_hi(0, hT, C_MIX, A)
            split_hi(1)
            split_hi(2)
            norm_stats(1, mem_tok, [junk, junk])

            def conv_taps(j):
                for c in (2 * j, 2 * j + 1):
                    act.wait_ge(summed, c + 1)
                    nc.scalar.activation(xcT[:, c, :], xbT[:, c, :], ACT.Identity, bias=prm[:, C_LCB + c:C_LCB + c + 1],
                                         scale=prm[:, C_LCW + 24 + c:C_LCW + 25 + c]).then_inc(cv_tap, 1)

            g0 = {g.name: g for g in GROUPS["l0"]}
            for j in range(4):
                g = g0[f"x{j}"]
                chan_lows(g)
                split_hi(g.unit + 3)
                if j == 0:
                    act.wait_ge(prm_t, 2)
                    copy(prm[:, 16:], U[1][:, 16:NPRM]).then_inc(prm_ready, 1)
                    act.wait_ge(prm_ready, 2)
                conv_taps(j)
                if j == 1:
                    norm_hi(1, memT, C_MEM, U)
            act.wait_ge(lam_exp, 1)
            nc.scalar.activation(lam_t[:, 1, :], lam_t[:, 0, :], ACT.Exp, scale=-1.0).then_inc(lam_exp, 1)
            act.wait_ge(trig_args, 1)
            nc.scalar.activation(trig[:, 0], ang[:, :, :], ACT.Sin)
            nc.scalar.activation(trig[:, 1], wrap[:, :, :], ACT.Sin).then_inc(trig_ready, 1)
            load_table(ACT.Sigmoid)
            for name in ("mq0", "mq1"):
                chan_lows(g0[name])
                split_hi(g0[name].unit + 3)
            for c in range(KD):
                act.wait_ge(gate_mm, c + 1)
                nc.scalar.activation(rT[:, c, :], U[c % 4][:, 0:S], ACT.Sigmoid, bias=prm[:, C_BA + c:C_BA + c + 1])
                nc.scalar.activation(iT[:, c, :], U[c % 4][:, S:2 * S], ACT.Sigmoid,
                                     bias=prm[:, C_BX + c:C_BX + c + 1]).then_inc(gate_sig, 1)

            def decay(h):
                act.wait_ge(gate_sig, KD)
                act.wait_ge(lam_ready, 1)
                for c in range(4 * h, 4 * h + 4):
                    nc.scalar.activation(xbT[:, c, :], rT[:, c, :], ACT.Exp, scale=sp8[:, 1, c:c + 1]).then_inc(l_exp, 1)
                    nc.scalar.activation(tT[:, c, :], rT[:, c, :], ACT.Tanh, scale=sp8[:, 0, c:c + 1]).then_inc(l_tanh, 1)
                cs = slice(4 * h, 4 * h + 4)
                act.wait_ge(l_exp, 4 * h + 4)
                act.wait_ge(l_ix, h + 1)
                nc.scalar.activation(xcT[:, cs, :], xbT[:, cs, :], ACT.Square).then_inc(l_a2, 1)

            chan_lows(g0["mk0"])
            split_hi(g0["mk0"].unit + 3)
            decay(0)
            chan_lows(g0["mk1"])
            split_hi(g0["mk1"].unit + 3)
            decay(1)
            load_table(ACT.Sqrt)
            split_hi(g0["mv"].unit + 3)
            for h in range(2):
                cs = slice(4 * h, 4 * h + 4)
                act.wait_ge(l_gain2, h + 1)
                nc.scalar.activation(rT[:, cs, :], tT[:, cs, :], ACT.Sqrt).then_inc(l_sqrt, 1)
            load_table(ACT.Exp)
            tok_copies(g0["mv"], [mv[:, t, :] for t in range(NT)])
            split_hi(g0["mv"].unit + 4)
            for j in range(4):
                g = g0[f"gate{j}"]
                chan_lows(g)
                split_hi(g.unit + 3)
                heads(j, 0, MEM_H)
            heads(4, 0, MEM_H)
            heads(5, 0, MEM_H)
            act.wait_ge(summed, g0["gate3"].after)
            for h in range(2):
                cs = slice(4 * h, 4 * h + 4)
                nc.scalar.activation(gbT[:, cs, :], gbT[:, cs, :], ACT.Gelu_apprx_tanh).then_inc(l_gelu, 1)
            split_hi(U_OUT[0] + 3)
            for h in range(2):
                cs = slice(4 * h, 4 * h + 4)
                act.wait_ge(l_y, h + 1)
                copy(cat[:, cs, 0, :], xbT[:, cs, :]).then_inc(l_yhi, 1)

            def out_and_norm(l, k, gain, dst=hT):
                for j in range(l + 1 - l, 5) if l == 0 else range(5):
                    split_hi(U_OUT[l] + j + 3)
                load_table(ACT.Sqrt)
                norm_stats(k, x, [xn[:, 0, :], xn[:, 1, :]])
                split_hi(U_OUT[l] + 5 + 3)

            out_and_norm(0, 2, None)
            for i, g in enumerate(GROUPS["fill1"]):
                chan_lows(g, U[2 * i:2 * i + 2], fill_low)
                if i == 0:
                    norm_hi(2, hT, C_FFN, A)
                split_hi(g.unit + 3)

            def ffn(l):
                first = U_FFN[l]
                cw, cb = C_F[l], C_F[l] + FFN_TAPS * FC

                def turn(ahead, i):
                    return ((first + ahead) // RING + 1) * 16 + i * 16

                def half(i, h, unit, ahead):
                    act.wait_ge(unit_done, unit + 1)
                    for c in range(2):
                        copy(ffn_low[:, 2 * h + c, :], U[2 * h + c][:, S:2 * S]).then_inc(f_low[l], 1)
                    if ahead is not None:
                        split_hi(first + ahead + i * 3, (first + ahead) % RING, turn(ahead, i))
                    for c in range(2):
                        ch = i * 2 + (h * (FC // 2) + c)
                        act.wait_ge(f_sum[l], i * 4 + (2 * h + c + 1))
                        nc.scalar.activation(ffn_y[:, 2 * h + c, :], ffn_u[:, 2 * h + c, :], ACT.Identity,
                                             bias=prm[:, ds(cb + ch, 1)], scale=prm[:, ds(cw + 2 * FC + ch, 1)]).then_inc(f_tap[l], 1)

                def tail(i, ahead, used):
                    act.wait_ge(f_conv[l], i * 4 + 2)
                    nc.scalar.activation(ffn_g[:, :, :], ffn_y[:, 0:2, :], ACT.Silu).then_inc(f_silu[l], 1)
                    if ahead is not None:
                        split_hi(first + ahead + i * 3, (first + ahead) % RING, turn(ahead, i))
                    if used:
                        act.wait_ge(unit_done, first + 2 + i * 3)
                    act.wait_ge(f_prod[l], i + 1)
                    copy(cat[:, 0:2, 0, :], ffn_p[:, :, :]).then_inc(f_hi[l], 1)

                half(0, 0, first, 3)
                half(0, 1, first + 1, 4)
                tail(0, None, False)
                with act.Fori(1, NPAIR - 1) as i:
                    half(i, 0, first - 1 + i * 3, 2)
                    half(i, 1, first + i * 3, 3)
                    tail(i, 4, True)
                i = NPAIR - 1
                half(i, 0, first - 1 + 3 * i, 2)
                half(i, 1, first + 3 * i, None)
                tail(i, None, True)
                load_table(ACT.Sqrt)
                split_hi(first + 3 + 3 * i)
                split_hi(first + 4 + 3 * i)

            ffn(0)
            norm_stats(3, x, [xn[:, 0, :], xn[:, 1, :]])
            split_hi(START["fill2"] + 2)
            g = GROUPS["fill2"][0]
            split_hi(g.unit + 3)
            tok_copies(g, [mv[:, t, :] for t in range(NT)], U[0:2])
            norm_hi(3, hT, C_MIX + KD, A)
            split_hi(g.unit + 4)

            g1 = {g.name: g for g in GROUPS["l1"]}
            iq_f = iq_tok[:, :, :, :].rearrange("p t h d -> p t (h d)")
            qk_f = qk_tok[:, :, :, :].rearrange("p t h d -> p t (h d)")

            def place(name):
                if name == "iq":
                    return [iq_f[:, t, :] for t in range(NT)]
                if name == "ikw":
                    return [ikw_tok[:, t, :] for t in range(NT)]
                v = v_tok if name[0] == "v" else qk_f
                c0 = 512 * int(name[1]) + (D if name[0] == "k" else 0)
                return [v[:, t, c0:c0 + 512] for t in range(NT)]

            def idx_relu(steps):
                for step in steps:
                    width = (step % NT + 1) * P
                    act.wait_ge(ix_mm, step + 1)
                    if step >= 2:
                        act.wait_ge(ix_acc, 2 * (step - 1))
                    nc.scalar.activation(prob[:, step % 2, 0:2 * width], U[step % 4][:, 0:2 * width], ACT.Relu,
                                         scale=ID ** -0.5).then_inc(ix_relu, 1)

            def qk_turned(c):
                for b in range(4):
                    act.wait_ge(q_tr, 4 * c + b + 1)
                    h = 4 * c + 2 * (b % 2) + AH * (b // 2)
                    copy(qkT[:, h:h + 2, :].rearrange("p h s -> p (h s)"), U[b % 2][:, :]).then_inc(q_trc, 1)

            def dense(name, mid, end):
                g = g1[name]
                if g.kind == "chan":
                    chan_lows(g)
                    split_hi(g.unit + 3)
                else:
                    act.wait_ge(unit_done, g.unit + 1)
                    split_hi(g.unit + 3)
                    mid()
                    tok_copies(g, place(name))
                    split_hi(g.unit + 4)
                end()

            def nothing():
                pass

            dense("iq", nothing, nothing)
            dense("ikw", nothing, nothing)
            dense("mq0", nothing, nothing)
            dense("mq1", nothing, nothing)
            for b in range(3):
                act.wait_ge(ix_tr, b + 1)
                dst = ikT[:, :, :] if b == 2 else iqT[:, 2 * b:2 * b + 2, :]
                copy(dst.rearrange("p c s -> p (c s)"), U[b][:, :]).then_inc(ix_trc, 1)
            dense("v0", lambda: idx_relu((0, 1)), lambda: idx_relu((2, 3)))
            dense("q0", lambda: idx_relu((4, 5)), lambda: idx_relu((6, 7)))
            dense("k0", lambda: heads(4, 4, 16), lambda: heads(5, 4, 16))
            dense("q1", lambda: heads(6, 4, 16), lambda: heads(7, 4, 16))
            dense("k1", lambda: qk_turned(0), lambda: heads(8, 4, 16))
            dense("v1", lambda: heads(9, 4, 16), lambda: (qk_turned(1), heads(10, 4, 16)))
            for step in range(11, 18):
                heads(step, 4, 16)
            out_and_norm(1, 4, None)
            norm_hi(4, hT, C_FFN + KD, A)
            ffn(1)
            norm_stats(5, x, [xn[:, 0, :], xn[:, 1, :]])

        @block.vector
        def _(dve):
            TT, TS, STT = nc.vector.tensor_tensor, nc.vector.tensor_scalar, nc.vector.scalar_tensor_tensor
            links = [0]

            def link(ins):
                links[0] += 1
                ins.then_inc(chain, 1)
                dve.wait_ge(chain, links[0])

            def split_lo(n, slot=None):
                if isinstance(n, int):
                    if n >= U_END:
                        return
                    slot = n % RING
                size = unit_size(n)
                dve.wait_ge(hi_ready, n + 1)
                TT(w_lo[:, slot, 0:size], w_raw[:, slot, 0:size], w_hi[:, slot, 0:size].bitcast(fp32),
                   ALU.subtract).then_inc(lo_ready, 1)

            def norm_scale(k, t, dst, src):
                dve.wait_ge(std_s, 2 * k + t + 1)
                nc.vector.reciprocal(rstd[:, t:t + 1], std[:, t:t + 1]).then_inc(rstd_s, 1)
                dve.wait_ge(rstd_s, 2 * k + t + 1)
                if k < 5:
                    TS(dst[:, t, :], src[:, t, :], rstd[:, t:t + 1], None, ALU.mult).then_inc(xn_ready, 1)

            def norm_lo(k, dst, gain, banks):
                for b in range(4):
                    dve.wait_ge(n_hi, 4 * k + b + 1)
                    for e in range(2):
                        c = 2 * b + e
                        ins = STT(dst[:, c, 1, :], banks[b][:, e * S:(e + 1) * S], prm[:, gain + c:gain + c + 1],
                                  dst[:, c, 0, :].bitcast(fp32), ALU.mult, ALU.subtract)
                    ins.then_inc(n_lo, 1)

            def chan_sums(g, dsts, banks=None, buf=chan_low):
                for e in range(2):
                    dve.wait_ge(lowed, g.before + e + 1)
                    src = (banks or A[2 * g.pair:2 * g.pair + 2])[e]
                    TT(dsts[e], src[:, 0:S], buf[:, e, :], ALU.add).then_inc(summed, 1)

            def scores_max(m):
                b = m % 2
                dve.wait_ge(at_s, m + 1)
                if is_mem(m):
                    src, scale, spans = SCORES[b], MEM_HD ** -0.5, MEM_SPANS
                else:
                    if m >= 2:
                        dve.wait_ge(at_t, m - 1)
                    STT(prob[:, b, 0:3 * P], SCORES[b][:, 0:3 * P], AD ** -0.5, kbias, ALU.mult, ALU.add).then_inc(at_sc, 1)
                    dve.wait_ge(at_sc, m - 2 * MEM_H + 1)
                    src, scale, spans = prob[:, b, :], 1.0, DSA_SPANS
                for t, (lo, hi_) in enumerate(spans):
                    ins = nc.vector.reduce_max(smax[:, b, t:t + 1], src[:, lo:hi_], AX.X)
                ins.then_inc(at_max, 1)
                dve.wait_ge(at_max, m + 1)
                TS(nmax[:, b, :], smax[:, b, :], -scale, None, ALU.mult).then_inc(at_nmax, 1)

            def prob_scale(m):
                b = m % 2
                dve.wait_ge(at_exp, m + 1)
                nc.vector.reciprocal(rsum[:, b, :], ssum[:, b, :]).then_inc(at_rs, 1)
                dve.wait_ge(at_rs, m + 1)
                for t, (lo, hi_) in enumerate(MEM_SPANS if is_mem(m) else DSA_SPANS):
                    ins = TS(prob[:, b, lo:hi_], prob[:, b, lo:hi_], rsum[:, b, t:t + 1], None, ALU.mult)
                ins.then_inc(at_p, 1)

            def values_lo(m):
                dve.wait_ge(at_hi, m + 1)
                c = cat_tile(m)
                TT(cat[:, c, 1, :], VALUES[:, 0:S], cat[:, c, 0, :].bitcast(fp32), ALU.subtract).then_inc(at_lo, 1)

            def heads(step, lo, hi_):
                if lo <= step < hi_:
                    scores_max(step)
                if lo <= step - 2 < hi_:
                    values_lo(step - 2)
                if lo <= step < hi_:
                    prob_scale(step)

            def residual(k, last_unit, t):
                if t == 0:
                    dve.wait_ge(tile_done, k + 1)
                else:
                    dve.wait_ge(unit_done, last_unit + 1)
                for n in range(2):
                    xs = x[:, t, 512 * n:512 * n + 512]
                    TT(xs, xs, A[2 * t + n][:, :], ALU.add).then_inc(res_done, 1)

            def residual_norm(k, last_unit):
                residual(k - 2, last_unit, 0)
                residual(k - 2, last_unit, 1)
                for t in range(NT):
                    norm_scale(k, t, xn, x)

            for t in range(NT):
                norm_scale(0, t, xn, x)
            split_lo(0)
            dve.wait_ge(prm_ready, 1)
            norm_lo(0, hT, C_MIX, A)
            split_lo(1)
            split_lo(2)
            for t in range(NT):
                norm_scale(1, t, mem_tok, mem_tok)

            def conv_sums(j):
                for tap in range(1, LRU_TAPS):
                    for c in (2 * j, 2 * j + 1):
                        w = C_LCW + 8 * (LRU_TAPS - 1 - tap) + c
                        if tap == 1:
                            dve.wait_ge(cv_tap, c + 1)
                        else:
                            dve.wait_ge(cv_acc, 4 * j + 2 * (tap - 2) + c % 2 + 1)
                        STT(xcT[:, c, tap:], xbT[:, c, 0:S - tap], prm[:, w:w + 1], xcT[:, c, tap:], ALU.mult,
                            ALU.add).then_inc(xc_ready if tap == LRU_TAPS - 1 else cv_acc, 1)

            def softplus():
                lam = prm[:, C_LAM:C_LAM + KD]
                absl, u, den, s1, s2, q = (lam_t[:, r, :] for r in range(6))
                STT(absl, lam, -1.0, lam, ALU.mult, ALU.max).then_inc(lam_exp, 1)
                dve.wait_ge(lam_exp, 2)
                link(TS(den, u, 2.0, None, ALU.add))
                link(nc.vector.reciprocal(den, den))
                link(TT(s1, u, den, ALU.mult))
                link(TT(s2, s1, s1, ALU.mult))
                link(TS(q, s2, 1.0 / 17, None, ALU.mult))
                for odd in range(15, 1, -2):
                    link(STT(q, q, 1.0 / odd, s2, ALU.add, ALU.mult))
                link(STT(q, q, 1.0, s1, ALU.add, ALU.mult))
                link(TS(den, lam, -1.0, 0.0, ALU.mult, ALU.max))
                link(STT(q, q, 2.0, den, ALU.mult, ALU.add))
                TS(sp8[:, 0, :], q, 8.0, None, ALU.mult)
                TS(sp8[:, 1, :], q, -8.0, None, ALU.mult).then_inc(lam_ready, 1)

            def angles():
                dve.wait_ge(pos_in_s, 16 * NT)
                dve.wait_ge(inv_ready, 1)
                link(nc.vector.tensor_copy(pos_f, pos_i))
                for t in range(NT):
                    link(TS(ang[:, t, :], inv_t[:, t, :], pos_f[:, t:t + 1], None, ALU.mult))
                magic = 1.5 * 2.0 ** 23
                link(TS(turns, ang, 1.0 / (2 * math.pi), magic, ALU.mult, ALU.add))
                link(TS(turns, turns, -magic, None, ALU.add))
                c1 = 6.28125
                c2 = round((2 * math.pi - c1) * 2 ** 18) / 2 ** 18
                c3 = 2 * math.pi - c1 - c2
                for c in (c1, c2, c3):
                    link(STT(ang, turns, -c, ang, ALU.mult, ALU.add))
                top = float(np.nextafter(np.float32(math.pi), np.float32(0)))
                link(TS(wrap, ang, math.pi / 2, None, ALU.add))
                link(TS(turns, wrap, math.pi, -2 * math.pi, ALU.is_gt, ALU.mult))
                link(TT(wrap, wrap, turns, ALU.add))
                link(TS(wrap, wrap, top, -top, ALU.min, ALU.max))
                TS(ang, ang, top, -top, ALU.min, ALU.max).then_inc(trig_args, 1)

            g0 = {g.name: g for g in GROUPS["l0"]}
            for j in range(4):
                g = g0[f"x{j}"]
                chan_sums(g, [xbT[:, 2 * j + e, :] for e in range(2)])
                split_lo(g.unit + 3)
                dve.wait_ge(prm_ready, 2)
                conv_sums(j)
                if j == 0:
                    angles()
                if j == 1:
                    norm_lo(1, memT, C_MEM, U)
            softplus()
            for j in range(2):
                g = g0[f"mq{j}"]
                chan_sums(g, [mqT[:, 2 * j + e, :] for e in range(2)])
                split_lo(g.unit + 3)
            for j in range(2):
                g = g0[f"mk{j}"]
                chan_sums(g, [mkT[:, 2 * j + e, :] for e in range(2)])
                split_lo(g.unit + 3)

            def gain2(h):
                cs = slice(4 * h, 4 * h + 4)
                dve.wait_ge(l_tanh, 4 * h + 4)
                dve.wait_ge(l_a2, h + 1)
                STT(tT[:, cs, :], xcT[:, cs, :], 1.0, tT[:, cs, :], ALU.add, ALU.mult).then_inc(l_gain2, 1)

            def recurrence(h):
                cs = slice(4 * h, 4 * h + 4)
                dve.wait_ge(l_sqrt, h + 1)
                dve.wait_ge(l_ix, h + 1)
                TT(iT[:, cs, :], iT[:, cs, :], rT[:, cs, :], ALU.mult).then_inc(l_bt, 1)
                dve.wait_ge(l_bt, h + 1)
                for c in range(4 * h, 4 * h + 4):
                    nc.vector.tensor_tensor_scan(tT[:, c, :], xbT[:, c, :], iT[:, c, :], 0.0, ALU.mult,
                                                 ALU.add).then_inc(l_h, 1)

            gain2(0)
            split_lo(g0["mv"].unit + 3)
            gain2(1)
            recurrence(0)
            split_lo(g0["mv"].unit + 4)
            for j in range(4):
                g = g0[f"gate{j}"]
                chan_sums(g, [gbT[:, 2 * j + e, :] for e in range(2)])
                split_lo(g.unit + 3)
                heads(j, 0, MEM_H)
                if j == 0:
                    recurrence(1)
            heads(4, 0, MEM_H)
            heads(5, 0, MEM_H)
            split_lo(U_OUT[0] + 3)
            for h in range(2):
                cs = slice(4 * h, 4 * h + 4)
                dve.wait_ge(l_gelu, h + 1)
                dve.wait_ge(l_h, 4 * h + 4)
                TT(xbT[:, cs, :], tT[:, cs, :], gbT[:, cs, :], ALU.mult).then_inc(l_y, 1)
            for h in range(2):
                cs = slice(4 * h, 4 * h + 4)
                dve.wait_ge(l_yhi, h + 1)
                TT(cat[:, cs, 1, :], xbT[:, cs, :], cat[:, cs, 0, :].bitcast(fp32), ALU.subtract).then_inc(l_ylo, 1)
            for j in range(1, 5):
                split_lo(U_OUT[0] + j + 3)
            residual_norm(2, U_OUT[0] + 5)
            split_lo(U_OUT[0] + 5 + 3)
            for i, g in enumerate(GROUPS["fill1"]):
                chan_sums(g, [mkT[:, 2 * i + e, :] for e in range(2)], U[2 * i:2 * i + 2], fill_low)
                if i == 0:
                    norm_lo(2, hT, C_FFN, A)
                split_lo(g.unit + 3)

            def ffn(l):
                first = U_FFN[l]
                cw = C_F[l]

                def half(i, h, ahead):
                    for c in range(2):
                        dve.wait_ge(f_low[l], i * 4 + (2 * h + c + 1))
                        TT(ffn_u[:, 2 * h + c, :], U[2 * h + c][:, 0:S], ffn_low[:, 2 * h + c, :],
                           ALU.add).then_inc(f_sum[l], 1)
                    if ahead is not None:
                        split_lo(first + ahead + i * 3, (first + ahead) % RING)
                    for c in range(2):
                        ch = i * 2 + (h * (FC // 2) + c)
                        k = 2 * h + c
                        dve.wait_ge(f_tap[l], i * 4 + (k + 1))
                        STT(ffn_y[:, k, 1:], ffn_u[:, k, 0:S - 1], prm[:, ds(cw + FC + ch, 1)], ffn_y[:, k, 1:], ALU.mult,
                            ALU.add).then_inc(f_acc[l], 1)
                    for c in range(2):
                        ch = i * 2 + (h * (FC // 2) + c)
                        k = 2 * h + c
                        dve.wait_ge(f_acc[l], i * 4 + (k + 1))
                        STT(ffn_y[:, k, 2:], ffn_u[:, k, 0:S - 2], prm[:, ds(cw + ch, 1)], ffn_y[:, k, 2:], ALU.mult,
                            ALU.add).then_inc(f_conv[l], 1)

                def tail(i, ahead):
                    dve.wait_ge(f_silu[l], i + 1)
                    dve.wait_ge(f_conv[l], i * 4 + 4)
                    TT(ffn_p[:, :, :], ffn_g[:, :, :], ffn_y[:, 2:4, :], ALU.mult).then_inc(f_prod[l], 1)
                    if ahead is not None:
                        split_lo(first + ahead + i * 3, (first + ahead) % RING)
                    dve.wait_ge(f_hi[l], i + 1)
                    TT(cat[:, 0:2, 1, :], ffn_p[:, :, :], cat[:, 0:2, 0, :].bitcast(fp32), ALU.subtract).then_inc(f_lo[l], 1)

                half(0, 0, 3)
                half(0, 1, 4)
                tail(0, None)
                with dve.Fori(1, NPAIR - 1) as i:
                    half(i, 0, 2)
                    half(i, 1, 3)
                    tail(i, 4)
                i = NPAIR - 1
                half(i, 0, 2)
                half(i, 1, None)
                tail(i, None)
                split_lo(first + 3 + 3 * i)
                split_lo(first + 4 + 3 * i)

            ffn(0)
            residual_norm(3, U_FFN[0] + 3 * NPAIR - 1)
            split_lo(START["fill2"] + 2)
            split_lo(START["fill2"] + 3)
            norm_lo(3, hT, C_MIX + KD, A)
            split_lo(START["fill2"] + 4)

            ropes = [0]

            def rope(v, half, f0, done, count):
                heads_ = v.shape[2]
                a, b = v[:, :, :, 0:half], v[:, :, :, half:2 * half]
                sin, cos = (trig[:, r, :, f0:f0 + half].unsqueeze(2).broadcast_to((P, NT, heads_, half)) for r in range(2))
                n = NT * heads_ * half
                t0, t1, t2, t3 = (rope_t[:, r, 0:n].rearrange("p (t h d) -> p t h d", t=NT, h=heads_) for r in range(4))
                TT(t0, a, cos, ALU.mult)
                TT(t1, b, sin, ALU.mult)
                TT(t2, b, cos, ALU.mult)
                link(TT(t3, a, sin, ALU.mult))
                TT(a, t0, t1, ALU.subtract)
                TT(b, t2, t3, ALU.add).then_inc(done, 1)
                dve.wait_ge(done, count)

            def rope_chunk(name, count):
                h = 4 * int(name[1]) + (AH if name[0] == "k" else 0)
                dve.wait_ge(copied, g1[name].after)
                rope(qk_tok[:, :, h:h + 4, :], AROT // 2, 0, rope_q, count)

            def idx_sums(steps):
                for step in steps:
                    hp, t = step // NT, step % NT
                    width = (t + 1) * P
                    dst = score[:, 0:P] if t == 0 else score[:, P:3 * P]
                    dve.wait_ge(ix_relu, step + 1)
                    for e in range(2):
                        h = 2 * hp + e
                        src = prob[:, step % 2, e * width:(e + 1) * width]
                        w = ikw_tok[:, t, ID + h:ID + h + 1]
                        if h == 0:
                            TS(dst, src, w, None, ALU.mult).then_inc(ix_acc, 1)
                        else:
                            dve.wait_ge(ix_acc, 2 * step + e if e else 2 * step - 2)
                            STT(dst, src, w, dst, ALU.mult, ALU.add).then_inc(ix_acc, 1)

            def top_rounds(rounds):
                for r in rounds:
                    for t, (lo, hi_) in enumerate(DSA_SPANS):
                        if r:
                            dve.wait_ge(top_s, 4 * r - 1 + t)
                        nc.vector.max(top8[:, t, :], score[:, lo:hi_]).then_inc(top_s, 1)
                    for t, (lo, hi_) in enumerate(DSA_SPANS):
                        dve.wait_ge(top_s, 4 * r + 1 + t)
                        nc.vector.match_replace(score[:, lo:hi_], top8[:, t, :], score[:, lo:hi_], PICKED).then_inc(top_s, 1)

            g1 = {g.name: g for g in GROUPS["l1"]}

            def splits(name, mid):
                g = g1[name]
                split_lo(g.unit + 3)
                if g.units == 2:
                    mid()
                    split_lo(g.unit + 4)

            def nothing():
                pass

            splits("iq", nothing)
            splits("ikw", nothing)
            dve.wait_ge(trig_ready, 1)
            dve.wait_ge(copied, g1["ikw"].after)
            rope(iq_tok[:, :, :, :], IROT // 2, AROT // 2, rope_i, 1)
            rope(ikw_tok[:, :, 0:ID].unsqueeze(2), IROT // 2, AROT // 2, rope_i, 2)
            dve.wait_ge(ik_zero, 1)
            for e in range(2):
                nc.vector.tensor_copy(ikpad[:, :, e, ID * e:ID * e + ID], ikw_tok[:, :, 0:ID])
            TS(ikw_tok[:, :, ID:], ikw_tok[:, :, ID:], IH ** -0.5, None, ALU.mult).then_inc(ik_copied, 1)
            dve.wait_ge(ik_copied, 1)
            for j in range(2):
                chan_sums(g1[f"mq{j}"], [mqT[:, 2 * j + e, :] for e in range(2)])
                split_lo(g1[f"mq{j}"].unit + 3)
            splits("v0", lambda: idx_sums((0, 1)))
            idx_sums((2, 3))
            splits("q0", lambda: idx_sums((4, 5)))
            idx_sums((6, 7))
            dve.wait_ge(causal_s, 1)
            top_rounds((0,))
            splits("k0", lambda: (heads(4, 4, 16), top_rounds((1,))))
            heads(5, 4, 16)
            top_rounds((2,))
            rope_chunk("q0", 1)
            splits("q1", lambda: (heads(6, 4, 16), top_rounds((3, 4)), rope_chunk("k0", 2)))
            heads(7, 4, 16)
            top_rounds((5, 6))
            splits("k1", lambda: top_rounds((7,)))
            dve.wait_ge(top_s, 4 * (TOPK // 8))
            TS(kbias, score, PICKED, FILL, ALU.not_equal, ALU.mult).then_inc(bias_s, 1)
            rope_chunk("q1", 3)
            dve.wait_ge(bias_ready, 1)
            heads(8, 4, 16)
            splits("v1", lambda: (heads(9, 4, 16), rope_chunk("k1", 4)))
            for step in range(10, 18):
                heads(step, 4, 16)
            for j in range(5):
                split_lo(U_OUT[1] + j + 3)
            residual_norm(4, U_OUT[1] + 5)
            split_lo(U_OUT[1] + 5 + 3)
            norm_lo(4, hT, C_FFN + KD, A)
            ffn(1)
            residual(3, U_END - 1, 0)
            residual(3, U_END - 1, 1)
            dve.wait_ge(fg_in_s, 16)
            for t in range(NT):
                norm_scale(5, t, None, None)
                STT(xn[:, t, :], x[:, t, :], rstd[:, t:t + 1], fin_g, ALU.mult, ALU.mult).then_inc(out_ready, 1)

        @block.tensor
        def _(pe):
            mm = nc.tensor.matmul

            def transpose(dst, src):
                return nc.tensor.transpose(dst, src, ident[0:src.shape[0], 0:src.shape[0]])

            def weights(n):
                pe.wait_ge(lo_ready, n + 1)

            def norm_transpose(k, src, banks):
                for t in range(NT):
                    pe.wait_ge(xn_ready, 2 * k + t + 1)
                for b in range(4):
                    for e in range(2):
                        c = 2 * b + e
                        for t in range(NT):
                            ins = transpose(banks[b][:, e * S + t * P:e * S + (t + 1) * P], src[:, t, c * P:(c + 1) * P])
                    ins.then_inc(n_tr, 1)

            def channel_ready(norm, k):
                if norm is not None:
                    pe.wait_ge(n_lo, 4 * norm + k // 2 + 1)

            def chan_major(slot, e, rhs, bank, norm=None):
                for k in range(8):
                    channel_ready(norm, k)
                    at = k * 256 + e * P
                    hi_args = (bank[:, :], w_hi[:, slot, at:at + P], rhs[:, k, :, :].rearrange("p a s -> p (a s)"))
                    lo_args = (bank[:, 0:S], w_lo[:, slot, at:at + P], rhs[:, k, 0, :])
                    if k < 7:
                        mm(*hi_args, start=(k == 0), stop=False)
                        mm(*lo_args, start=False, stop=False)
                    else:
                        mm(*lo_args, start=False, stop=False)
                        last = mm(*hi_args, start=False, stop=True)
                return last

            def tok_major(slot, width, ktiles, lhs, k0, first, last, banks, done=None, norm=None):
                cols = [(n, a, min(width, a + 512)) for n, a in enumerate(range(0, width, 512))]
                for t in range(NT):
                    for k in range(ktiles):
                        if t == 0:
                            channel_ready(norm, k0 + k)
                        hi_l = lhs[:, k0 + k, 0, t * P:(t + 1) * P]
                        lo_l = lhs[:, k0 + k, 1, t * P:(t + 1) * P]
                        for part_no, (l_, src) in enumerate(((hi_l, w_hi), (hi_l, w_lo), (lo_l, w_hi))):
                            for n, a, b in cols:
                                ins = mm(banks[t][n][:, 0:b - a], l_, src[:, slot, k * width + a:k * width + b],
                                         start=(first and k == 0 and part_no == 0),
                                         stop=(last and k == ktiles - 1 and part_no == 2))
                    if done is not None and t == 0:
                        ins.then_inc(done, 1)
                return ins

            def dense_unit(g, j, lhs, banks=None, norm=None):
                n = g.unit + j
                b0, b1 = banks or A[2 * g.pair:2 * g.pair + 2]
                weights(n)
                if g.kind == "chan":
                    chan_major(n % RING, 0, lhs, b0, norm)
                    ins = chan_major(n % RING, 1, lhs, b1)
                else:
                    ins = tok_major(n % RING, unit_size(n) // 4, 4, lhs, 4 * j, j == 0, j == 1, [[b0], [b1]], None, norm)
                ins.then_inc(unit_done, 1)

            def wait_evacuated(g):
                pe.wait_ge(summed if g.kind == "chan" else copied, g.after)

            def dense(key, name, lhs, mid=None, end=None, norm=None):
                groups = GROUPS[key]
                at = [g.name for g in groups].index(name)
                if at >= 2:
                    wait_evacuated(groups[at - 2])
                for j in range(groups[at].units):
                    dense_unit(groups[at], j, lhs, None, norm)
                    for do in (mid, end)[j + 2 - groups[at].units:][:1]:
                        if do is not None:
                            do()

            def out_units(l, lhs):
                for g in GROUPS["l0" if l == 0 else "l1"][-2:]:
                    wait_evacuated(g)
                for j, k0 in enumerate(out_order):
                    n = U_OUT[l] + j
                    if l == 0 and k0 in (0, 4):
                        pe.wait_ge(l_ylo, k0 // 4 + 1)
                    if k0 == 0:
                        if l == 1:
                            pe.wait_ge(at_lo, 16)
                    weights(n)
                    last = j == 5
                    tok_major(n % RING, D, 2, lhs, k0, j == 0, last, [A[0:2], A[2:4]],
                              tile_done if last else None).then_inc(unit_done, 1)

            def scores(m):
                b = m % 2
                if m >= 2:
                    if is_mem(m - 2):
                        pe.wait_ge(at_exp, m - 1)
                    else:
                        pe.wait_ge(at_sc, m - 1 - 2 * MEM_H)
                if is_mem(m):
                    h = m % MEM_H
                    for t in range(NT):
                        ins = mm(SCORES[b][:, t * S:(t + 1) * S], mqT[:, h, t * P:(t + 1) * P], mkT[:, h, :],
                                 start=True, stop=True)
                else:
                    h = m - 2 * MEM_H
                    mm(SCORES[b][:, 0:P], qkT[:, h, 0:P], qkT[:, AH + h, 0:P], start=True, stop=True)
                    ins = mm(SCORES[b][:, P:3 * P], qkT[:, h, P:2 * P], qkT[:, AH + h, :], start=True, stop=True)
                ins.then_inc(at_s, 1)

            def turn(m):
                b = m % 2
                pe.wait_ge(at_p, m + 1)
                if m:
                    pe.wait_ge(at_pt, m)
                if is_mem(m):
                    for k in range(NT):
                        for t in range(NT):
                            ins = transpose(TURNED[:, k * S + t * P:k * S + (t + 1) * P],
                                            prob[:, b, t * S + k * P:t * S + (k + 1) * P])
                else:
                    for k in range(3):
                        ins = transpose(TURNED[:, k * P:(k + 1) * P], prob[:, b, k * P:(k + 1) * P])
                ins.then_inc(at_t, 1)

            def values(m):
                pe.wait_ge(at_pt, m + 1)
                if m:
                    pe.wait_ge(at_lo, m)
                if is_mem(m):
                    h = m % MEM_H
                    for k in range(NT):
                        ins = mm(VALUES[:, 0:S], mv[:, k, h * P:(h + 1) * P], probT[:, k * S:(k + 1) * S],
                                 start=(k == 0), stop=(k == 1))
                else:
                    h = m - 2 * MEM_H
                    mm(VALUES[:, 0:S], v_tok[:, 0, h * P:(h + 1) * P], probT[:, 0:S], start=True, stop=False)
                    ins = mm(VALUES[:, P:S], v_tok[:, 1, h * P:(h + 1) * P], probT[:, S:S + P], start=False, stop=True)
                ins.then_inc(at_o, 1)

            def heads(step, lo, hi_):
                if lo <= step < hi_:
                    scores(step)
                if lo <= step - 2 < hi_:
                    values(step - 2)
                if lo <= step - 1 < hi_:
                    turn(step - 1)

            pe.wait_ge(consts, 1)
            norm_transpose(0, xn, A)
            pe.wait_ge(gain_in_s, 16)
            transpose(U[0][:, 0:16], rows[0:16, 0, :]).then_inc(prm_t, 1)

            dense("l0", "x0", hT, norm=0)
            pe.wait_ge(rows_in_s, 16 * 7)
            pe.wait_ge(taps_in_s, 16 * 6)
            nw2 = (FFN_TAPS + 1) * FC - P
            transpose(U[1][:, 0:C_MISC], rows[0:C_MISC, 0, :])
            for l in range(2):
                transpose(U[1][:, C_F[l]:C_F[l] + P], rows[:, 1 + 2 * l, :])
                last = transpose(U[1][:, C_F[l] + P:C_F[l] + P + nw2], rows[0:nw2, 2 + 2 * l, :])
            last.then_inc(prm_t, 1)
            dense("l0", "x1", hT)
            pe.wait_ge(prm_ready, 2)
            norm_transpose(1, mem_tok, U)
            for name in ("x2", "x3", "mq0", "mq1"):
                dense("l0", name, hT)
            pe.wait_ge(bd_in_s, 64)
            pe.wait_ge(n_lo, 8)
            for c in range(KD):
                pe.wait_ge(xc_ready, c + 1)
                if c >= 4:
                    pe.wait_ge(gate_sig, c - 3)
                mm(U[c % 4][:, 0:S], w_bd[:, 0, c, :], xcT[:, c, :], start=True, stop=True)
                mm(U[c % 4][:, S:2 * S], w_bd[:, 1, c, :], xcT[:, c, :], start=True, stop=True).then_inc(gate_mm, 1)
            for name in ("mk0", "mk1", "mv"):
                dense("l0", name, memT)
            for j in range(4):
                def step(j=j):
                    if j == 0:
                        pe.wait_ge(gate_sig, KD)
                        pe.wait_ge(copied, group("l0", "mv").after)
                        pe.wait_ge(summed, group("l0", "mk1").after)
                    heads(j, 0, MEM_H)
                dense("l0", f"gate{j}", hT, end=step)
            heads(4, 0, MEM_H)
            heads(5, 0, MEM_H)
            pe.wait_ge(at_lo, MEM_H)
            out_units(0, cat)
            for i, g in enumerate(GROUPS["fill1"]):
                dense_unit(g, 0, memT, U[2 * i:2 * i + 2])
                if i == 0:
                    norm_transpose(2, xn, A)

            def ffn(l, norm, fillers=()):
                first = U_FFN[l]

                def up(i, h, n, slot, norm_=None):
                    weights(n)
                    if fillers and isinstance(i, int) and i == 0:
                        pe.wait_ge(summed, fillers[h].after)
                    if not (isinstance(i, int) and i == 0):
                        pe.wait_ge(f_sum[l], i * 4 - 4 + (2 * h + 2))
                    chan_major(slot, 0, hT, U[2 * h], norm_)
                    chan_major(slot, 1, hT, U[2 * h + 1]).then_inc(unit_done, 1)

                def down(i, n, slot, first_, last_):
                    weights(n)
                    pe.wait_ge(f_lo[l], i + 1)
                    tok_major(slot, D, 2, cat, 0, first_, last_, [A[0:2], A[2:4]],
                              tile_done if last_ else None).then_inc(unit_done, 1)

                up(0, 0, first, first % RING, norm)
                up(0, 1, first + 1, (first + 1) % RING)
                up(1, 0, first + 2, (first + 2) % RING)
                up(1, 1, first + 3, first % RING)
                down(0, first + 4, (first + 1) % RING, True, False)
                with pe.Fori(2, NPAIR) as i:
                    up(i, 0, first - 1 + i * 3, (first - 1) % RING)
                    up(i, 1, first + i * 3, first % RING)
                    down(i - 1, first + 1 + i * 3, (first + 1) % RING, False, False)
                down(NPAIR - 1, first + 3 * NPAIR - 1, (first + 3 * NPAIR - 1) % RING, False, True)

            ffn(0, 2, GROUPS["fill1"])
            pe.wait_ge(f_sum[0], 4 * NPAIR)
            g = GROUPS["fill2"][0]
            dense_unit(g, 0, memT, U[0:2])
            dense_unit(g, 1, memT, U[0:2])
            norm_transpose(3, xn, A)

            dense("l1", "iq", hT, norm=3)
            dense("l1", "ikw", hT)
            dense("l1", "mq0", hT)
            dense("l1", "mq1", hT)
            pe.wait_ge(rope_i, 2)
            pe.wait_ge(ik_copied, 1)
            pe.wait_ge(copied, g.after)
            iq_f = iq_tok[:, :, :, :].rearrange("p t h d -> p t (h d)")
            for b in range(3):
                for e in range(2):
                    for t in range(NT):
                        src = ikpad[:, t, e, :] if b == 2 else iq_f[:, t, (2 * b + e) * P:(2 * b + e + 1) * P]
                        ins = transpose(U[b][:, e * S + t * P:e * S + (t + 1) * P], src)
                ins.then_inc(ix_tr, 1)

            def idx_scores(steps):
                pe.wait_ge(ix_trc, 3)
                for step in steps:
                    hp, t = step // NT, step % NT
                    width = (t + 1) * P
                    if step >= 4:
                        pe.wait_ge(ix_relu, step - 3)
                    for e in range(2):
                        ins = mm(U[step % 4][:, e * width:(e + 1) * width], iqT[:, hp, t * P:(t + 1) * P],
                                 ikT[:, e, 0:width], start=True, stop=True)
                    ins.then_inc(ix_mm, 1)

            qk_f = qk_tok[:, :, :, :].rearrange("p t h d -> p t (h d)")

            def qk_turn(c, exps):
                pe.wait_ge(rope_q, 2 * c + 2)
                pe.wait_ge(at_exp, exps)
                for b in range(4):
                    if b >= 2:
                        pe.wait_ge(q_trc, 4 * c + b - 1)
                    h = 4 * c + 2 * (b % 2) + AH * (b // 2)
                    for e in range(2):
                        for t in range(NT):
                            ins = transpose(U[b % 2][:, e * S + t * P:e * S + (t + 1) * P],
                                            qk_f[:, t, (h + e) * P:(h + e + 1) * P])
                    ins.then_inc(q_tr, 1)

            def dsa_heads(step):
                def do():
                    if step == 4:
                        pe.wait_ge(ix_relu, IH)
                        pe.wait_ge(summed, group("l1", "mq1").after)
                    if step == 8:
                        pe.wait_ge(q_trc, 4)
                    heads(step, 4, 16)
                return do

            def last_turn():
                qk_turn(1, 10)
                pe.wait_ge(q_trc, 8)
                dsa_heads(10)()

            dense("l1", "v0", hT, lambda: idx_scores((0, 1)), lambda: idx_scores((2, 3)))
            dense("l1", "q0", hT, lambda: idx_scores((4, 5)), lambda: idx_scores((6, 7)))
            dense("l1", "k0", hT, dsa_heads(4), dsa_heads(5))
            dense("l1", "q1", hT, dsa_heads(6), dsa_heads(7))
            dense("l1", "k1", hT, lambda: qk_turn(0, 8), dsa_heads(8))
            dense("l1", "v1", hT, dsa_heads(9), last_turn)
            pe.wait_ge(copied, group("l1", "v1").after)
            for step in range(11, 18):
                heads(step, 4, 16)
            out_units(1, cat)
            norm_transpose(4, xn, A)
            ffn(1, 4)


_INS = ["x", "mem", "positions", "norm_mix", "norm_ffn", "mem_norm", "final_norm", "w_mem_kv", "w_ffn_up", "ffn_conv_w",
        "ffn_conv_b", "w_ffn_down", "lru_w_in", "lru_conv_w", "lru_conv_b", "lru_w_a", "lru_b_a", "lru_w_x", "lru_b_x",
        "lru_lambda", "lru_w_out", "dsa_w_in", "dsa_w_out"]


def kernel(**inputs):
    import numpy as _np
    import concourse.bacc as _bacc
    from concourse import mybir as _mybir
    from concourse.bass_utils import run_bass_kernel_spmd as _run

    nc = _bacc.Bacc("TRN2", target_bir_lowering=False, num_devices=1)
    arrays, args = {}, []
    for name in _INS:
        a = _np.ascontiguousarray(inputs[name])
        arrays[f"in_{name}_dram"] = a
        args.append(nc.dram_tensor(f"in_{name}_dram", a.shape, _mybir.dt.from_np(a.dtype), kind="ExternalInput").ap())
    args.append(nc.dram_tensor("out_0_dram", (1, S, D), _mybir.dt.from_np(_np.dtype("float32")), kind="ExternalOutput").ap())
    trunk(nc, *args)
    r = _run(nc, [arrays], core_ids=[0])
    return r.results[0]["out_0_dram"]
```

```python
import math
from contextlib import ExitStack

import numpy as np
import concourse.bass as bass
from concourse import mybir


P = 128
S = 256
D = 1024
NT = S // P
KD = D // P
MEM_H, MEM_HD = 4, 128
MEM_W = MEM_H * MEM_HD
LRU_TAPS = 4
FF = 2816
FFN_TAPS = 3
AH, AD = 8, 128
AROT = AD // 4
IH, ID = 8, 64
IROT = ID // 4
TOPK = min(256, S // 4)
NPAIR = FF // (2 * P)
FC = 2 * FF // P
CAT = (D + MEM_W) // P
EPS = 1e-6
THETA = 500000.0
FILL = -3.0e38
PICKED = -3.4e38


L0_GROUPS = [("chan", "x0"), ("chan", "x1"), ("chan", "mq0"), ("chan", "x2"), ("chan", "x3"), ("chan", "mq1"),
             ("chan", "mk0"), ("chan", "mk1"), ("tok", "mv"),
             ("chan", "gate0"), ("chan", "gate1"), ("chan", "gate2"), ("chan", "gate3")]
FILL1_GROUPS = [("chan", "mk0"), ("chan", "mk1")]
FILL2_GROUPS = [("tok", "mv")]
L1_GROUPS = [("tok", "iq"), ("tok", "ikw"), ("chan", "mq0"), ("chan", "mq1"),
             ("tok", "v0"), ("tok", "q0"), ("tok", "k0"), ("tok", "q1"), ("tok", "k1"), ("tok", "v1")]


class Group:

    def __init__(self, kind, name, layer, unit, turn, chans, toks):
        self.kind, self.name, self.layer, self.unit, self.pair = kind, name, layer, unit, turn % 2
        self.units = 1 if kind == "chan" else 2
        self.before = chans if kind == "chan" else toks
        self.after = self.before + 2


def place_groups():
    unit, chans, toks, placed, starts = 0, 0, 0, {}, {}
    for key, layer, groups in (("l0", 0, L0_GROUPS), ("out0", 0, 6), ("fill1", 1, FILL1_GROUPS), ("ffn0", 0, 3 * NPAIR),
                               ("fill2", 1, FILL2_GROUPS), ("l1", 1, L1_GROUPS), ("out1", 1, 6), ("ffn1", 1, 3 * NPAIR)):
        starts[key] = unit
        if isinstance(groups, int):
            unit += groups
            continue
        placed[key] = []
        for turn, (kind, name) in enumerate(groups):
            g = Group(kind, name, layer, unit, turn, chans, toks)
            placed[key].append(g)
            unit += g.units
            if kind == "chan":
                chans += 2
            else:
                toks += 2
    return placed, starts, unit


GROUPS, START, U_END = place_groups()
U_OUT = (START["out0"], START["out1"])
U_FFN = (START["ffn0"], START["ffn1"])
RING = 3

C_MIX, C_FFN, C_MEM, C_LCW, C_LCB, C_BA, C_BX, C_LAM = 0, 16, 32, 40, 72, 80, 88, 96
C_MISC = 104
C_F = (C_FFN_W0, C_FFN_W1) = (C_MISC, C_MISC + (FFN_TAPS + 1) * FC)
NPRM = C_MISC + 2 * (FFN_TAPS + 1) * FC


def trunk(nc, x_in, mem_in, pos_in, norm_mix, norm_ffn, mem_norm, final_norm, w_mem_kv, w_ffn_up, ffn_conv_w,
          ffn_conv_b, w_ffn_down, lru_w_in, lru_conv_w, lru_conv_b, lru_w_a, lru_b_a, lru_w_x, lru_b_x,
          lru_lambda, lru_w_out, dsa_w_in, dsa_w_out, out):
    fp32, f32r, i32 = mybir.dt.float32, mybir.dt.float32r, mybir.dt.int32
    ALU, ACT, AX = mybir.AluOpType, mybir.ActivationFunctionType, mybir.AxisListType
    ds = bass.ds

    with ExitStack() as ctx:
        def sb(name, shape, dt=fp32):
            return ctx.enter_context(nc.sbuf_tensor(name, shape, dt))

        def sem(name):
            return ctx.enter_context(nc.semaphore(name))

        w_raw = sb("w_raw", [P, RING, 2048])
        w_hi = sb("w_hi", [P, RING, 2048], f32r)
        w_lo = sb("w_lo", [P, RING, 2048], f32r)
        x = sb("x_res", [P, NT, D])
        hT = sb("hT", [P, KD, 2, S], f32r)
        memT = sb("memT", [P, KD, 2, S], f32r)
        cat = sb("cat", [P, CAT, 2, S], f32r)
        mkT = sb("mkT", [P, MEM_H, S])
        mv = sb("mv", [P, NT, MEM_W])
        mqT = sb("mqT", [P, MEM_H, S])
        ident = sb("ident", [P, P])
        prm = sb("prm", [P, NPRM])
        trig = sb("trig", [P, 2, NT, 24])
        eps_t = sb("eps_t", [P, 1])
        warm = sb("warm", [P, 16])
        ssq = sb("ssq", [P, NT])
        ssq_b = sb("ssq_b", [P, NT])
        msq = sb("msq", [P, NT])
        std = sb("std", [P, NT])
        rstd = sb("rstd", [P, NT])
        sp8 = sb("sp8", [P, 2, KD])
        smax = sb("smax", [P, 2, NT])
        nmax = sb("nmax", [P, 2, NT])
        ssum = sb("ssum", [P, 2, NT])
        rsum = sb("rsum", [P, 2, NT])
        scratch = sb("scratch", [P, 2048])
        arena = sb("arena", [P, 12 * 1024])

        xn = scratch[:, :].rearrange("p (t d) -> p t d", t=NT)
        prob = scratch[:, 0:1024].rearrange("p (b n) -> p b n", b=2)
        probT = scratch[:, 1024:1536]
        chan_low = scratch[:, 1536:2048].rearrange("p (e s) -> p e s", e=2)

        def part(kib, n, pattern=None, **dims):
            v = arena[:, kib * 256:kib * 256 + n]
            return v.rearrange(pattern, **dims) if pattern else v

        B = [part(8 * n, 2048, "p (c s) -> p c s", c=KD) for n in range(6)]
        xbT, xcT, rT, iT, gbT, tT = B
        w_bd = part(40, 2048, "p (w c n) -> p w c n", w=2, c=KD)
        rows = part(16, 640, "p (r c) -> p r c", r=5)
        junk = part(20, 1024)
        mem_tok = part(32, 2048, "p (t d) -> p t d", t=NT)
        inv_t = part(24, NT * 24, "p (t f) -> p t f", t=NT)
        ang = part(25, NT * 24, "p (t f) -> p t f", t=NT)
        turns = part(26, NT * 24, "p (t f) -> p t f", t=NT)
        wrap = part(27, NT * 24, "p (t f) -> p t f", t=NT)
        pos_i = part(28, NT).bitcast(i32)
        pos_f = part(29, NT)
        lam_t = scratch[:, 0:6 * KD].rearrange("p (r c) -> p r c", r=6)
        ffn_low = part(0, 1024, "p (c s) -> p c s", c=4)
        ffn_u = part(4, 1024, "p (c s) -> p c s", c=4)
        ffn_y = part(8, 1024, "p (c s) -> p c s", c=4)
        ffn_g = part(12, 512, "p (c s) -> p c s", c=2)
        ffn_p = part(14, 512, "p (c s) -> p c s", c=2)
        fill_low = part(20, 512, "p (e s) -> p e s", e=2)
        qk_tok = part(0, 4096, "p (t h d) -> p t h d", t=NT, h=2 * AH)
        v_tok = part(16, 2048, "p (t d) -> p t d", t=NT)
        qkT = part(24, 4096, "p (h s) -> p h s", h=2 * AH)
        ikT = part(28, 512, "p (e s) -> p e s", e=2)
        ikpad = part(30, 512, "p (t e d) -> p t e d", t=NT, e=2)
        iqT = part(32, 1024, "p (c s) -> p c s", c=4)
        iq_tok = part(36, 1024, "p (t h d) -> p t h d", t=NT, h=IH)
        score = part(40, 384)
        kbias = arena[:, 40 * 256 + 384:40 * 256 + 768]
        ikw_tok = part(43, 144, "p (t d) -> p t d", t=NT)
        top8 = arena[:, 43 * 256 + 144:43 * 256 + 160].rearrange("p (t d) -> p t d", t=NT)
        rope_t = part(44, 4 * 128 * NT // 2 * 2, "p (r n) -> p r n", r=4)
        fin_g = part(20, D)

        U = [ctx.enter_context(nc.psum_tensor(f"ps_u{n}", [P, 512], fp32)) for n in range(4)]
        A = [ctx.enter_context(nc.psum_tensor(f"ps_a{n}", [P, 512], fp32)) for n in range(4)]
        SCORES, TURNED, VALUES = U[0:2], U[2], U[3]

        x_in_s = [sem(f"x_loaded{t}") for t in range(NT)]
        mem_in_s, gain_in_s, rows_in_s, taps_in_s, pos_in_s, bd_in_s, fg_in_s = (
            sem(n) for n in ("mem_loaded", "gain_loaded", "rows_loaded", "taps_loaded", "pos_loaded", "bd_loaded", "fg_loaded"))
        raw_in = [sem(f"raw_loaded{n}") for n in range(RING)]
        out_ready, out_s = sem("out_ready"), sem("out_stored")
        hi_ready, lo_ready, unit_done = sem("hi_ready"), sem("lo_ready"), sem("unit_done")
        eps_ready, zeroed, consts, inv_ready, bd_zero = sem("eps_ready"), sem("zeroed"), sem("consts"), sem("inv_ready"), sem("bd_zero")
        prm_t, prm_ready = sem("prm_transposed"), sem("prm_ready")
        chain, pool_chain = sem("dve_chain"), sem("pool_chain")
        lam_exp, lam_ready = sem("lam_exp"), sem("lam_ready")
        trig_args, trig_ready = sem("trig_args"), sem("trig_ready")
        sq_s, msq_s, std_s, rstd_s, xn_ready = (sem(n) for n in ("squares", "mean_square", "std", "rstd", "xn_ready"))
        n_tr, n_hi, n_lo = sem("norm_transposed"), sem("norm_hi"), sem("norm_lo")
        tile_done, res_done = sem("tile_done"), sem("res_done")
        lowed, summed, copied = sem("chan_lowed"), sem("chan_summed"), sem("tok_copied")
        cv_tap, cv_acc, xc_ready = sem("conv_tap"), sem("conv_acc"), sem("xc_ready")
        gate_mm, gate_sig = sem("gate_mm"), sem("gate_sig")
        l_exp, l_tanh, l_ix, l_a2, l_gain2, l_sqrt, l_bt, l_h, l_gelu, l_y, l_yhi, l_ylo = (
            sem("lru_" + n) for n in ("exp", "tanh", "ix", "a2", "gain2", "sqrt", "bt", "h", "gelu", "y", "yhi", "ylo"))
        at_s, at_sc, at_max, at_nmax, at_exp, at_rs, at_p, at_t, at_pt, at_o, at_hi, at_lo = (
            sem("att_" + n) for n in ("s", "sc", "max", "nmax", "exp", "rsum", "p", "t", "pt", "o", "hi", "lo"))
        ik_zero, rope_i, ik_copied = sem("ik_zero"), sem("rope_i"), sem("ik_copied")
        ix_tr, ix_trc, ix_mm, ix_relu, ix_acc = (sem("idx_" + n) for n in ("tr", "trc", "mm", "relu", "acc"))
        causal_s, top_s, bias_s, bias_ready = sem("causal"), sem("top"), sem("bias"), sem("bias_ready")
        rope_q, q_tr, q_trc = sem("rope_q"), sem("q_tr"), sem("q_trc")
        f_low, f_sum, f_tap, f_acc, f_conv, f_silu, f_prod, f_hi, f_lo = (
            [sem(f"ffn{l}_{n}") for l in range(2)]
            for n in ("lowed", "summed", "tap", "acc", "conv", "silu", "prod", "hi", "lo"))

        block = ctx.enter_context(nc.Block())

        def kxc(w, k0, k, c0, c):
            return k, c, w[k0 * P:(k0 + k) * P, c0:c0 + c].rearrange("(k p) c -> p k c", p=P)

        kv, lru_in, dsa_in = w_mem_kv, lru_w_in[0], dsa_w_in[0]
        c_idx = 3 * D
        c_ik = c_idx + IH * ID
        sources = {}
        for j in range(4):
            sources[0, f"x{j}"] = (lru_in, 256 * j, 256)
            sources[0, f"gate{j}"] = (lru_in, D + 256 * j, 256)
        for j in range(2):
            sources[0, f"mq{j}"] = (lru_in, 2 * D + 256 * j, 256)
            sources[1, f"mq{j}"] = (dsa_in, c_ik + ID + IH + 256 * j, 256)
            for l in range(2):
                sources[l, f"mk{j}"] = (kv[l], 256 * j, 256)
            for c, name in enumerate("qkv"):
                sources[1, f"{name}{j}"] = (dsa_in, D * c + 512 * j, 512)
        for l in range(2):
            sources[l, "mv"] = (kv[l], MEM_W, MEM_W)
        sources[1, "iq"] = (dsa_in, c_idx, IH * ID)
        sources[1, "ikw"] = (dsa_in, c_ik, ID + IH)
        out_order = (8, 10, 0, 2, 4, 6)

        units = {}
        for key, groups in GROUPS.items():
            for g in groups:
                w, c0, c = sources[g.layer, g.name]
                k = KD // g.units
                for j in range(g.units):
                    units[g.unit + j] = kxc(w, k * j, k, c0, c)
        for l, w in enumerate((lru_w_out[0], dsa_w_out[0])):
            for j, k in enumerate(out_order):
                units[U_OUT[l] + j] = kxc(w, k, 2, 0, D)

        def unit_size(n):
            k, c, _ = units.get(n, (2, 1024, None)) if isinstance(n, int) else (2, 1024, None)
            return k * c

        def group(key, name):
            return next(g for g in GROUPS[key] if g.name == name)

        @block.sync
        def _(sp):
            def load(n, slot, k, c, src):
                if not isinstance(n, int) or n >= RING:
                    sp.wait_ge(lo_ready, n - (RING - 1))
                sp.dma_start(w_raw[:, slot, 0:k * c].rearrange("p (k c) -> p k c", k=k), src).then_inc(raw_in[slot], 16)

            x_v = x_in[0].rearrange("(t p) d -> p t d", p=P)
            for t in range(NT):
                sp.dma_start(x[:, t, :], x_v[:, t, :]).then_inc(x_in_s[t], 16)
            for n in range(RING):
                load(n, n, *units[n])
            for t in range(NT):
                sp.dma_start(pos_i[:, t:t + 1], pos_in[0, t * P:(t + 1) * P].rearrange("(p o) -> p o", o=1)).then_inc(pos_in_s, 16)
            for l in range(2):
                taps = ffn_conv_w[l].rearrange("k (r c) -> (k r) c", c=P)
                nw = FFN_TAPS * FC
                sp.dma_start(rows[:, 1 + 2 * l, :], taps[0:P]).then_inc(taps_in_s, 16)
                sp.dma_start(rows[0:nw - P, 2 + 2 * l, :], taps[P:nw]).then_inc(taps_in_s, 16)
                sp.dma_start(rows[nw - P:nw - P + FC, 2 + 2 * l, :],
                             ffn_conv_b[l].rearrange("(r c) -> r c", c=P)).then_inc(taps_in_s, 16)
            sp.dma_start(mem_tok[:, :, :], mem_in[0].rearrange("(t p) d -> p t d", p=P)).then_inc(mem_in_s, 16)

            def ffn_loads(l):
                first = U_FFN[l]

                def up(n, i, half, slot):
                    load(n, slot, 8, 256, w_ffn_up[l][:, ds(half * FF + i * 256, 256)].rearrange("(k p) c -> p k c", p=P))

                def down(n, i, slot):
                    load(n, slot, 2, 1024, w_ffn_down[l][ds(i * 256, 256), :].rearrange("(k p) c -> p k c", p=P))

                up(first, 0, 0, first % RING)
                up(first + 1, 0, 1, (first + 1) % RING)
                with sp.Fori(1, NPAIR) as i:
                    up(first - 1 + i * 3, i, 0, (first - 1) % RING)
                    up(first + i * 3, i, 1, first % RING)
                    down(first + 1 + i * 3, i - 1, (first + 1) % RING)
                down(first + 3 * NPAIR - 1, NPAIR - 1, (first + 3 * NPAIR - 1) % RING)

            for n in range(RING, U_FFN[0]):
                load(n, n % RING, *units[n])
                if n == RING + 1:
                    sp.wait_ge(bd_zero, 1)
                    for w, src in enumerate((lru_w_a, lru_w_x)):
                        two = src[0].rearrange("(c e) i d -> e i c d", e=2)
                        for e in range(2):
                            sp.dma_start(w_bd[64 * e:64 * e + 64, w, :, 64 * e:64 * e + 64], two[e]).then_inc(bd_in_s, 16)

            ffn_loads(0)
            for n in range(START["fill2"], U_FFN[1]):
                load(n, n % RING, *units[n])
            ffn_loads(1)
            sp.dma_start(fin_g, final_norm.rearrange("(o d) -> o d", o=1).broadcast_to((P, D))).then_inc(fg_in_s, 16)
            out_v = out[0].rearrange("(t p) d -> p t d", p=P)
            for t in range(NT):
                sp.wait_ge(out_ready, 2 * t + 1)
                sp.dma_start(out_v[:, t, 0:512], xn[:, t, 0:512]).then_inc(out_s, 16)
            sp.wait_ge(out_s, 2 * 16 * NT)

        @block.gpsimd
        def _(pool):
            nc.gpsimd.memset(eps_t[:, :], EPS).then_inc(eps_ready, 1)
            nc.gpsimd.memset(ident[:, :], 0.0).then_inc(zeroed, 1)
            pool.wait_ge(zeroed, 1)
            nc.gpsimd.affine_select(out=ident[:, :], in_=ident[:, :], compare_op=ALU.not_equal, fill=1.0, base=0,
                                    pattern=[[-1, P]], channel_multiplier=1).then_inc(consts, 1)
            for v, at, n in ((norm_ffn, 16, 16), (mem_norm, 32, 8), (lru_conv_w, 40, 32), (lru_conv_b, 72, 8),
                             (lru_b_a, 80, 8), (lru_b_x, 88, 8), (lru_lambda, 96, 8)):
                flat = {1: "(r c) -> r c", 2: "a (r c) -> (a r) c", 3: "a b (r c) -> (a b r) c"}[len(v.shape)]
                pool.dma_start(rows[at:at + n, 0, :], v.rearrange(flat, c=P)).then_inc(rows_in_s, 16)
            nc.gpsimd.memset(w_bd[:, :, :, :], 0.0).then_inc(bd_zero, 1)
            freqs = [THETA ** (-f / AROT) for f in range(0, AROT, 2)] + [THETA ** (-f / IROT) for f in range(0, IROT, 2)]
            for f, v in enumerate(freqs):
                ins = nc.gpsimd.memset(inv_t[:, :, f:f + 1], float(np.float32(v)))
            ins.then_inc(inv_ready, 1)
            TS, TT = nc.gpsimd.tensor_scalar, nc.gpsimd.tensor_tensor
            links = [0]

            def link(ins):
                links[0] += 1
                ins.then_inc(pool_chain, 1)
                pool.wait_ge(pool_chain, links[0])

            pool.wait_ge(pos_in_s, 16 * NT)
            pool.wait_ge(inv_ready, 1)
            link(nc.gpsimd.tensor_copy(pos_f, pos_i))
            for t in range(NT):
                link(TS(ang[:, t, :], inv_t[:, t, :], pos_f[:, t:t + 1], None, ALU.mult))
            magic = 1.5 * 2.0 ** 23
            link(TS(turns, ang, 1.0 / (2 * math.pi), magic, ALU.mult, ALU.add))
            link(TS(turns, turns, -magic, None, ALU.add))
            c1 = 6.28125
            c2 = round((2 * math.pi - c1) * 2 ** 18) / 2 ** 18
            c3 = 2 * math.pi - c1 - c2
            for c in (c1, c2, c3):
                link(TS(wrap, turns, -c, None, ALU.mult))
                link(TT(ang, ang, wrap, ALU.add))
            top = float(np.nextafter(np.float32(math.pi), np.float32(0)))
            link(TS(wrap, ang, math.pi / 2, None, ALU.add))
            link(TS(turns, wrap, math.pi, -2 * math.pi, ALU.is_gt, ALU.mult))
            link(TT(wrap, wrap, turns, ALU.add))
            link(TS(wrap, wrap, top, -top, ALU.min, ALU.max))
            TS(ang, ang, top, -top, ALU.min, ALU.max).then_inc(trig_args, 1)

            for h in range(2):
                cs = slice(4 * h, 4 * h + 4)
                pool.wait_ge(gate_sig, 4 * h + 4)
                nc.gpsimd.tensor_tensor(iT[:, cs, :], iT[:, cs, :], xcT[:, cs, :], ALU.mult).then_inc(l_ix, 1)
            for h in range(2):
                cs = slice(4 * h, 4 * h + 4)
                pool.wait_ge(l_sqrt, h + 1)
                pool.wait_ge(l_ix, h + 1)
                nc.gpsimd.tensor_tensor(iT[:, cs, :], iT[:, cs, :], rT[:, cs, :], ALU.mult).then_inc(l_bt, 1)
            pool.wait_ge(unit_done, START["fill2"])
            nc.gpsimd.memset(ikpad[:, :, :, :], 0.0).then_inc(ik_zero, 1)

            def causal(src, n):
                nc.gpsimd.affine_select(out=src[:, 0:P], in_=src[:, 0:P], compare_op=ALU.is_ge, fill=FILL, base=0,
                                        pattern=[[-1, P]], channel_multiplier=1)
                nc.gpsimd.affine_select(out=src[:, P:3 * P], in_=src[:, P:3 * P], compare_op=ALU.is_ge, fill=FILL,
                                        base=P, pattern=[[-1, S]], channel_multiplier=1).then_inc(n, 1)

            pool.wait_ge(ix_acc, IH * NT)
            causal(score, causal_s)
            pool.wait_ge(bias_s, 1)
            causal(kbias, bias_ready)

        LAST_PLACE = 2
        MEM_SPANS, DSA_SPANS = ((0, S), (S, 2 * S)), ((0, P), (P, 3 * P))

        def is_mem(m):
            return m < 2 * MEM_H

        def cat_tile(m):
            return KD + m % MEM_H if is_mem(m) else m - 2 * MEM_H

        @block.scalar
        def _(act):
            def copy(dst, src):
                return nc.scalar.activation(dst, src, ACT.Copy)

            def split_hi(n, slot=None, turn=None):
                if isinstance(n, int):
                    if n >= U_END:
                        return
                    slot, turn = n % RING, 16 * (n // RING + 1)
                act.wait_ge(raw_in[slot], turn)
                if not isinstance(n, int) or n >= RING:
                    act.wait_ge(unit_done, n - (RING - 1))
                size = unit_size(n)
                copy(w_hi[:, slot, 0:size], w_raw[:, slot, 0:size]).then_inc(hi_ready, 1)

            loads = [0]

            def load_table(func):
                nc.scalar.activation(warm[:, loads[0]:loads[0] + 1], eps_t[:, :], func)
                loads[0] += 1

            def norm_stats(k, src, scrap):
                for t in range(NT):
                    if k == 0:
                        act.wait_ge(x_in_s[t], 16)
                    else:
                        act.wait_ge(mem_in_s, 16)
                    nc.scalar.activation(scrap[t], src[:, t, :], ACT.Square, accum_out=ssq[:, t:t + 1]).then_inc(sq_s, 1)
                    act.wait_ge(sq_s, 2 * k + t + 1)
                    nc.scalar.activation(std[:, t:t + 1], ssq[:, t:t + 1], ACT.Sqrt, scale=1.0 / D,
                                         bias=eps_t[:, 0:1]).then_inc(std_s, 1)
                    if k == 0 and t == 0:
                        gains_copy()

            def residual_stats(k, tiles=range(NT)):
                for t in tiles:
                    n = 2 * NT * (k - 2) + 2 * t
                    for half in range(2):
                        at = slice(512 * half, 512 * half + 512)
                        act.wait_ge(res_done, n + half + 1)
                        nc.scalar.activation(xn[:, t, at], x[:, t, at], ACT.Square,
                                             accum_out=(ssq, ssq_b)[half][:, t:t + 1]).then_inc(sq_s, 1)
                        act.wait_ge(sq_s, 2 * NT + n + half + 1)
                        if half == 0:
                            nc.scalar.activation(msq[:, t:t + 1], ssq[:, t:t + 1], ACT.Identity, scale=1.0 / D,
                                                 bias=eps_t[:, 0:1]).then_inc(msq_s, 1)
                    act.wait_ge(msq_s, NT * (k - 2) + t + 1)
                    nc.scalar.activation(std[:, t:t + 1], ssq_b[:, t:t + 1], ACT.Sqrt, scale=1.0 / D,
                                         bias=msq[:, t:t + 1]).then_inc(std_s, 1)

            def norm_hi(k, dst, gain, banks):
                for b in range(4):
                    act.wait_ge(n_tr, 4 * k + b + 1)
                    for e in range(2):
                        c = 2 * b + e
                        ins = nc.scalar.activation(dst[:, c, 0, :], banks[b][:, e * S:(e + 1) * S], ACT.Copy,
                                                   scale=prm[:, gain + c:gain + c + 1])
                    ins.then_inc(n_hi, 1)

            def norm_hi_tile(k, t, dst, gain):
                for b in range(2):
                    act.wait_ge(n_tr, 4 * k + 2 * t + b + 1)
                    for c in range(4 * b, 4 * b + 4):
                        ins = nc.scalar.activation(dst[:, c, 0, t * P:(t + 1) * P], A[2 * t + b][:, c % 4 * P:(c % 4 + 1) * P],
                                                   ACT.Copy, scale=prm[:, gain + c:gain + c + 1])
                    ins.then_inc(n_hi, 1)

            def chan_lows(g, banks=None, buf=chan_low):
                act.wait_ge(unit_done, g.unit + 1)
                for e in range(2):
                    if g.before:
                        act.wait_ge(summed, g.before + e - 1)
                    src = (banks or A[2 * g.pair:2 * g.pair + 2])[e]
                    copy(buf[:, e, :], src[:, S:2 * S]).then_inc(lowed, 1)

            def tok_copies(g, dsts, banks=None):
                act.wait_ge(unit_done, g.unit + 2)
                for t in range(NT):
                    src = (banks or A[2 * g.pair:2 * g.pair + 2])[t]
                    copy(dsts[t], src[:, 0:dsts[t].free_size()]).then_inc(copied, 1)

            def exp_of(m):
                b = m % 2
                act.wait_ge(at_nmax, m + 1)
                if is_mem(m) and m >= 2:
                    act.wait_ge(at_t, m - 1)
                for t, (lo, hi_) in enumerate(MEM_SPANS if is_mem(m) else DSA_SPANS):
                    src = SCORES[b][:, lo:hi_] if is_mem(m) else prob[:, b, lo:hi_]
                    ins = nc.scalar.activation(prob[:, b, lo:hi_], src, ACT.Exp, bias=nmax[:, b, t:t + 1],
                                               scale=MEM_HD ** -0.5 if is_mem(m) else 1.0, accum_out=ssum[:, b, t:t + 1])
                ins.then_inc(at_exp, 1)

            def turned_of(m):
                act.wait_ge(at_t, m + 1)
                if m:
                    act.wait_ge(at_o, m)
                width = 2 * S if is_mem(m) else 3 * P
                copy(probT[:, 0:width], TURNED[:, 0:width]).then_inc(at_pt, 1)

            def values_hi(m):
                act.wait_ge(at_o, m + 1)
                copy(cat[:, cat_tile(m), 0, :], VALUES[:, 0:S]).then_inc(at_hi, 1)

            def heads(step, lo, hi_):
                if lo <= step - 2 < hi_:
                    values_hi(step - 2)
                if lo <= step - 1 < hi_:
                    turned_of(step - 1)
                if lo <= step < hi_:
                    exp_of(step)

            act.dma_start(rows[0:16, 0, :], norm_mix.rearrange("a (r c) -> (a r) c", c=P)).then_inc(gain_in_s, 16)
            act.wait_ge(eps_ready, 1)
            load_table(ACT.Sqrt)
            def gains_copy():
                act.wait_ge(prm_t, 1)
                copy(prm[:, 0:16], U[0][:, 0:16]).then_inc(prm_ready, 1)
                act.wait_ge(prm_ready, 1)

            norm_stats(0, x, [xn[:, 0, :], xn[:, 1, :]])
            norm_hi(0, hT, C_MIX, A)
            act.wait_ge(hi_ready, 1)
            split_hi(1)
            split_hi(2)
            norm_stats(1, mem_tok, [junk, junk])

            def conv_taps(j):
                for c in (2 * j, 2 * j + 1):
                    act.wait_ge(summed, g0[f"x{j}"].before + c - 2 * j + 1)
                    nc.scalar.activation(xcT[:, c, :], xbT[:, c, :], ACT.Identity, bias=prm[:, C_LCB + c:C_LCB + c + 1],
                                         scale=prm[:, C_LCW + 24 + c:C_LCW + 25 + c]).then_inc(cv_tap, 1)

            g0 = {g.name: g for g in GROUPS["l0"]}

            def lows_hi(name):
                chan_lows(g0[name])
                split_hi(g0[name].unit + 3)

            lows_hi("x0")
            act.wait_ge(prm_t, 2)
            copy(prm[:, 16:], U[1][:, 16:NPRM]).then_inc(prm_ready, 1)
            act.wait_ge(prm_ready, 2)
            conv_taps(0)
            lows_hi("x1")
            conv_taps(1)
            lows_hi("mq0")
            norm_hi(1, memT, C_MEM, U)
            for j in (2, 3):
                lows_hi(f"x{j}")
                conv_taps(j)
            act.wait_ge(lam_exp, 1)
            nc.scalar.activation(lam_t[:, 1, :], lam_t[:, 0, :], ACT.Exp, scale=-1.0).then_inc(lam_exp, 1)
            act.wait_ge(trig_args, 1)
            nc.scalar.activation(trig[:, 0], ang[:, :, :], ACT.Sin)
            nc.scalar.activation(trig[:, 1], wrap[:, :, :], ACT.Sin).then_inc(trig_ready, 1)
            load_table(ACT.Sigmoid)
            lows_hi("mq1")

            def sigmoids(cs):
                for c in cs:
                    act.wait_ge(gate_mm, c + 1)
                    nc.scalar.activation(rT[:, c, :], U[c % 4][:, 0:S], ACT.Sigmoid, bias=prm[:, C_BA + c:C_BA + c + 1])
                    nc.scalar.activation(iT[:, c, :], U[c % 4][:, S:2 * S], ACT.Sigmoid,
                                         bias=prm[:, C_BX + c:C_BX + c + 1]).then_inc(gate_sig, 1)

            act.wait_ge(trig_ready, 1)
            sigmoids(range(4))
            lows_hi("mk0")
            sigmoids(range(4, KD))

            def decay(h):
                act.wait_ge(gate_sig, KD)
                act.wait_ge(lam_ready, 1)
                for c in range(4 * h, 4 * h + 4):
                    nc.scalar.activation(xbT[:, c, :], rT[:, c, :], ACT.Exp, scale=sp8[:, 1, c:c + 1]).then_inc(l_exp, 1)
                    nc.scalar.activation(tT[:, c, :], rT[:, c, :], ACT.Tanh, scale=sp8[:, 0, c:c + 1]).then_inc(l_tanh, 1)
                cs = slice(4 * h, 4 * h + 4)
                act.wait_ge(l_exp, 4 * h + 4)
                act.wait_ge(l_ix, h + 1)
                nc.scalar.activation(xcT[:, cs, :], xbT[:, cs, :], ACT.Square).then_inc(l_a2, 1)

            def gelu(h):
                cs = slice(4 * h, 4 * h + 4)
                act.wait_ge(summed, g0[f"gate{2 * h + 1}"].after)
                nc.scalar.activation(gbT[:, cs, :], gbT[:, cs, :], ACT.Gelu_apprx_tanh).then_inc(l_gelu, 1)

            def y_hi(h):
                cs = slice(4 * h, 4 * h + 4)
                act.wait_ge(l_y, h + 1)
                copy(cat[:, cs, 0, :], xbT[:, cs, :]).then_inc(l_yhi, 1)

            decay(0)
            lows_hi("mk1")
            decay(1)
            heads(0, 0, MEM_H)
            split_hi(g0["mv"].unit + 3)
            tok_copies(g0["mv"], [mv[:, t, :] for t in range(NT)])
            heads(1, 0, MEM_H)
            split_hi(g0["mv"].unit + 4)
            for j in range(4):
                g = g0[f"gate{j}"]
                chan_lows(g)
                heads(j + 2, 0, MEM_H)
                if j < 3:
                    split_hi(g.unit + 3)
                if j == 1:
                    load_table(ACT.Sqrt)
                    for h in range(2):
                        cs = slice(4 * h, 4 * h + 4)
                        act.wait_ge(l_gain2, h + 1)
                        nc.scalar.activation(rT[:, cs, :], tT[:, cs, :], ACT.Sqrt).then_inc(l_sqrt, 1)
                    load_table(ACT.Gelu_apprx_tanh)
                    gelu(0)
            y_hi(0)
            split_hi(g0["gate3"].unit + 3)
            gelu(1)
            y_hi(1)
            split_hi(U_OUT[0] + 3)

            for j in range(1, 5):
                split_hi(U_OUT[0] + j + 3)
            load_table(ACT.Sqrt)
            residual_stats(2)
            split_hi(U_OUT[0] + 5 + 3)
            for i, g in enumerate(GROUPS["fill1"]):
                chan_lows(g, U[2 * i:2 * i + 2], fill_low)
                if i == 0:
                    norm_hi(2, hT, C_FFN, A)
                split_hi(g.unit + 3)

            def ffn(l):
                first = U_FFN[l]
                cw, cb = C_F[l], C_F[l] + FFN_TAPS * FC

                def turn(ahead, i):
                    return ((first + ahead) // RING + 1) * 16 + i * 16

                def half(i, h, unit, ahead):
                    act.wait_ge(unit_done, unit + 1)
                    for c in range(2):
                        copy(ffn_low[:, 2 * h + c, :], U[2 * h + c][:, S:2 * S]).then_inc(f_low[l], 1)
                    if ahead is not None:
                        split_hi(first + ahead + i * 3, (first + ahead) % RING, turn(ahead, i))
                    for c in range(2):
                        ch = i * 2 + (h * (FC // 2) + c)
                        act.wait_ge(f_sum[l], i * 4 + (2 * h + c + 1))
                        nc.scalar.activation(ffn_y[:, 2 * h + c, :], ffn_u[:, 2 * h + c, :], ACT.Identity,
                                             bias=prm[:, ds(cb + ch, 1)], scale=prm[:, ds(cw + 2 * FC + ch, 1)]).then_inc(f_tap[l], 1)

                def tail(i, ahead, used):
                    act.wait_ge(f_conv[l], i * 4 + 2)
                    nc.scalar.activation(ffn_g[:, :, :], ffn_y[:, 0:2, :], ACT.Silu).then_inc(f_silu[l], 1)
                    if ahead is not None:
                        split_hi(first + ahead + i * 3, (first + ahead) % RING, turn(ahead, i))
                    if used:
                        act.wait_ge(unit_done, first + 2 + i * 3)
                    act.wait_ge(f_prod[l], i + 1)
                    copy(cat[:, 0:2, 0, :], ffn_p[:, :, :]).then_inc(f_hi[l], 1)

                half(0, 0, first, 3)
                half(0, 1, first + 1, 4)
                tail(0, None, False)
                with act.Fori(1, NPAIR - 1) as i:
                    half(i, 0, first - 1 + i * 3, 2)
                    half(i, 1, first + i * 3, 3)
                    tail(i, 4, True)
                i = NPAIR - 1
                half(i, 0, first - 1 + 3 * i, 2)
                half(i, 1, first + 3 * i, None)
                act.wait_ge(f_conv[l], i * 4 + 2)
                nc.scalar.activation(ffn_g[:, :, :], ffn_y[:, 0:2, :], ACT.Silu).then_inc(f_silu[l], 1)
                for c in range(2):
                    act.wait_ge(f_prod[l], i + c + 1)
                    copy(cat[:, LAST_PLACE + c, 0, :], ffn_p[:, c, :]).then_inc(f_hi[l], 1)
                load_table(ACT.Sqrt)
                split_hi(first + 3 + 3 * i)
                split_hi(first + 4 + 3 * i)

            ffn(0)
            residual_stats(3)
            split_hi(START["fill2"] + 2)
            g = GROUPS["fill2"][0]
            norm_hi(3, hT, C_MIX + KD, A)
            split_hi(g.unit + 3)
            tok_copies(g, [mv[:, t, :] for t in range(NT)], U[0:2])
            split_hi(g.unit + 4)

            g1 = {g.name: g for g in GROUPS["l1"]}
            iq_f = iq_tok[:, :, :, :].rearrange("p t h d -> p t (h d)")
            qk_f = qk_tok[:, :, :, :].rearrange("p t h d -> p t (h d)")

            def place(name):
                if name == "iq":
                    return [iq_f[:, t, :] for t in range(NT)]
                if name == "ikw":
                    return [ikw_tok[:, t, :] for t in range(NT)]
                v = v_tok if name[0] == "v" else qk_f
                c0 = 512 * int(name[1]) + (D if name[0] == "k" else 0)
                return [v[:, t, c0:c0 + 512] for t in range(NT)]

            def idx_relu(steps):
                for step in steps:
                    width = (step % NT + 1) * P
                    act.wait_ge(ix_mm, step + 1)
                    if step >= 2:
                        act.wait_ge(ix_acc, 2 * (step - 1))
                    nc.scalar.activation(prob[:, step % 2, 0:2 * width], U[step % 4][:, 0:2 * width], ACT.Relu,
                                         scale=ID ** -0.5).then_inc(ix_relu, 1)

            def qk_turned(c, half):
                for b in range(2 * half, 2 * half + 2):
                    act.wait_ge(q_tr, 4 * c + b + 1)
                    h = 4 * c + 2 * (b % 2) + AH * (b // 2)
                    copy(qkT[:, h:h + 2, :].rearrange("p h s -> p (h s)"), U[b % 2][:, :]).then_inc(q_trc, 1)

            def dense(name, mid, end):
                g = g1[name]
                if g.kind == "chan":
                    chan_lows(g)
                    split_hi(g.unit + 3)
                else:
                    mid()
                    split_hi(g.unit + 3)
                    tok_copies(g, place(name))
                    end()
                    split_hi(g.unit + 4)

            def nothing():
                pass

            dense("iq", nothing, nothing)
            dense("ikw", nothing, nothing)
            dense("mq0", nothing, nothing)
            dense("mq1", nothing, nothing)
            for b in range(3):
                act.wait_ge(ix_tr, b + 1)
                dst = ikT[:, :, :] if b == 2 else iqT[:, 2 * b:2 * b + 2, :]
                copy(dst.rearrange("p c s -> p (c s)"), U[b][:, :]).then_inc(ix_trc, 1)
            dense("v0", lambda: idx_relu((0, 1)), lambda: idx_relu((2, 3)))
            dense("q0", lambda: idx_relu((4, 5)), lambda: idx_relu((6, 7)))
            dense("k0", lambda: heads(4, 4, 16), lambda: heads(5, 4, 16))
            dense("q1", lambda: heads(6, 4, 16), lambda: heads(7, 4, 16))
            dense("k1", lambda: qk_turned(0, 0), lambda: qk_turned(0, 1))
            dense("v1", lambda: heads(8, 4, 16), lambda: heads(9, 4, 16))
            for step in range(10, 18):
                heads(step, 4, 16)
                if step == 11:
                    split_hi(U_OUT[1] + 3)
                    qk_turned(1, 0)
                    qk_turned(1, 1)
                if step in (12, 14, 16):
                    split_hi(U_OUT[1] + step // 2 - 2)
            split_hi(U_OUT[1] + 7)
            load_table(ACT.Sqrt)
            for t in range(NT):
                residual_stats(4, [t])
                norm_hi_tile(4, t, hT, C_FFN + KD)
            split_hi(U_OUT[1] + 8)
            ffn(1)
            residual_stats(5)
            out_v = out[0].rearrange("(t p) d -> p t d", p=P)
            for t in range(NT):
                act.wait_ge(out_ready, 2 * t + 2)
                act.dma_start(out_v[:, t, 512:D], xn[:, t, 512:D]).then_inc(out_s, 16)

        @block.vector
        def _(dve):
            TT, TS, STT = nc.vector.tensor_tensor, nc.vector.tensor_scalar, nc.vector.scalar_tensor_tensor
            links = [0]

            def link(ins):
                links[0] += 1
                ins.then_inc(chain, 1)
                dve.wait_ge(chain, links[0])

            def split_lo(n, slot=None):
                if isinstance(n, int):
                    if n >= U_END:
                        return
                    slot = n % RING
                size = unit_size(n)
                dve.wait_ge(hi_ready, n + 1)
                TT(w_lo[:, slot, 0:size], w_raw[:, slot, 0:size], w_hi[:, slot, 0:size].bitcast(fp32),
                   ALU.subtract).then_inc(lo_ready, 1)

            def norm_scale(k, t, dst, src):
                dve.wait_ge(std_s, 2 * k + t + 1)
                nc.vector.reciprocal(rstd[:, t:t + 1], std[:, t:t + 1]).then_inc(rstd_s, 1)
                dve.wait_ge(rstd_s, 2 * k + t + 1)
                if k < 5:
                    TS(dst[:, t, :], src[:, t, :], rstd[:, t:t + 1], None, ALU.mult).then_inc(xn_ready, 1)

            def norm_lo(k, dst, gain, banks):
                for b in range(4):
                    dve.wait_ge(n_hi, 4 * k + b + 1)
                    for e in range(2):
                        c = 2 * b + e
                        ins = STT(dst[:, c, 1, :], banks[b][:, e * S:(e + 1) * S], prm[:, gain + c:gain + c + 1],
                                  dst[:, c, 0, :].bitcast(fp32), ALU.mult, ALU.subtract)
                    ins.then_inc(n_lo, 1)

            def norm_lo_tile(k, t, dst, gain):
                for b in range(2):
                    dve.wait_ge(n_hi, 4 * k + 2 * t + b + 1)
                    for c in range(4 * b, 4 * b + 4):
                        ins = STT(dst[:, c, 1, t * P:(t + 1) * P], A[2 * t + b][:, c % 4 * P:(c % 4 + 1) * P],
                                  prm[:, gain + c:gain + c + 1], dst[:, c, 0, t * P:(t + 1) * P].bitcast(fp32),
                                  ALU.mult, ALU.subtract)
                    ins.then_inc(n_lo, 1)

            def chan_sums(g, dsts, banks=None, buf=chan_low):
                for e in range(2):
                    dve.wait_ge(lowed, g.before + e + 1)
                    src = (banks or A[2 * g.pair:2 * g.pair + 2])[e]
                    TT(dsts[e], src[:, 0:S], buf[:, e, :], ALU.add).then_inc(summed, 1)

            def scores_max(m):
                b = m % 2
                dve.wait_ge(at_s, m + 1)
                if is_mem(m):
                    src, scale, spans = SCORES[b], MEM_HD ** -0.5, MEM_SPANS
                else:
                    if m >= 2:
                        dve.wait_ge(at_t, m - 1)
                    STT(prob[:, b, 0:3 * P], SCORES[b][:, 0:3 * P], AD ** -0.5, kbias, ALU.mult, ALU.add).then_inc(at_sc, 1)
                    dve.wait_ge(at_sc, m - 2 * MEM_H + 1)
                    src, scale, spans = prob[:, b, :], 1.0, DSA_SPANS
                for t, (lo, hi_) in enumerate(spans):
                    ins = nc.vector.reduce_max(smax[:, b, t:t + 1], src[:, lo:hi_], AX.X)
                ins.then_inc(at_max, 1)
                dve.wait_ge(at_max, m + 1)
                TS(nmax[:, b, :], smax[:, b, :], -scale, None, ALU.mult).then_inc(at_nmax, 1)

            def prob_scale(m):
                b = m % 2
                dve.wait_ge(at_exp, m + 1)
                nc.vector.reciprocal(rsum[:, b, :], ssum[:, b, :]).then_inc(at_rs, 1)
                dve.wait_ge(at_rs, m + 1)
                for t, (lo, hi_) in enumerate(MEM_SPANS if is_mem(m) else DSA_SPANS):
                    ins = TS(prob[:, b, lo:hi_], prob[:, b, lo:hi_], rsum[:, b, t:t + 1], None, ALU.mult)
                ins.then_inc(at_p, 1)

            def values_lo(m):
                dve.wait_ge(at_hi, m + 1)
                c = cat_tile(m)
                TT(cat[:, c, 1, :], VALUES[:, 0:S], cat[:, c, 0, :].bitcast(fp32), ALU.subtract).then_inc(at_lo, 1)

            def heads(step, lo, hi_):
                if lo <= step < hi_:
                    scores_max(step)
                if lo <= step - 2 < hi_:
                    values_lo(step - 2)
                if lo <= step < hi_:
                    prob_scale(step)

            def residual(k, last_unit, t):
                if t == 0:
                    dve.wait_ge(tile_done, k + 1)
                else:
                    dve.wait_ge(unit_done, last_unit + 1)
                for n in range(2):
                    xs = x[:, t, 512 * n:512 * n + 512]
                    TT(xs, xs, A[2 * t + n][:, :], ALU.add).then_inc(res_done, 1)

            def residual_norm(k, last_unit):
                residual(k - 2, last_unit, 0)
                residual(k - 2, last_unit, 1)
                for t in range(NT):
                    norm_scale(k, t, xn, x)

            def conv_sums(j):
                for tap in range(1, LRU_TAPS):
                    for c in (2 * j, 2 * j + 1):
                        w = C_LCW + 8 * (LRU_TAPS - 1 - tap) + c
                        if tap == 1:
                            dve.wait_ge(cv_tap, c + 1)
                        else:
                            dve.wait_ge(cv_acc, 4 * j + 2 * (tap - 2) + c % 2 + 1)
                        STT(xcT[:, c, tap:], xbT[:, c, 0:S - tap], prm[:, w:w + 1], xcT[:, c, tap:], ALU.mult,
                            ALU.add).then_inc(xc_ready if tap == LRU_TAPS - 1 else cv_acc, 1)

            def softplus(first):
                lam = prm[:, C_LAM:C_LAM + KD]
                absl, u, den, s1, s2, q = (lam_t[:, r, :] for r in range(6))
                if first:
                    STT(absl, lam, -1.0, lam, ALU.mult, ALU.max).then_inc(lam_exp, 1)
                    return
                dve.wait_ge(lam_exp, 2)
                link(TS(den, u, 2.0, None, ALU.add))
                link(nc.vector.reciprocal(den, den))
                link(TT(s1, u, den, ALU.mult))
                link(TT(s2, s1, s1, ALU.mult))
                link(TS(q, s2, 1.0 / 17, None, ALU.mult))
                for odd in range(15, 1, -2):
                    link(STT(q, q, 1.0 / odd, s2, ALU.add, ALU.mult))
                link(STT(q, q, 1.0, s1, ALU.add, ALU.mult))
                link(TS(den, lam, -1.0, 0.0, ALU.mult, ALU.max))
                link(STT(q, q, 2.0, den, ALU.mult, ALU.add))
                TS(sp8[:, 0, :], q, 8.0, None, ALU.mult)
                TS(sp8[:, 1, :], q, -8.0, None, ALU.mult).then_inc(lam_ready, 1)

            for t in range(NT):
                norm_scale(0, t, xn, x)
            dve.wait_ge(raw_in[0], 16)
            nc.vector.tensor_copy(w_hi[:, 0, :], w_raw[:, 0, :]).then_inc(hi_ready, 1)
            dve.wait_ge(prm_ready, 1)
            norm_lo(0, hT, C_MIX, A)
            split_lo(0)
            split_lo(1)
            split_lo(2)
            for t in range(NT):
                norm_scale(1, t, mem_tok, mem_tok)

            g0 = {g.name: g for g in GROUPS["l0"]}

            def sums_lo(name, dst):
                n = int(name[-1])
                chan_sums(g0[name], [dst[:, 2 * n + e, :] for e in range(2)])
                split_lo(g0[name].unit + 3)

            sums_lo("x0", xbT)
            dve.wait_ge(prm_ready, 2)
            conv_sums(0)
            sums_lo("x1", xbT)
            conv_sums(1)
            sums_lo("mq0", mqT)
            norm_lo(1, memT, C_MEM, U)
            for j in (2, 3):
                sums_lo(f"x{j}", xbT)
                if j == 3:
                    softplus(True)
                conv_sums(j)
            sums_lo("mq1", mqT)
            softplus(False)
            sums_lo("mk0", mkT)
            sums_lo("mk1", mkT)

            def gain2(h):
                cs = slice(4 * h, 4 * h + 4)
                dve.wait_ge(l_tanh, 4 * h + 4)
                dve.wait_ge(l_a2, h + 1)
                STT(tT[:, cs, :], xcT[:, cs, :], 1.0, tT[:, cs, :], ALU.add, ALU.mult).then_inc(l_gain2, 1)

            def recurrence(h):
                dve.wait_ge(l_bt, h + 1)
                for c in range(4 * h, 4 * h + 4):
                    nc.vector.tensor_tensor_scan(tT[:, c, :], xbT[:, c, :], iT[:, c, :], 0.0, ALU.mult,
                                                 ALU.add).then_inc(l_h, 1)

            def lru_y(h):
                cs = slice(4 * h, 4 * h + 4)
                dve.wait_ge(l_gelu, h + 1)
                dve.wait_ge(l_h, 4 * h + 4)
                TT(xbT[:, cs, :], tT[:, cs, :], gbT[:, cs, :], ALU.mult).then_inc(l_y, 1)

            def y_lo(h):
                cs = slice(4 * h, 4 * h + 4)
                dve.wait_ge(l_yhi, h + 1)
                TT(cat[:, cs, 1, :], xbT[:, cs, :], cat[:, cs, 0, :].bitcast(fp32), ALU.subtract).then_inc(l_ylo, 1)

            gain2(0)
            heads(0, 0, MEM_H)
            gain2(1)
            split_lo(g0["mv"].unit + 3)
            heads(1, 0, MEM_H)
            split_lo(g0["mv"].unit + 4)
            for j in range(4):
                g = g0[f"gate{j}"]
                chan_sums(g, [gbT[:, 2 * j + e, :] for e in range(2)])
                heads(j + 2, 0, MEM_H)
                if j == 2:
                    lru_y(0)
                if j < 3:
                    split_lo(g.unit + 3)
                if j == 1:
                    recurrence(0)
            recurrence(1)
            y_lo(0)
            lru_y(1)
            split_lo(g0["gate3"].unit + 3)
            y_lo(1)
            split_lo(U_OUT[0] + 3)
            for j in range(1, 5):
                split_lo(U_OUT[0] + j + 3)
            residual_norm(2, U_OUT[0] + 5)
            split_lo(U_OUT[0] + 5 + 3)
            for i, g in enumerate(GROUPS["fill1"]):
                chan_sums(g, [mkT[:, 2 * i + e, :] for e in range(2)], U[2 * i:2 * i + 2], fill_low)
                if i == 0:
                    norm_lo(2, hT, C_FFN, A)
                split_lo(g.unit + 3)

            def ffn(l):
                first = U_FFN[l]
                cw = C_F[l]

                def half(i, h, ahead):
                    for c in range(2):
                        dve.wait_ge(f_low[l], i * 4 + (2 * h + c + 1))
                        TT(ffn_u[:, 2 * h + c, :], U[2 * h + c][:, 0:S], ffn_low[:, 2 * h + c, :],
                           ALU.add).then_inc(f_sum[l], 1)
                    if ahead is not None:
                        split_lo(first + ahead + i * 3, (first + ahead) % RING)
                    for c in range(2):
                        ch = i * 2 + (h * (FC // 2) + c)
                        k = 2 * h + c
                        dve.wait_ge(f_tap[l], i * 4 + (k + 1))
                        STT(ffn_y[:, k, 1:], ffn_u[:, k, 0:S - 1], prm[:, ds(cw + FC + ch, 1)], ffn_y[:, k, 1:], ALU.mult,
                            ALU.add).then_inc(f_acc[l], 1)
                    for c in range(2):
                        ch = i * 2 + (h * (FC // 2) + c)
                        k = 2 * h + c
                        dve.wait_ge(f_acc[l], i * 4 + (k + 1))
                        STT(ffn_y[:, k, 2:], ffn_u[:, k, 0:S - 2], prm[:, ds(cw + ch, 1)], ffn_y[:, k, 2:], ALU.mult,
                            ALU.add).then_inc(f_conv[l], 1)

                def tail(i, ahead):
                    dve.wait_ge(f_silu[l], i + 1)
                    dve.wait_ge(f_conv[l], i * 4 + 4)
                    TT(ffn_p[:, :, :], ffn_g[:, :, :], ffn_y[:, 2:4, :], ALU.mult).then_inc(f_prod[l], 1)
                    if ahead is not None:
                        split_lo(first + ahead + i * 3, (first + ahead) % RING)
                    dve.wait_ge(f_hi[l], i + 1)
                    TT(cat[:, 0:2, 1, :], ffn_p[:, :, :], cat[:, 0:2, 0, :].bitcast(fp32), ALU.subtract).then_inc(f_lo[l], 1)

                half(0, 0, 3)
                half(0, 1, 4)
                tail(0, None)
                with dve.Fori(1, NPAIR - 1) as i:
                    half(i, 0, 2)
                    half(i, 1, 3)
                    tail(i, 4)
                i = NPAIR - 1
                half(i, 0, 2)
                half(i, 1, None)
                dve.wait_ge(f_silu[l], i + 1)
                for c in range(2):
                    dve.wait_ge(f_conv[l], i * 4 + c + 3)
                    TT(ffn_p[:, c, :], ffn_g[:, c, :], ffn_y[:, 2 + c, :], ALU.mult).then_inc(f_prod[l], 1)
                for c in range(2):
                    dve.wait_ge(f_hi[l], i + c + 1)
                    TT(cat[:, LAST_PLACE + c, 1, :], ffn_p[:, c, :], cat[:, LAST_PLACE + c, 0, :].bitcast(fp32),
                       ALU.subtract).then_inc(f_lo[l], 1)
                split_lo(first + 3 + 3 * i)

            ffn(0)
            residual_norm(3, U_FFN[0] + 3 * NPAIR - 1)
            split_lo(START["fill2"] + 1)
            norm_lo(3, hT, C_MIX + KD, A)
            split_lo(START["fill2"] + 2)
            split_lo(START["fill2"] + 3)
            split_lo(START["fill2"] + 4)

            def rope(v, half, f0, done, count):
                heads_ = v.shape[2]
                a, b = v[:, :, :, 0:half], v[:, :, :, half:2 * half]
                sin, cos = (trig[:, r, :, f0:f0 + half].unsqueeze(2).broadcast_to((P, NT, heads_, half)) for r in range(2))
                n = NT * heads_ * half
                t0, t1, t2, t3 = (rope_t[:, r, 0:n].rearrange("p (t h d) -> p t h d", t=NT, h=heads_) for r in range(4))
                TT(t0, a, cos, ALU.mult)
                TT(t1, b, sin, ALU.mult)
                TT(t2, b, cos, ALU.mult)
                link(TT(t3, a, sin, ALU.mult))
                TT(a, t0, t1, ALU.subtract)
                TT(b, t2, t3, ALU.add).then_inc(done, 1)
                dve.wait_ge(done, count)

            def rope_chunk(name, count):
                h = 4 * int(name[1]) + (AH if name[0] == "k" else 0)
                dve.wait_ge(copied, g1[name].after)
                rope(qk_tok[:, :, h:h + 4, :], AROT // 2, 0, rope_q, count)

            def idx_sums(steps):
                for step in steps:
                    hp, t = step // NT, step % NT
                    width = (t + 1) * P
                    dst = score[:, 0:P] if t == 0 else score[:, P:3 * P]
                    dve.wait_ge(ix_relu, step + 1)
                    for e in range(2):
                        h = 2 * hp + e
                        src = prob[:, step % 2, e * width:(e + 1) * width]
                        w = ikw_tok[:, t, ID + h:ID + h + 1]
                        if h == 0:
                            TS(dst, src, w, None, ALU.mult).then_inc(ix_acc, 1)
                        else:
                            dve.wait_ge(ix_acc, 2 * step + e if e else 2 * step - 2)
                            STT(dst, src, w, dst, ALU.mult, ALU.add).then_inc(ix_acc, 1)

            def top_rounds(rounds):
                for r in rounds:
                    for t, (lo, hi_) in enumerate(DSA_SPANS):
                        if r:
                            dve.wait_ge(top_s, 4 * r - 1 + t)
                        nc.vector.max(top8[:, t, :], score[:, lo:hi_]).then_inc(top_s, 1)
                    for t, (lo, hi_) in enumerate(DSA_SPANS):
                        dve.wait_ge(top_s, 4 * r + 1 + t)
                        nc.vector.match_replace(score[:, lo:hi_], top8[:, t, :], score[:, lo:hi_], PICKED).then_inc(top_s, 1)

            g1 = {g.name: g for g in GROUPS["l1"]}

            for name in ("iq", "ikw"):
                split_lo(g1[name].unit + 3)
                split_lo(g1[name].unit + 4)
            dve.wait_ge(trig_ready, 1)
            dve.wait_ge(copied, g1["ikw"].after)
            rope(iq_tok[:, :, :, :], IROT // 2, AROT // 2, rope_i, 1)
            rope(ikw_tok[:, :, 0:ID].unsqueeze(2), IROT // 2, AROT // 2, rope_i, 2)
            dve.wait_ge(ik_zero, 1)
            for e in range(2):
                nc.vector.tensor_copy(ikpad[:, :, e, ID * e:ID * e + ID], ikw_tok[:, :, 0:ID])
            TS(ikw_tok[:, :, ID:], ikw_tok[:, :, ID:], IH ** -0.5, None, ALU.mult).then_inc(ik_copied, 1)
            dve.wait_ge(ik_copied, 1)
            for j in range(2):
                chan_sums(g1[f"mq{j}"], [mqT[:, 2 * j + e, :] for e in range(2)])
                split_lo(g1[f"mq{j}"].unit + 3)
            idx_sums((0, 1))
            split_lo(g1["v0"].unit + 3)
            idx_sums((2, 3))
            split_lo(g1["v0"].unit + 4)
            idx_sums((4, 5))
            split_lo(g1["q0"].unit + 3)
            idx_sums((6, 7))
            split_lo(g1["q0"].unit + 4)
            dve.wait_ge(causal_s, 1)
            top_rounds((0,))
            heads(4, 4, 16)
            top_rounds((1,))
            split_lo(g1["k0"].unit + 3)
            heads(5, 4, 16)
            top_rounds((2,))
            rope_chunk("q0", 1)
            split_lo(g1["k0"].unit + 4)
            heads(6, 4, 16)
            top_rounds((3,))
            split_lo(g1["q1"].unit + 3)
            rope_chunk("k0", 2)
            heads(7, 4, 16)
            top_rounds((4,))
            split_lo(g1["q1"].unit + 4)
            top_rounds((5, 6))
            split_lo(g1["k1"].unit + 3)
            top_rounds((7,))
            dve.wait_ge(top_s, 4 * (TOPK // 8))
            TS(kbias, score, PICKED, FILL, ALU.not_equal, ALU.mult).then_inc(bias_s, 1)
            rope_chunk("q1", 3)
            split_lo(g1["k1"].unit + 4)
            dve.wait_ge(bias_ready, 1)
            heads(8, 4, 16)
            rope_chunk("k1", 4)
            split_lo(g1["v1"].unit + 3)
            heads(9, 4, 16)
            split_lo(g1["v1"].unit + 4)
            for step in range(10, 18):
                heads(step, 4, 16)
                if step == 11:
                    split_lo(U_OUT[1] + 3)
                if step in (12, 14, 16):
                    split_lo(U_OUT[1] + step // 2 - 2)
            residual(2, U_OUT[1] + 5, 0)
            norm_scale(4, 0, xn, x)
            residual(2, U_OUT[1] + 5, 1)
            norm_lo_tile(4, 0, hT, C_FFN + KD)
            norm_scale(4, 1, xn, x)
            split_lo(U_OUT[1] + 7)
            norm_lo_tile(4, 1, hT, C_FFN + KD)
            split_lo(U_OUT[1] + 5 + 3)
            ffn(1)
            residual(3, U_END - 1, 0)
            residual(3, U_END - 1, 1)
            dve.wait_ge(fg_in_s, 16)
            for t in range(NT):
                norm_scale(5, t, None, None)
                for at in (slice(0, 512), slice(512, D)):
                    STT(xn[:, t, at], x[:, t, at], rstd[:, t:t + 1], fin_g[:, at], ALU.mult,
                        ALU.mult).then_inc(out_ready, 1)

        @block.tensor
        def _(pe):
            mm = nc.tensor.matmul

            def transpose(dst, src):
                return nc.tensor.transpose(dst, src, ident[0:src.shape[0], 0:src.shape[0]])

            def keep_busy(count):
                for n in range(count):
                    transpose(U[3][:, (n % 4) * P:(n % 4 + 1) * P], ident[:, :])

            def weights(n):
                pe.wait_ge(lo_ready, n + 1)

            def norm_transpose(k, src, banks):
                for t in range(NT):
                    pe.wait_ge(xn_ready, 2 * k + t + 1)
                for b in range(4):
                    for e in range(2):
                        c = 2 * b + e
                        for t in range(NT):
                            ins = transpose(banks[b][:, e * S + t * P:e * S + (t + 1) * P], src[:, t, c * P:(c + 1) * P])
                    ins.then_inc(n_tr, 1)

            def norm_transpose_tile(k, t):
                pe.wait_ge(xn_ready, 2 * k + t + 1)
                for c in range(KD):
                    ins = transpose(A[2 * t + c // 4][:, c % 4 * P:(c % 4 + 1) * P], xn[:, t, c * P:(c + 1) * P])
                    if c % 4 == 3:
                        ins.then_inc(n_tr, 1)

            def channel_ready(norm, k):
                if norm is not None:
                    pe.wait_ge(n_lo, 4 * norm + k // 2 + 1)

            def chan_major(slot, e, rhs, bank, norm=None):
                for k in range(8):
                    channel_ready(norm, k)
                    at = k * 256 + e * P
                    hi_args = (bank[:, :], w_hi[:, slot, at:at + P], rhs[:, k, :, :].rearrange("p a s -> p (a s)"))
                    lo_args = (bank[:, 0:S], w_lo[:, slot, at:at + P], rhs[:, k, 0, :])
                    if k < 7:
                        mm(*hi_args, start=(k == 0), stop=False)
                        mm(*lo_args, start=False, stop=False)
                    else:
                        mm(*lo_args, start=False, stop=False)
                        last = mm(*hi_args, start=False, stop=True)
                return last

            def chan_major_tile(slot, e, t, bank, norm):
                both = bank[:, :].rearrange("p (a s) -> p a s", a=2)[:, :, t * P:(t + 1) * P]
                for k in range(8):
                    pe.wait_ge(n_lo, 4 * norm + 2 * t + k // 4 + 1)
                    at = k * 256 + e * P
                    hi_args = (both, w_hi[:, slot, at:at + P], hT[:, k, :, t * P:(t + 1) * P])
                    lo_args = (bank[:, t * P:(t + 1) * P], w_lo[:, slot, at:at + P], hT[:, k, 0, t * P:(t + 1) * P])
                    if k < 7:
                        mm(*hi_args, start=(k == 0), stop=False)
                        mm(*lo_args, start=False, stop=False)
                    else:
                        mm(*lo_args, start=False, stop=False)
                        last = mm(*hi_args, start=False, stop=True)
                return last

            def first_unit(banks, norm):
                pe.wait_ge(hi_ready, 1)
                for e in range(2):
                    for k in range(7):
                        channel_ready(norm, max(k, 3 * e))
                        at = k * 256 + e * P
                        mm(banks[e][:, :], w_hi[:, 0, at:at + P], hT[:, k, :, :].rearrange("p a s -> p (a s)"),
                           start=(k == 0), stop=False)
                channel_ready(norm, 7)
                weights(0)
                for e in range(2):
                    for k in range(8):
                        at = k * 256 + e * P
                        mm(banks[e][:, 0:S], w_lo[:, 0, at:at + P], hT[:, k, 0, :], start=False, stop=False)
                    last = mm(banks[e][:, :], w_hi[:, 0, at:at + P], hT[:, 7, :, :].rearrange("p a s -> p (a s)"),
                              start=False, stop=True)
                last.then_inc(unit_done, 1)

            def tok_major(slot, width, ktiles, lhs, k0, first, last, banks, done=None, ready=None, tiles=range(NT)):
                cols = [(n, a, min(width, a + 512)) for n, a in enumerate(range(0, width, 512))]
                for t in tiles:
                    for k in range(ktiles):
                        if ready is not None and t == tiles[0]:
                            ready(k)
                        hi_l = lhs[:, k0 + k, 0, t * P:(t + 1) * P]
                        lo_l = lhs[:, k0 + k, 1, t * P:(t + 1) * P]
                        for part_no, (l_, src) in enumerate(((hi_l, w_hi), (hi_l, w_lo), (lo_l, w_hi))):
                            for n, a, b in cols:
                                ins = mm(banks[t][n][:, 0:b - a], l_, src[:, slot, k * width + a:k * width + b],
                                         start=(first and k == 0 and part_no == 0),
                                         stop=(last and k == ktiles - 1 and part_no == 2))
                    if done is not None and t == 0:
                        ins.then_inc(done, 1)
                return ins

            def dense_unit(g, j, lhs, banks=None, norm=None):
                n = g.unit + j
                b0, b1 = banks or A[2 * g.pair:2 * g.pair + 2]
                weights(n)
                if g.kind == "chan":
                    chan_major(n % RING, 0, lhs, b0, norm)
                    ins = chan_major(n % RING, 1, lhs, b1)
                else:
                    ins = tok_major(n % RING, unit_size(n) // 4, 4, lhs, 4 * j, j == 0, j == 1, [[b0], [b1]],
                                    ready=lambda k: channel_ready(norm, 4 * j + k))
                ins.then_inc(unit_done, 1)

            def wait_evacuated(g):
                pe.wait_ge(summed if g.kind == "chan" else copied, g.after)

            def dense(key, name, lhs, mid=None, end=None, norm=None):
                groups = GROUPS[key]
                at = [g.name for g in groups].index(name)
                if at >= 2:
                    wait_evacuated(groups[at - 2])
                for j in range(groups[at].units):
                    dense_unit(groups[at], j, lhs, None, norm)
                    for do in (mid, end)[j + 2 - groups[at].units:][:1]:
                        if do is not None:
                            do()

            def out_unit(l, j, tiles=range(NT), done=True):
                n, k0, last = U_OUT[l] + j, out_order[j], j == 5
                if j == 0:
                    for g in GROUPS["l0" if l == 0 else "l1"][-2:]:
                        if g.pair in tiles:
                            wait_evacuated(g)
                if l == 0 and k0 in (0, 4):
                    pe.wait_ge(l_ylo, k0 // 4 + 1)
                if l == 0 and k0 >= KD:
                    pe.wait_ge(at_lo, k0 - KD + 2)
                if l == 1 and k0 < KD:
                    pe.wait_ge(at_lo, 2 * MEM_H + k0 + 2)
                weights(n)
                ins = tok_major(n % RING, D, 2, cat, k0, j == 0, last, [A[0:2], A[2:4]],
                                tile_done if last else None, tiles=tiles)
                if done:
                    ins.then_inc(unit_done, 1)

            def scores(m):
                b = m % 2
                if m >= 2:
                    if is_mem(m - 2):
                        pe.wait_ge(at_exp, m - 1)
                    else:
                        pe.wait_ge(at_sc, m - 1 - 2 * MEM_H)
                if is_mem(m):
                    h = m % MEM_H
                    for t in range(NT):
                        ins = mm(SCORES[b][:, t * S:(t + 1) * S], mqT[:, h, t * P:(t + 1) * P], mkT[:, h, :],
                                 start=True, stop=True)
                else:
                    h = m - 2 * MEM_H
                    mm(SCORES[b][:, 0:P], qkT[:, h, 0:P], qkT[:, AH + h, 0:P], start=True, stop=True)
                    ins = mm(SCORES[b][:, P:3 * P], qkT[:, h, P:2 * P], qkT[:, AH + h, :], start=True, stop=True)
                ins.then_inc(at_s, 1)

            def turn(m):
                b = m % 2
                pe.wait_ge(at_p, m + 1)
                if m:
                    pe.wait_ge(at_pt, m)
                if is_mem(m):
                    for k in range(NT):
                        for t in range(NT):
                            ins = transpose(TURNED[:, k * S + t * P:k * S + (t + 1) * P],
                                            prob[:, b, t * S + k * P:t * S + (k + 1) * P])
                else:
                    for k in range(3):
                        ins = transpose(TURNED[:, k * P:(k + 1) * P], prob[:, b, k * P:(k + 1) * P])
                ins.then_inc(at_t, 1)

            def values(m):
                pe.wait_ge(at_pt, m + 1)
                if m:
                    pe.wait_ge(at_lo, m)
                if is_mem(m):
                    h = m % MEM_H
                    for k in range(NT):
                        ins = mm(VALUES[:, 0:S], mv[:, k, h * P:(h + 1) * P], probT[:, k * S:(k + 1) * S],
                                 start=(k == 0), stop=(k == 1))
                else:
                    h = m - 2 * MEM_H
                    mm(VALUES[:, 0:S], v_tok[:, 0, h * P:(h + 1) * P], probT[:, 0:S], start=True, stop=False)
                    ins = mm(VALUES[:, P:S], v_tok[:, 1, h * P:(h + 1) * P], probT[:, S:S + P], start=False, stop=True)
                ins.then_inc(at_o, 1)

            def heads(step, lo, hi_):
                if lo <= step < hi_:
                    scores(step)
                if lo <= step - 2 < hi_:
                    values(step - 2)
                if lo <= step - 1 < hi_:
                    turn(step - 1)

            pe.wait_ge(consts, 1)
            keep_busy(16)
            pe.wait_ge(gain_in_s, 16)
            transpose(U[0][:, 0:16], rows[0:16, 0, :]).then_inc(prm_t, 1)
            keep_busy(22)
            norm_transpose(0, xn, A)
            keep_busy(6)

            first_unit(A[0:2], 0)
            pe.wait_ge(rows_in_s, 16 * 7)
            pe.wait_ge(taps_in_s, 16 * 6)
            nw2 = (FFN_TAPS + 1) * FC - P
            transpose(U[1][:, 0:C_MISC], rows[0:C_MISC, 0, :])
            for l in range(2):
                transpose(U[1][:, C_F[l]:C_F[l] + P], rows[:, 1 + 2 * l, :])
                last = transpose(U[1][:, C_F[l] + P:C_F[l] + P + nw2], rows[0:nw2, 2 + 2 * l, :])
            last.then_inc(prm_t, 1)
            dense("l0", "x1", hT)
            dense("l0", "mq0", hT)
            pe.wait_ge(prm_ready, 2)
            norm_transpose(1, mem_tok, U)
            for name in ("x2", "x3", "mq1"):
                dense("l0", name, hT)

            def gates(cs):
                for c in cs:
                    pe.wait_ge(xc_ready, c + 1)
                    if c >= 4:
                        pe.wait_ge(gate_sig, c - 3)
                    mm(U[c % 4][:, 0:S], w_bd[:, 0, c, :], xcT[:, c, :], start=True, stop=True)
                    mm(U[c % 4][:, S:2 * S], w_bd[:, 1, c, :], xcT[:, c, :], start=True, stop=True).then_inc(gate_mm, 1)

            pe.wait_ge(bd_in_s, 64)
            pe.wait_ge(n_lo, 8)
            gates(range(4))
            dense("l0", "mk0", memT)
            gates(range(4, KD))
            dense("l0", "mk1", memT)

            def heads0(step):
                if step == 0:
                    pe.wait_ge(gate_sig, KD)
                    pe.wait_ge(summed, group("l0", "mk1").after)
                if step == 2:
                    pe.wait_ge(copied, group("l0", "mv").after)
                heads(step, 0, MEM_H)

            dense("l0", "mv", memT, lambda: heads0(0), lambda: heads0(1))
            for j in range(4):
                dense("l0", f"gate{j}", hT, end=lambda: heads0(j + 2))
            out_unit(0, 0, [1], False)
            out_unit(0, 0, [0])
            for j in range(1, 6):
                out_unit(0, j)
            for i, g in enumerate(GROUPS["fill1"]):
                dense_unit(g, 0, memT, U[2 * i:2 * i + 2])
                if i == 0:
                    norm_transpose(2, xn, A)

            def ffn(l, norm, fillers=()):
                first = U_FFN[l]

                def up(i, h, n, slot, norm_=None):
                    weights(n)
                    if fillers and isinstance(i, int) and i == 0:
                        pe.wait_ge(summed, fillers[h].after)
                    if not (isinstance(i, int) and i == 0):
                        pe.wait_ge(f_sum[l], i * 4 - 4 + (2 * h + 2))
                    chan_major(slot, 0, hT, U[2 * h], norm_)
                    chan_major(slot, 1, hT, U[2 * h + 1]).then_inc(unit_done, 1)

                def down(i, n, slot, first_, last_):
                    weights(n)
                    if last_:
                        tok_major(slot, D, 2, cat, LAST_PLACE, False, True, [A[0:2], A[2:4]], tile_done,
                                  ready=lambda k: pe.wait_ge(f_lo[l], i + k + 1)).then_inc(unit_done, 1)
                    else:
                        pe.wait_ge(f_lo[l], i + 1)
                        tok_major(slot, D, 2, cat, 0, first_, False, [A[0:2], A[2:4]]).then_inc(unit_done, 1)

                if l == 0:
                    up(0, 0, first, first % RING, norm)
                    up(0, 1, first + 1, (first + 1) % RING)
                else:
                    for t in range(NT):
                        for h in range(2):
                            if h == 0 and t == 0:
                                keep_busy(10)
                                norm_transpose_tile(norm, 0)
                                keep_busy(10)
                            if h == 1 and t == 0:
                                norm_transpose_tile(norm, 1)
                            weights(first + h)
                            for e in range(2):
                                ins = chan_major_tile((first + h) % RING, e, t, U[2 * h + e], norm)
                            if t == NT - 1:
                                ins.then_inc(unit_done, 1)
                up(1, 0, first + 2, (first + 2) % RING)
                up(1, 1, first + 3, first % RING)
                down(0, first + 4, (first + 1) % RING, True, False)
                with pe.Fori(2, NPAIR) as i:
                    up(i, 0, first - 1 + i * 3, (first - 1) % RING)
                    up(i, 1, first + i * 3, first % RING)
                    down(i - 1, first + 1 + i * 3, (first + 1) % RING, False, False)
                down(NPAIR - 1, first + 3 * NPAIR - 1, (first + 3 * NPAIR - 1) % RING, False, True)

            ffn(0, 2, GROUPS["fill1"])
            pe.wait_ge(f_sum[0], 4 * NPAIR)
            g = GROUPS["fill2"][0]
            dense_unit(g, 0, memT, U[0:2])
            norm_transpose(3, xn, A)
            dense_unit(g, 1, memT, U[0:2])

            dense("l1", "iq", hT, norm=3)
            dense("l1", "ikw", hT)
            dense("l1", "mq0", hT)
            dense("l1", "mq1", hT)
            pe.wait_ge(rope_i, 2)
            pe.wait_ge(ik_copied, 1)
            pe.wait_ge(copied, g.after)
            iq_f = iq_tok[:, :, :, :].rearrange("p t h d -> p t (h d)")
            for b in range(3):
                for e in range(2):
                    for t in range(NT):
                        src = ikpad[:, t, e, :] if b == 2 else iq_f[:, t, (2 * b + e) * P:(2 * b + e + 1) * P]
                        ins = transpose(U[b][:, e * S + t * P:e * S + (t + 1) * P], src)
                ins.then_inc(ix_tr, 1)

            def idx_scores(steps):
                pe.wait_ge(ix_trc, 3)
                for step in steps:
                    hp, t = step // NT, step % NT
                    width = (t + 1) * P
                    if step >= 4:
                        pe.wait_ge(ix_relu, step - 3)
                    for e in range(2):
                        ins = mm(U[step % 4][:, e * width:(e + 1) * width], iqT[:, hp, t * P:(t + 1) * P],
                                 ikT[:, e, 0:width], start=True, stop=True)
                    ins.then_inc(ix_mm, 1)

            qk_f = qk_tok[:, :, :, :].rearrange("p t h d -> p t (h d)")

            def qk_turn(c, half):
                pe.wait_ge(rope_q, 2 * c + half + 1)
                pe.wait_ge(at_exp, 8 + 4 * c)
                for b in range(2 * half, 2 * half + 2):
                    if b >= 2:
                        pe.wait_ge(q_trc, 4 * c + b - 1)
                    h = 4 * c + 2 * (b % 2) + AH * (b // 2)
                    for e in range(2):
                        for t in range(NT):
                            ins = transpose(U[b % 2][:, e * S + t * P:e * S + (t + 1) * P],
                                            qk_f[:, t, (h + e) * P:(h + e + 1) * P])
                    ins.then_inc(q_tr, 1)

            def heads1(step):
                if step == 4:
                    pe.wait_ge(ix_relu, IH)
                    pe.wait_ge(summed, group("l1", "mq1").after)
                if step == 8:
                    pe.wait_ge(q_trc, 4)
                if step == 10:
                    pe.wait_ge(copied, group("l1", "v1").after)
                if step == 12:
                    pe.wait_ge(q_trc, 8)
                heads(step, 4, 16)

            dense("l1", "v0", hT, lambda: idx_scores((0, 1)), lambda: idx_scores((2, 3)))
            dense("l1", "q0", hT, lambda: idx_scores((4, 5)), lambda: idx_scores((6, 7)))
            dense("l1", "k0", hT, lambda: heads1(4), lambda: heads1(5))
            dense("l1", "q1", hT, lambda: heads1(6), lambda: heads1(7))
            dense("l1", "k1", hT, lambda: qk_turn(0, 0), lambda: qk_turn(0, 1))
            dense("l1", "v1", hT, lambda: heads1(8), lambda: heads1(9))
            out_unit(1, 0, [0], False)
            heads1(10)
            out_unit(1, 0, [1])
            heads1(11)
            out_unit(1, 1, [0], False)
            qk_turn(1, 0)
            qk_turn(1, 1)
            out_unit(1, 1, [1])
            heads1(12)
            out_unit(1, 2, [0], False)
            heads1(13)
            out_unit(1, 2, [1])
            heads1(14)
            out_unit(1, 3, [0], False)
            heads1(15)
            out_unit(1, 3, [1])
            heads1(16)
            out_unit(1, 4, [0], False)
            heads1(17)
            out_unit(1, 4, [1])
            out_unit(1, 5)
            ffn(1, 4)


_INS = ["x", "mem", "positions", "norm_mix", "norm_ffn", "mem_norm", "final_norm", "w_mem_kv", "w_ffn_up", "ffn_conv_w",
        "ffn_conv_b", "w_ffn_down", "lru_w_in", "lru_conv_w", "lru_conv_b", "lru_w_a", "lru_b_a", "lru_w_x", "lru_b_x",
        "lru_lambda", "lru_w_out", "dsa_w_in", "dsa_w_out"]


def kernel(**inputs):
    import numpy as _np
    import concourse.bacc as _bacc
    from concourse import mybir as _mybir
    from concourse.bass_utils import run_bass_kernel_spmd as _run

    nc = _bacc.Bacc("TRN2", target_bir_lowering=False, num_devices=1)
    arrays, args = {}, []
    for name in _INS:
        a = _np.ascontiguousarray(inputs[name])
        arrays[f"in_{name}_dram"] = a
        args.append(nc.dram_tensor(f"in_{name}_dram", a.shape, _mybir.dt.from_np(a.dtype), kind="ExternalInput").ap())
    args.append(nc.dram_tensor("out_0_dram", (1, S, D), _mybir.dt.from_np(_np.dtype("float32")), kind="ExternalOutput").ap())
    trunk(nc, *args)
    r = _run(nc, [arrays], core_ids=[0])
    return r.results[0]["out_0_dram"]
```
